# Optimizing a Trainium2 kernel written in Bass

```python
import jax, jax.numpy as jnp
from jax import lax
import numpy as np
import math
import jax
import jax.numpy as jnp

D_MODEL = 1024
BATCH = 1
SEQ = 512
DEPTH = 1

HEAD_DIM = 64
N_HEADS = 8
N_KV_HEADS = 2
GROUP = N_HEADS // N_KV_HEADS
WINDOW = 128
BLOCK = 128
ATTN_SCALE = HEAD_DIM ** -0.5
ATTN_WIDTH = N_HEADS * HEAD_DIM
KV_WIDTH = N_KV_HEADS * HEAD_DIM
CONV_GROUPS = 8
CONV_WIDTH = CONV_GROUPS * 64
CONV_K = 3
IN_WIDTH = ATTN_WIDTH + 2 * KV_WIDTH + 3 * CONV_WIDTH + 2 * D_MODEL
D_FF = 2816
FFN_CONV_K = 3
NORM_EPS = 1e-5


def rms_norm(x, g):
    xf = x.astype(jnp.float32)
    y = xf * lax.rsqrt(jnp.mean(xf * xf, axis=-1, keepdims=True) + NORM_EPS)
    return (y * g.astype(jnp.float32)).astype(x.dtype)

def causal_depthwise_conv(x, w):
    k_width, ch = w.shape
    return lax.conv_general_dilated(
        x, w[:, None, :].astype(x.dtype), window_strides=(1,), padding=((k_width - 1, 0),),
        dimension_numbers=("NWC", "WIO", "NWC"), feature_group_count=ch)

def sliding_window_attention(q, k, v, sinks):
    b, s, _ = q.shape
    nb = s // BLOCK
    q = q.reshape(b, nb, BLOCK, N_KV_HEADS, GROUP, HEAD_DIM)
    k = k.reshape(b, nb, BLOCK, N_KV_HEADS, HEAD_DIM)
    v = v.reshape(b, nb, BLOCK, N_KV_HEADS, HEAD_DIM)

    def with_prev(t):
        prev = jnp.pad(t, ((0, 0), (1, 0), (0, 0), (0, 0), (0, 0)))[:, :-1]
        return jnp.concatenate([prev, t], axis=2)

    kw, vw = with_prev(k), with_prev(v)
    scores = jnp.einsum("bnqhgd,bnkhd->bnhgqk", q, kw).astype(jnp.float32) * ATTN_SCALE
    qi = jnp.arange(BLOCK)[:, None]
    kj = jnp.arange(2 * BLOCK)[None, :]
    dist = qi + BLOCK - kj
    band = (dist >= 0) & (dist < WINDOW)
    real = (jnp.arange(nb)[:, None, None] > 0) | (kj[None] >= BLOCK)
    mask = band[None] & real
    scores = jnp.where(mask[None, :, None, None], scores, -jnp.inf)
    sink = jnp.broadcast_to(sinks.astype(jnp.float32).reshape(1, 1, N_KV_HEADS, GROUP, 1, 1),
                            scores.shape[:-1] + (1,))
    probs = jax.nn.softmax(jnp.concatenate([scores, sink], axis=-1), axis=-1)[..., :-1]
    out = jnp.einsum("bnhgqk,bnkhd->bnqhgd", probs.astype(v.dtype), vw)
    return out.reshape(b, s, ATTN_WIDTH)

def first_inputs(seed: int = 0) -> dict:
    key = jax.random.key(seed)
    ks = jax.random.split(key, 16)
    f32 = jnp.float32

    def nrm(k, shape, scale):
        return jax.random.normal(k, shape, f32) * scale

    return {
        "x": nrm(ks[0], (BATCH, SEQ, D_MODEL), 1.0),
        "mix_norm": 1.0 + nrm(ks[1], (DEPTH, D_MODEL), 0.02),
        "w_in": nrm(ks[2], (DEPTH, D_MODEL, IN_WIDTH), D_MODEL ** -0.5),
        "b_in": nrm(ks[3], (DEPTH, IN_WIDTH), 0.02),
        "sinks": nrm(ks[4], (DEPTH, N_HEADS), 0.5),
        "conv_w": nrm(ks[5], (DEPTH, CONV_K, CONV_WIDTH), CONV_K ** -0.5),
        "w_attn_branch": nrm(ks[6], (DEPTH, ATTN_WIDTH, D_MODEL), ATTN_WIDTH ** -0.5),
        "w_conv_branch": nrm(ks[7], (DEPTH, CONV_WIDTH, D_MODEL), CONV_WIDTH ** -0.5),
        "w_out": nrm(ks[8], (DEPTH, D_MODEL, D_MODEL), D_MODEL ** -0.5),
        "ffn_norm": 1.0 + nrm(ks[9], (DEPTH, D_MODEL), 0.02),
        "w_up": nrm(ks[10], (DEPTH, D_MODEL, 2 * D_FF), D_MODEL ** -0.5),
        "ffn_conv_w": nrm(ks[11], (DEPTH, FFN_CONV_K, 2 * D_FF), FFN_CONV_K ** -0.5),
        "w_down": nrm(ks[12], (DEPTH, D_FF, D_MODEL), D_FF ** -0.5),
        "final_norm": 1.0 + nrm(ks[13], (D_MODEL,), 0.02),
    }

def first_block(x, mix_norm, w_in, b_in, sinks, conv_w, w_attn_branch, w_conv_branch, w_out,
              ffn_norm, w_up, ffn_conv_w, w_down, final_norm):
    h = x
    splits = np.cumsum([ATTN_WIDTH, KV_WIDTH, KV_WIDTH, CONV_WIDTH, CONV_WIDTH, CONV_WIDTH, D_MODEL])
    for l in range(DEPTH):
        xn = rms_norm(h, mix_norm[l])
        proj = jnp.einsum("bsd,dp->bsp", xn, w_in[l]) + b_in[l]
        q, k, v, cb, cc, cx, ga, gc = jnp.split(proj, splits, axis=-1)
        attn = sliding_window_attention(q, k, v, sinks[l])
        conv = cb * causal_depthwise_conv(cc * cx, conv_w[l])
        merged = (jax.nn.sigmoid(ga) * jnp.einsum("bsc,cd->bsd", attn, w_attn_branch[l])
                  + jax.nn.sigmoid(gc) * jnp.einsum("bsc,cd->bsd", conv, w_conv_branch[l]))
        h = h + jnp.einsum("bsd,de->bse", merged, w_out[l])
        hn = rms_norm(h, ffn_norm[l])
        up = causal_depthwise_conv(jnp.einsum("bsd,df->bsf", hn, w_up[l]), ffn_conv_w[l])
        gate, val = jnp.split(up, 2, axis=-1)
        h = h + jnp.einsum("bsf,fd->bsd", jax.nn.silu(gate) * val, w_down[l])
    return rms_norm(h, final_norm)


HEAD_DIM_2 = D_MODEL // 16
NSA_HEADS = 6
NSA_KV_GROUPS = 2
NSA_HPG = NSA_HEADS // NSA_KV_GROUPS
CMP_BLOCK = 32
CMP_STRIDE = 16
CMP_HIDDEN = 2 * HEAD_DIM_2
SLC_BLOCK = 64
SLC_TOPN = 16
WINDOW_2 = 512
NSA_QBLOCK = 64
FORCE_BONUS = 1000.0
NEG_BIG = -1e30
LB_FLOOR = 1e-30
SB_HEADS = 4
SB_QBLOCK = 128
HG_HEADS = 6
HG_KDIM = HEAD_DIM_2
HG_VDIM = HEAD_DIM_2
HG_CHUNK = 64
NUM_BUCKETS = 32
MAX_DISTANCE = 128
D_NSA = NSA_HEADS * HEAD_DIM_2
D_KV = NSA_KV_GROUPS * HEAD_DIM_2
D_SB = SB_HEADS * HEAD_DIM_2
D_HG = HG_HEADS * HG_VDIM
D_MIX = D_NSA + D_SB + D_HG
N_GATES = NSA_HEADS * 3
SPLIT_SIZES = (D_NSA, D_KV, D_KV, D_KV, D_KV, D_KV, D_KV, N_GATES, D_NSA,
               D_SB, D_SB, D_SB, D_SB,
               HG_HEADS * HG_KDIM, HG_HEADS * HG_KDIM, D_HG, D_HG)
D_IN = sum(SPLIT_SIZES)
ALPHA = (2 * DEPTH) ** 0.25
OUT_INIT_SCALE = (8 * DEPTH) ** -0.25
LN_EPS = 1e-5
RMS_EPS = 1e-6


def t5_bucket(rel):
    n = jnp.maximum(rel, 0)
    max_exact = NUM_BUCKETS // 2
    large = max_exact + (jnp.log(jnp.maximum(n, 1).astype(jnp.float32) / max_exact)
                         / math.log(MAX_DISTANCE / max_exact)
                         * (NUM_BUCKETS - max_exact)).astype(jnp.int32)
    large = jnp.clip(large, 0, NUM_BUCKETS - 1)
    return jnp.where(n < max_exact, n, large)

def masked_softmax(s, mask):
    s = jnp.where(mask, s.astype(jnp.float32), NEG_BIG)
    p = jax.nn.softmax(s, axis=-1)
    return jnp.where(mask, p, 0.0)

def layer_norm(v, g, b):
    v32 = v.astype(jnp.float32)
    mu = jnp.mean(v32, axis=-1, keepdims=True)
    var = jnp.mean(jnp.square(v32 - mu), axis=-1, keepdims=True)
    return ((v32 - mu) * lax.rsqrt(var + LN_EPS) * g + b).astype(v.dtype)

def nsa_mixer(q, kc_src, vc_src, ks_src, vs_src, kw_src, vw_src, gate_logits,
              cmp_pos, w_ck1, w_ck2, w_cv1, w_cv2, rel_bias):
    B, S = q.shape[:2]
    G, HPG, dk, QB = NSA_KV_GROUPS, NSA_HPG, HEAD_DIM_2, NSA_QBLOCK
    scale = 1.0 / math.sqrt(dk)
    q = q.reshape(B, S, G, HPG, dk).transpose(0, 2, 3, 1, 4)
    gates = jax.nn.sigmoid(gate_logits.reshape(B, S, G, HPG, 3).transpose(0, 2, 3, 1, 4))

    n_cmp = (S - CMP_BLOCK) // CMP_STRIDE + 1
    blk_idx = np.arange(n_cmp)[:, None] * CMP_STRIDE + np.arange(CMP_BLOCK)[None, :]

    def compress(src, w1, w2):
        blocks = src.reshape(B, S, G, dk)[:, blk_idx] + cmp_pos[None, None, :, None, :]
        blocks = blocks.transpose(0, 3, 1, 2, 4).reshape(B, G, n_cmp, CMP_BLOCK * dk)
        return jax.nn.gelu(blocks @ w1) @ w2

    kc = compress(kc_src, w_ck1, w_ck2)
    vc = compress(vc_src, w_cv1, w_cv2)
    cmp_start = np.arange(n_cmp) * CMP_STRIDE
    cmp_end = jnp.asarray(cmp_start + CMP_BLOCK - 1, dtype=jnp.int32)

    n_slc = S // SLC_BLOCK
    topn = min(SLC_TOPN, n_slc)
    slc_start = np.arange(n_slc) * SLC_BLOCK
    overlap = jnp.asarray(((cmp_start[:, None] < slc_start[None, :] + SLC_BLOCK)
                           & (cmp_start[:, None] + CMP_BLOCK > slc_start[None, :])).astype(np.float32))
    ks = ks_src.reshape(B, S, G, dk).transpose(0, 2, 1, 3).reshape(B, G, n_slc, SLC_BLOCK, dk)
    vs = vs_src.reshape(B, S, G, dk).transpose(0, 2, 1, 3).reshape(B, G, n_slc, SLC_BLOCK, dk)

    pad = ((0, 0), (0, 0), (WINDOW_2, 0), (0, 0))
    kw = jnp.pad(kw_src.reshape(B, S, G, dk).transpose(0, 2, 1, 3), pad)
    vw = jnp.pad(vw_src.reshape(B, S, G, dk).transpose(0, 2, 1, 3), pad)

    tbl = rel_bias.reshape(NUM_BUCKETS, G, HPG)
    tbl_g = tbl.transpose(1, 0, 2)
    b_ix = jnp.arange(B)[:, None, None, None]
    g_ix = jnp.arange(G)[None, :, None, None]
    blk = jnp.arange(n_slc)

    def block(i):
        t0 = i * QB
        t = t0 + jnp.arange(QB)
        qb = lax.dynamic_slice_in_dim(q, t0, QB, axis=3)
        gb = lax.dynamic_slice_in_dim(gates, t0, QB, axis=3)

        rel_c = t[:, None] - cmp_end[None, :]
        bias_c = tbl[t5_bucket(rel_c)].transpose(2, 3, 0, 1)
        s_c = jnp.einsum('bghtd,bgnd->bghtn', qb, kc) * scale + bias_c
        p_c = masked_softmax(s_c, rel_c >= 0)
        o_c = jnp.einsum('bghtn,bgnd->bghtd', p_c.astype(vc.dtype), vc)

        imp = jnp.einsum('bghtn,nj->bgtj', p_c, overlap)
        cur = t // SLC_BLOCK
        forced = (blk[None, :] == 0) | (blk[None, :] == cur[:, None]) | (blk[None, :] == cur[:, None] - 1)
        valid = blk[None, :] * SLC_BLOCK <= t[:, None]
        score = jnp.where(valid, imp + FORCE_BONUS * forced.astype(jnp.float32), NEG_BIG)
        _, idx = lax.top_k(score, topn)
        k_sel = ks[b_ix, g_ix, idx].reshape(B, G, QB, topn * SLC_BLOCK, dk)
        v_sel = vs[b_ix, g_ix, idx].reshape(B, G, QB, topn * SLC_BLOCK, dk)
        pos = (idx[..., None] * SLC_BLOCK + jnp.arange(SLC_BLOCK)).reshape(B, G, QB, topn * SLC_BLOCK)
        rel_s = t[:, None] - pos
        bias_s = jnp.moveaxis(tbl_g[g_ix, t5_bucket(rel_s)], -1, 2)
        s_s = jnp.einsum('bghtd,bgtkd->bghtk', qb, k_sel) * scale + bias_s
        p_s = masked_softmax(s_s, (rel_s >= 0)[:, :, None])
        o_s = jnp.einsum('bghtk,bgtkd->bghtd', p_s.astype(v_sel.dtype), v_sel)

        kwb = lax.dynamic_slice_in_dim(kw, t0, WINDOW_2 + QB, axis=2)
        vwb = lax.dynamic_slice_in_dim(vw, t0, WINDOW_2 + QB, axis=2)
        pos_w = t0 - WINDOW_2 + jnp.arange(WINDOW_2 + QB)
        rel_w = t[:, None] - pos_w[None, :]
        mask_w = (rel_w >= 0) & (rel_w < WINDOW_2) & (pos_w[None, :] >= 0)
        bias_w = tbl[t5_bucket(rel_w)].transpose(2, 3, 0, 1)
        s_w = jnp.einsum('bghtd,bgkd->bghtk', qb, kwb) * scale + bias_w
        p_w = masked_softmax(s_w, mask_w)
        o_w = jnp.einsum('bghtk,bgkd->bghtd', p_w.astype(vwb.dtype), vwb)

        return gb[..., 0:1] * o_c + gb[..., 1:2] * o_s + gb[..., 2:3] * o_w

    o = lax.map(block, jnp.arange(S // QB))
    return o.transpose(1, 0, 4, 2, 3, 5).reshape(B, S, D_NSA)

def stick_breaking_mixer(q, k, v):
    B, S = q.shape[:2]
    H, dk, QB = SB_HEADS, HEAD_DIM_2, SB_QBLOCK
    scale = 1.0 / math.sqrt(dk)
    q = q.reshape(B, S, H, dk).transpose(0, 2, 1, 3)
    k = k.reshape(B, S, H, dk).transpose(0, 2, 1, 3)
    v = v.reshape(B, S, H, dk).transpose(0, 2, 1, 3)
    s_idx = jnp.arange(S)

    def block(i):
        t0 = i * QB
        t = t0 + jnp.arange(QB)
        qb = lax.dynamic_slice_in_dim(q, t0, QB, axis=2)
        z = jnp.einsum('bhtd,bhsd->bhts', qb, k).astype(jnp.float32) * scale
        mask = s_idx[None, :] < t[:, None]
        log_rest = jnp.where(mask, jax.nn.log_sigmoid(-z), 0.0)
        rcs = lax.cumsum(log_rest, axis=3, reverse=True)
        between = jnp.pad(rcs[..., 1:], ((0, 0), (0, 0), (0, 0), (0, 1)))
        log_a = jnp.where(mask, jax.nn.log_sigmoid(z) + between, 0.0)
        a = jnp.where(mask, jnp.exp(log_a), 0.0)
        return jnp.einsum('bhts,bhsd->bhtd', a.astype(v.dtype), v)

    o = lax.map(block, jnp.arange(S // QB))
    return o.transpose(1, 0, 3, 2, 4).reshape(B, S, D_SB)

def hgrn2_mixer(q, f_logit, i_val, lb):
    B, S = q.shape[:2]
    H, dk, dv, C = HG_HEADS, HG_KDIM, HG_VDIM, HG_CHUNK
    n_c = S // C
    f32 = f_logit.astype(jnp.float32)
    log_f = jnp.logaddexp(jnp.log(jnp.maximum(lb, LB_FLOOR)), jnp.log1p(-lb) + jax.nn.log_sigmoid(f32))
    key = (1.0 - lb) * jax.nn.sigmoid(-f32)

    def heads(a, d):
        return a.astype(jnp.float32).reshape(B, n_c, C, H, d).transpose(1, 0, 3, 2, 4)

    qc, kc, lfc, vc = heads(q, dk), heads(key, dk), heads(log_f, dk), heads(i_val, dv)
    causal = jnp.asarray(np.tril(np.ones((C, C), dtype=bool)))[None, None, :, :, None]

    def step(state, inp):
        qx, kx, lf, vx = inp
        b = jnp.cumsum(lf, axis=2)
        diff = b[:, :, :, None, :] - b[:, :, None, :, :]
        decay = jnp.where(causal, jnp.exp(jnp.where(causal, diff, 0.0)), 0.0)
        att = jnp.einsum('bhtd,bhsd,bhtsd->bhts', qx, kx, decay)
        o = att @ vx + jnp.einsum('bhtd,bhde->bhte', qx * jnp.exp(b), state)
        b_last = b[:, :, -1:, :]
        state = (jnp.exp(b_last[:, :, 0, :])[..., None] * state
                 + jnp.einsum('bhsd,bhse->bhde', kx * jnp.exp(b_last - b), vx))
        return state, o

    s0 = jnp.zeros((B, H, dk, dv), jnp.float32)
    _, o = lax.scan(step, s0, (qc, kc, lfc, vc))
    return o.transpose(1, 0, 3, 2, 4).reshape(B, S, H, dv)

def second_inputs(seed: int = 0) -> dict:
    key = jax.random.key(seed)
    ks = jax.random.split(key, 13)

    def nrm(k, shape, scale):
        return jax.random.normal(k, shape, jnp.float32) * scale

    x = nrm(ks[0], (BATCH, SEQ, D_MODEL), 1.0)
    w_in = nrm(ks[1], (DEPTH, D_MODEL, D_IN), D_MODEL ** -0.5)
    cmp_pos = nrm(ks[2], (DEPTH, CMP_BLOCK, HEAD_DIM_2), 0.1)
    w_ck1 = nrm(ks[3], (DEPTH, CMP_BLOCK * HEAD_DIM_2, CMP_HIDDEN), (CMP_BLOCK * HEAD_DIM_2) ** -0.5)
    w_ck2 = nrm(ks[4], (DEPTH, CMP_HIDDEN, HEAD_DIM_2), CMP_HIDDEN ** -0.5)
    w_cv1 = nrm(ks[5], (DEPTH, CMP_BLOCK * HEAD_DIM_2, CMP_HIDDEN), (CMP_BLOCK * HEAD_DIM_2) ** -0.5)
    w_cv2 = nrm(ks[6], (DEPTH, CMP_HIDDEN, HEAD_DIM_2), CMP_HIDDEN ** -0.5)
    hg_lb = nrm(ks[7], (DEPTH, HG_HEADS * HG_KDIM), 0.5)
    hg_norm_w = 1.0 + nrm(ks[8], (DEPTH, D_HG), 0.05)
    w_out = nrm(ks[9], (DEPTH, D_MIX, D_MODEL), D_MIX ** -0.5 * OUT_INIT_SCALE)
    ln_g = 1.0 + nrm(ks[10], (DEPTH, D_MODEL), 0.05)
    ln_b = nrm(ks[11], (DEPTH, D_MODEL), 0.02)
    rel_bias = nrm(ks[12], (NUM_BUCKETS, NSA_HEADS), 0.5)
    return {'x': x, 'w_in': w_in, 'cmp_pos': cmp_pos, 'w_ck1': w_ck1, 'w_ck2': w_ck2,
            'w_cv1': w_cv1, 'w_cv2': w_cv2, 'hg_lb': hg_lb, 'hg_norm_w': hg_norm_w,
            'w_out': w_out, 'ln_g': ln_g, 'ln_b': ln_b, 'rel_bias': rel_bias}

def second_block(x, w_in, cmp_pos, w_ck1, w_ck2, w_cv1, w_cv2, hg_lb, hg_norm_w,
              w_out, ln_g, ln_b, rel_bias):
    lb_w = jax.nn.softmax(hg_lb.astype(jnp.float32), axis=0)
    lb_all = jnp.cumsum(lb_w, axis=0) - lb_w[0]
    offsets = np.cumsum(SPLIT_SIZES)[:-1].tolist()
    for l in range(DEPTH):
        h = x @ w_in[l]
        (nsa_q, nsa_kc, nsa_vc, nsa_ks, nsa_vs, nsa_kw, nsa_vw, nsa_g, nsa_z,
         sb_q, sb_k, sb_v, sb_z, hg_q, hg_f, hg_i, hg_z) = jnp.split(h, offsets, axis=-1)
        o_nsa = nsa_mixer(nsa_q, nsa_kc, nsa_vc, nsa_ks, nsa_vs, nsa_kw, nsa_vw, nsa_g,
                          cmp_pos[l], w_ck1[l], w_ck2[l], w_cv1[l], w_cv2[l], rel_bias)
        o_sb = stick_breaking_mixer(sb_q, sb_k, sb_v)
        o_hg = hgrn2_mixer(hg_q, hg_f, hg_i, lb_all[l])
        o_hg = o_hg * lax.rsqrt(jnp.mean(jnp.square(o_hg), axis=-1, keepdims=True) + RMS_EPS)
        o_hg = (o_hg * hg_norm_w[l].reshape(HG_HEADS, HG_VDIM)).reshape(o_hg.shape[0], o_hg.shape[1], D_HG)
        mixed = jnp.concatenate([o_nsa * jax.nn.silu(nsa_z),
                                 o_sb * jax.nn.silu(sb_z),
                                 o_hg.astype(x.dtype) * jax.nn.silu(hg_z)], axis=-1)
        x = layer_norm(ALPHA * x + (mixed @ w_out[l]).astype(x.dtype), ln_g[l], ln_b[l])
    return x


def setup_inputs(seed=0):
    out = dict(first_inputs(seed))
    for name, value in second_inputs(seed + 1).items():
        if name != "x":
            out[name + "_2"] = value
    return out


def reference(
    x, mix_norm, w_in, b_in, sinks, conv_w, w_attn_branch, w_conv_branch, w_out, ffn_norm, w_up,
    ffn_conv_w, w_down, final_norm, w_in_2, cmp_pos_2, w_ck1_2, w_ck2_2, w_cv1_2, w_cv2_2,
    hg_lb_2, hg_norm_w_2, w_out_2, ln_g_2, ln_b_2, rel_bias_2,
):
    x = first_block(
        x, mix_norm, w_in, b_in, sinks, conv_w, w_attn_branch, w_conv_branch, w_out, ffn_norm,
        w_up, ffn_conv_w, w_down, final_norm,
    )
    return second_block(
        x, w_in_2, cmp_pos_2, w_ck1_2, w_ck2_2, w_cv1_2, w_cv2_2, hg_lb_2, hg_norm_w_2, w_out_2,
        ln_g_2, ln_b_2, rel_bias_2,
    )


_drawn_inputs = setup_inputs


def setup_inputs(seed=0):
    import zlib

    import numpy as np

    out = dict(_drawn_inputs(seed))
    spreads = {}
    factors = {'sinks': 8.0,
     'ffn_norm': 3.853,
     'cmp_pos_2': 8.0,
     'w_ck1_2': 5.496,
     'w_ck2_2': 5.618,
     'hg_norm_w_2': 5.923,
     'ln_b_2': 2.667,
     'rel_bias_2': 5.353}
    for name, (base, spread) in spreads.items():
        noise = np.random.default_rng([zlib.crc32(name.encode()), seed]).standard_normal(out[name].shape)
        drawn = base * np.exp(spread * noise) if base else spread * noise
        out[name] = jnp.asarray(drawn.astype(out[name].dtype))
    for name, factor in factors.items():
        out[name] = (out[name] * factor).astype(out[name].dtype)
    return out
```

```python
from contextlib import ExitStack

import numpy as np
import concourse.bass as bass
from concourse import mybir

F = mybir.dt.float32
FR = mybir.dt.float32r
U32 = mybir.dt.uint32
ALU = mybir.AluOpType
ACT = mybir.ActivationFunctionType
AX = mybir.AxisListType

P = 128
S = 512
D = 1024
NEG = -1e30
BIG = 3e38

NF = 22
W1 = 0
SLOT_Q = [0, 1, 2, 3]
SLOT_K = 4
SLOT_V = 5
SLOT_CONV = 6
SLOT_GATE = 18
SLOT_WOUT = 42
SLOT_FFN = 50
N_HALF = 22 + 12
SLOT_B2 = SLOT_FFN + 2 * N_HALF
N_B2 = 3 + 3 + 4 + 2 + 2 + 4 + 4 + 3 + 8
SLOT_WOUT2 = SLOT_B2 + N_B2
N_SLOTS = SLOT_WOUT2 + 8

PP_B = 0
PP_G1 = 34
PP_G2 = 42
PP_CW = 50
PP_FW = 62
PP_LB = 194
PP_N = 197
C_ID = 0
C_BAND = 128
C_STRICT = 384
C_NTRI = 512
C_LEV = 640
C_ROW = 640 + 448
C_ONE = C_ROW + 1
C_N = C_ONE + 128
LEVELS = [64, 32, 16, 8, 4, 2, 1]
R_VB = 0
R_SINK = 128
R_HG = 136
R_N = 520
U_N = 896


class Queue:

    def __init__(self, sem):
        self.sem, self.count, self.items, self.seen = sem, 0, [], {}

    def wait(self, *toks):
        for t in toks:
            if t is None:
                continue
            if isinstance(t, list):
                self.wait(*t)
                continue
            sem, value = t
            if self.seen.get(sem.name, 0) < value:
                self.seen[sem.name] = value
                self.items.append(lambda e, sem=sem, value=value: e.wait_ge(sem, value))

    def do(self, fn, *waits):
        self.wait(*waits)
        self.count += 1
        self.items.append(lambda e: fn(e).then_inc(self.sem, 1))
        return (self.sem, self.count)

    def quiet(self, fn, *waits):
        self.wait(*waits)
        self.items.append(fn)

    def dma(self, out, in_, sem, value, *waits):
        self.wait(*waits)
        self.items.append(lambda e: e.dma_start(out, in_).then_inc(sem, 16))
        return (sem, value)

    def play(self, e):
        for f in self.items:
            f(e)


class Buf:

    def __init__(self, ap):
        self.ap, self.free = ap, []


def program(nc, wp, x, pp, cst, rows, brow, relb, oneh, w1c, w2c, posT, out, dbg=None):
    ctx = ExitStack()
    with ctx:
        def sem(name):
            return ctx.enter_context(nc.semaphore(name))

        def sb(name, shape, dt=F, c=ctx):
            return c.enter_context(nc.sbuf_tensor(name, shape, dt))

        pe, act, dve, pool, sp = (Queue(sem("q_" + n)) for n in ("pe", "act", "dve", "pool", "sp"))
        NR = NH = 3
        s_w = [sem(f"s_w{i}") for i in range(NR)]
        s_par = sem("s_par")
        s_x = [sem(f"s_x{i}") for i in range(4)]
        s_misc = [sem(f"s_m{i}") for i in range(10)]
        s_out = sem("s_out")

        psum = [ctx.enter_context(nc.psum_tensor(f"ps{i}", [P, S], F)) for i in range(8)]
        WB = [Buf(psum[i]) for i in range(4)]
        AB = [Buf(psum[4 + i]) for i in range(4)]

        raw = [sb(f"raw{i}", [P, 1024]) for i in range(NR)]
        whi = [sb(f"whi{i}", [P, 1024], FR) for i in range(NH)]
        wlo = [sb(f"wlo{i}", [P, 1024], FR) for i in range(NH)]
        XH = sb("XH", [P, 8, S], FR)
        XL = sb("XL", [P, 8, S], FR)
        H = sb("H", [P, 4, D])
        PPt = sb("PPt", [P, PP_N])
        C = sb("C", [P, C_N])
        RW = sb("RW", [P, R_N])
        st = sb("st", [P, 64])
        ID = C[:, C_ID:C_ID + 128]
        vec_dram = nc.dram_tensor("vec_dram", [P, 6, 1024], F, kind="Internal").ap()

        t_x = []
        for t in range(4):
            t_x.append(act.dma(H[:, t, :], x[t * P:(t + 1) * P, :], s_x[t], 16))
        act.dma(C[:, :], cst, s_par, 16)
        act.dma(PPt[:, :], pp, s_par, 32)
        t_par = act.dma(RW[:, :], rows.partition_broadcast(P), s_par, 48)

        widths = [1024] * N_SLOTS
        for hf in range(2):
            for c in range(2):
                widths[SLOT_FFN + hf * N_HALF + 22 + 6 * c + 5] = 512
        for i in range(4):
            widths[SLOT_B2 + 6 + i] = 804
        t_w, t_hi, t_lo, t_used = {}, {}, {}, {}

        def load(i):
            if i < N_SLOTS:
                w = widths[i]
                t_w[i] = sp.dma(raw[i % NR][:, 0:w], wp[i, :, 0:w], s_w[i % NR], 16 * (i // NR + 1),
                                t_hi.get(i - NR), t_lo.get(i - NR))

        def split(i):
            if i < N_SLOTS and i not in t_hi:
                w = widths[i]
                r, h, lo = raw[i % NR][:, 0:w], whi[i % NH][:, 0:w], wlo[i % NH][:, 0:w]
                t_hi[i] = act.do(lambda e: e.copy(h, r), t_w[i], t_used.get(i - NH))
                t_lo[i] = dve.do(lambda e: e.tensor_tensor(lo, r, h.bitcast(F), ALU.subtract),
                                 t_hi[i], t_used.get(i - NH))
                load(i + NR)

        for i in range(NR):
            load(i)

        def slot(i):
            for j in range(i, i + NH):
                if j - NH < 0 or (j - NH) in t_used:
                    split(j)
            pe.wait(t_hi[i], t_lo[i])
            return whi[i % NH], wlo[i % NH]

        def mm3(out_, ah, al, bh, bl, start, stop_):
            pe.quiet(lambda e: e.matmul(out_, ah, bh, start=start, stop=False))
            pe.quiet(lambda e: e.matmul(out_, ah, bl, start=False, stop=False))
            return lambda e: e.matmul(out_, al, bh, start=False, stop=stop_)

        bank_i = [0]

        def next_bank(pool_):
            bank_i[0] += 1
            return pool_[bank_i[0] % len(pool_)]

        def fm(i, banks, evac, Xh=None, Xl=None, x_tok=None, k0=0, nk=8, wk=0, last=True):
            Xh, Xl = Xh or XH, Xl or XL
            wh, wl = slot(i)
            b = next_bank(banks)
            pe.wait(b.free, x_tok[0] if isinstance(x_tok, dict) else x_tok)
            for k in range(nk):
                if isinstance(x_tok, dict):
                    pe.wait(x_tok[k])
                cs = slice((wk + k) * P, (wk + k + 1) * P)
                f = mm3(b.ap[:, :], wh[:, cs], wl[:, cs], Xh[:, k0 + k, :], Xl[:, k0 + k, :],
                        k == 0, k == nk - 1)
                if k == nk - 1:
                    tok = pe.do(f)
                else:
                    pe.quiet(f)
                if k % 2 and k < nk - 1:
                    yield
            if last:
                t_used[i] = tok
            b.free = evac(b.ap, tok)
            yield

        def tm(i0, width, nk, evac, Xh=None, Xl=None, x_tok=None, per=2, k0=0):
            Xh, Xl = Xh or XH, Xl or XL
            for s0 in range(0, nk, per):
                i = i0 + s0 // per
                ks = range(s0, min(s0 + per, nk))
                wh, wl = slot(i)
                for t in range(4):
                    b = WB[t]
                    if s0 == 0:
                        pe.wait(b.free)
                    for k in ks:
                        if x_tok is not None:
                            pe.wait(x_tok[k])
                        ws = slice((k - s0) * width, (k - s0 + 1) * width)
                        ts = slice(t * P, (t + 1) * P)
                        f = mm3(b.ap[:, 0:width], Xh[:, k0 + k, ts], Xl[:, k0 + k, ts], wh[:, ws], wl[:, ws],
                                k == 0, k == nk - 1)
                        if k == ks[-1]:
                            tok = pe.do(f)
                        else:
                            pe.quiet(f)
                    if t == 3:
                        t_used[i] = tok
                    if ks[-1] == nk - 1:
                        b.free = evac(t, b.ap, tok)
                    yield

        def run(*gens):
            main, side = gens[0], [g for g in gens[1:] if g is not None]
            for _ in main:
                for g in list(side):
                    try:
                        next(g)
                    except StopIteration:
                        side.remove(g)
            for g in side:
                for _ in g:
                    pass

        def drain(g):
            for _ in g:
                pass

        def chain(*gs):
            for g in gs:
                yield from g

        def par(col, n=1):
            return PPt[:, col:col + n]

        def split_out(src, hi, lo, *waits, scale=None, bias=None):
            if scale is not None:
                a = act.do(lambda e: e.activation(hi, src, ACT.Identity, scale=scale), *waits)
                d = dve.do(lambda e: e.scalar_tensor_tensor(lo, src, scale, hi.bitcast(F), ALU.mult, ALU.subtract), a, *waits)
            elif bias is not None:
                a = act.do(lambda e: e.activation(hi, src, ACT.Identity, bias=bias), *waits)
                d = dve.do(lambda e: e.scalar_tensor_tensor(lo, src, bias, hi.bitcast(F), ALU.add, ALU.subtract), a, *waits)
            else:
                a = act.do(lambda e: e.copy(hi, src), *waits)
                d = dve.do(lambda e: e.tensor_tensor(lo, src, hi.bitcast(F), ALU.subtract), a, *waits)
            return [a, d]

        def rms_cols(t_h, base, eps, junk):
            sq = []
            for t in range(4):
                sq.append(act.do(lambda e, t=t: e.activation(junk, H[:, t, :], ACT.Square,
                                                             accum_out=st[:, base + t:base + t + 1]),
                                 t_h[t], sq[-1] if sq else None))
            cs = slice(base, base + 4)
            e0 = dve.do(lambda e: e.tensor_scalar(st[:, cs], st[:, cs], 1.0 / D, eps, ALU.mult, ALU.add), sq)
            a = act.do(lambda e: e.activation(st[:, cs], st[:, cs], ACT.Sqrt), e0)
            return dve.do(lambda e: e.reciprocal(st[:, cs], st[:, cs]), a)

        def to_XT(src, t_src, banks, x_free, gcol=None):
            toks = {}
            for k in range(8):
                b = next_bank(banks)
                pe.wait(b.free, t_src)
                for t in range(4):
                    f = lambda e, b=b, k=k, t=t: e.transpose(b.ap[:, t * P:(t + 1) * P], src[:, t, k * P:(k + 1) * P], ID)
                    if t == 3:
                        tok = pe.do(f)
                    else:
                        pe.quiet(f)
                toks[k] = split_out(b.ap[:, :], XH[:, k, :], XL[:, k, :], tok, x_free,
                                    scale=None if gcol is None else par(gcol + k))
                b.free = toks[k]
            return toks

        p1 = ExitStack()
        junk = sb("junk", [P, D], F, p1)
        XS = sb("XS", [P, 4, D], F, p1)
        t_r = rms_cols(t_x, 0, 1e-5, junk[:, :])
        t_xs = []
        for t in range(4):
            f = lambda e, t=t: e.tensor_scalar(XS[:, t, :], H[:, t, :], st[:, t:t + 1], None, ALU.mult)
            g = lambda e, t=t: e.activation(XS[:, t, :], H[:, t, :], ACT.Identity, scale=st[:, t:t + 1])
            t_xs.append(dve.do(f, t_r, t_x[t]) if t % 2 else act.do(g, t_r, t_x[t]))
        split(0)
        xt = to_XT(XS, [t_xs, t_par], WB + AB, None, PP_G1)
        t_all = [xt[k] for k in range(8)]
        p1.close()

        p1 = ExitStack()
        Q = sb("Q", [P, 4, S], F, p1)
        K = sb("K", [P, S], F, p1)
        V = sb("V", [P, 4, 128], F, p1)
        SC = sb("SC", [P, 2, 2, 256], F, p1)
        PB = sb("PB", [P, 2, 2, 256], F, p1)
        PT = sb("PT", [P, 2, 512], F, p1)
        AT = sb("AT", [P, 4, S], F, p1)
        CA = sb("CA", [P, S], F, p1)
        CB = sb("CB", [P, S], F, p1)
        CC = sb("CC", [P, S], F, p1)
        GA = sb("GA", [P, 2, 2, S], F, p1)
        small = sb("small", [P, 4, 4, 8], F, p1)
        ATH = sb("ATH", [P, 4, S], FR, p1)
        ATL = sb("ATL", [P, 4, S], FR, p1)
        CVH = sb("CVH", [P, 4, S], FR, p1)
        CVL = sb("CVL", [P, 4, S], FR, p1)
        MH = sb("MH", [P, 8, S], FR, p1)
        ML = sb("ML", [P, 8, S], FR, p1)
        nsink = small[:, 3, 3, :]
        t_old = t_all

        t_q, t_v = {}, []
        b2 = WB[0:2]

        def ev_q(i):
            def f(ps, tok):
                t_q[i] = act.do(lambda e: e.activation(Q[:, i, :], ps[:, :], ACT.Identity, bias=par(PP_B + i)), tok, t_old)
                return [t_q[i]]
            return f

        def ev_k(ps, tok):
            t_q["k"] = act.do(lambda e: e.activation(K[:, :], ps[:, :], ACT.Identity, bias=par(PP_B + 4)), tok, t_old)
            return [t_q["k"]]

        def ev_v(t, ps, tok):
            t_v.append(dve.do(lambda e: e.tensor_tensor(V[:, t, :], ps[:, 0:128], RW[:, R_VB:R_VB + 128], ALU.add),
                              tok, t_par, t_old))
            return [t_v[-1]]

        t_ns = dve.do(lambda e: e.tensor_scalar(nsink, RW[:, R_SINK:R_SINK + 8], -1.0, None, ALU.mult), t_par, t_old)
        drain(chain(
            *[fm(i, b2, ev_q(i), x_tok=xt if i == 0 else None) for i in range(4)],
            fm(SLOT_K, b2, ev_k),
            tm(SLOT_V, 128, 8, ev_v, per=8)))

        SB_ = [(WB[2], WB[3]), (AB[0], AB[1])]
        bPT, bO = AB[2], AB[3]
        PBf, PTf, ATf = [Buf(None), Buf(None)], [Buf(None), Buf(None)], {}
        nm = lambda qb, h: small[:, 0, qb, h:h + 1]
        ls = lambda qb, h: small[:, 1, qb, h:h + 1]
        t_ath = []

        def attn1():
            ex_qb = {}
            pend = []
            n = 0
            for qb in range(4):
                k0, kn = (0, 128) if qb == 0 else ((qb - 1) * 128, 256)
                nb = kn // 128
                t_l, t_pv = [], []
                for i in range(4):
                    u = n % 2
                    n += 1
                    banks = SB_[u]
                    for j in range(2):
                        r = slice(64 * j, 64 * j + 64)
                        t_s = pe.do(lambda e, r=r, j=j, banks=banks, i=i, qb=qb, k0=k0, kn=kn: e.matmul(
                            banks[j].ap[:, 0:kn], Q[r, i, qb * 128:qb * 128 + 128], K[r, k0:k0 + kn],
                            start=True, stop=True), banks[j].free, t_q[i], t_q["k"])
                    yield
                    t_e = []
                    for j in range(2):
                        h = i + 4 * j
                        band = C[:, C_BAND + 256 - kn:C_BAND + 256]
                        tt = dve.do(lambda e, j=j, h=h, u=u, qb=qb, banks=banks, band=band, kn=kn: e.tensor_tensor_reduce(
                            SC[:, u, j, 0:kn], banks[j].ap[:, 0:kn], band, -0.125, nsink[:, h:h + 1],
                            ALU.add, ALU.min, nm(qb, h)), t_s, t_ns, PBf[u].free)
                        banks[j].free = [tt]
                        t_e.append(act.do(lambda e, j=j, h=h, u=u, qb=qb, kn=kn: e.activation(
                            PB[:, u, j, 0:kn], SC[:, u, j, 0:kn], ACT.Exp, bias=nm(qb, h), scale=-1.0,
                            accum_out=ls(qb, h)), tt, PBf[u].free))
                    t_l += t_e
                    yield
                    pe.wait(bPT.free, t_e)
                    for j in range(2):
                        for c in range(nb):
                            f = lambda e, j=j, c=c, u=u, nb=nb: e.transpose(
                                bPT.ap[:, (j * nb + c) * 128:(j * nb + c + 1) * 128], PB[:, u, j, c * 128:(c + 1) * 128], ID)
                            t_t = pe.do(f)
                    PBf[u].free = [t_t]
                    w = 2 * nb * 128
                    t_c = dve.do(lambda e, u=u, w=w: e.tensor_copy(PT[:, u, 0:w], bPT.ap[:, 0:w]), t_t, PTf[u].free, t_old)
                    bPT.free = [t_c]
                    yield
                    pe.wait(t_c, t_v[max(qb - 1, 0):qb + 1], bO.free)
                    for j in range(2):
                        h = i + 4 * j
                        for c in range(nb):
                            kb = k0 // 128 + c
                            t_p = pe.do(lambda e, j=j, c=c, u=u, h=h, kb=kb, nb=nb: e.matmul(
                                bO.ap[:, h * 64:h * 64 + 64], PT[:, u, (j * nb + c) * 128:(j * nb + c + 1) * 128],
                                V[:, kb, j * 64:j * 64 + 64], start=(c == 0), stop=(c == nb - 1)))
                    PTf[u].free = [t_p]
                sk = small[:, 2, qb, :]
                a = dve.do(lambda e, qb=qb, sk=sk: e.tensor_tensor(sk, small[:, 0, qb, :], nsink, ALU.subtract), t_l)
                b = act.do(lambda e, sk=sk: e.activation(sk, sk, ACT.Exp), a)
                c_ = dve.do(lambda e, qb=qb, sk=sk: e.tensor_tensor(sk, sk, small[:, 1, qb, :], ALU.add), b, t_l)
                d = dve.do(lambda e, sk=sk: e.reciprocal(sk, sk), c_)
                o3 = bO.ap[:, :].rearrange("p (h d) -> p h d", d=64)
                a3 = AT[:, qb, :].rearrange("p (h d) -> p h d", d=64)
                g = dve.do(lambda e, o3=o3, a3=a3, sk=sk: e.tensor_tensor(
                    a3, o3, sk.rearrange("p (h o) -> p h o", o=1).to_broadcast([P, 8, 64]), ALU.mult), d, t_p)
                bO.free = [g]
                yield
                pe.wait(bPT.free, g)
                for k in range(4):
                    t_t = pe.do(lambda e, k=k, qb=qb: e.transpose(bPT.ap[:, k * 128:(k + 1) * 128],
                                                                  AT[:, qb, k * 128:(k + 1) * 128], ID))
                src = bPT.ap[:, :].rearrange("p (k t) -> p k t", k=4)
                r = split_out(src, ATH[:, :, qb * 128:(qb + 1) * 128], ATL[:, :, qb * 128:(qb + 1) * 128], t_t)
                bPT.free = r
                t_ath.append(r)
                yield

        t_cv = []
        cv = {"a": None, "b": None, "c": None, "hi": None}

        def conv_tile(c):
            s = {}

            def ev_cc(ps, tok):
                s["cc"] = act.do(lambda e: e.activation(CA[:, :], ps[:, :], ACT.Identity, bias=par(PP_B + 10 + c)),
                                 tok, cv["a"], t_old)
                return [s["cc"]]

            def ev_cx(ps, tok):
                s["p"] = dve.do(lambda e: e.scalar_tensor_tensor(CB[:, :], ps[:, :], par(PP_B + 14 + c), CA[:, :],
                                                                 ALU.add, ALU.mult), tok, s["cc"], cv["b"])
                cv["a"] = s["p"]
                wc = PP_CW + 3 * c
                y2 = act.do(lambda e: e.activation(CC[:, :], CB[:, :], ACT.Identity, scale=par(wc + 2)), s["p"], cv["c"])
                y1 = dve.do(lambda e: e.scalar_tensor_tensor(CC[:, 1:S], CB[:, 0:S - 1], par(wc + 1), CC[:, 1:S],
                                                             ALU.mult, ALU.add), y2)
                s["y"] = dve.do(lambda e: e.scalar_tensor_tensor(CC[:, 2:S], CB[:, 0:S - 2], par(wc), CC[:, 2:S],
                                                                 ALU.mult, ALU.add), y1)
                return [s["p"]]

            def ev_cb(ps, tok):
                z = dve.do(lambda e: e.scalar_tensor_tensor(CB[:, :], ps[:, :], par(PP_B + 6 + c), CC[:, :],
                                                            ALU.add, ALU.mult), tok, s["y"])
                cv["c"] = z
                t_cv.append(split_out(CB[:, :], CVH[:, c, :], CVL[:, c, :], z, t_old))
                cv["b"] = t_cv[-1]
                return [z]

            i = SLOT_CONV + 3 * c
            return chain(fm(i, b2, ev_cc), fm(i + 1, b2, ev_cx), fm(i + 2, b2, ev_cb))

        run(chain(*[conv_tile(c) for c in range(4)]), attn1())

        t_m = {}
        gaf = [None, None]

        def merge_tile(n):
            u = n % 2
            s = {}

            def ev_g(j):
                def f(ps, tok):
                    s[j] = act.do(lambda e: e.activation(GA[:, u, j, :], ps[:, :], ACT.Sigmoid,
                                                         bias=par(PP_B + 18 + 8 * j + n)), tok, gaf[u], t_old)
                    return [s[j]]
                return f

            def ev_br(j):
                def f(ps, tok):
                    s[2 + j] = dve.do(lambda e: e.tensor_tensor(GA[:, u, j, :], ps[:, :], GA[:, u, j, :], ALU.mult),
                                      tok, s[j])
                    return [s[2 + j]]
                return f

            i = SLOT_GATE + 3 * n
            yield from fm(i, WB, ev_g(0))
            yield from fm(i + 1, WB, ev_g(1))
            yield from fm(i + 2, WB, ev_br(0), ATH, ATL, t_ath, 0, 4, 0, last=False)
            yield from fm(i + 2, WB, ev_br(1), CVH, CVL, t_cv, 0, 4, 4)
            a = dve.do(lambda e: e.tensor_tensor(GA[:, u, 0, :], GA[:, u, 0, :], GA[:, u, 1, :], ALU.add), s[2], s[3])
            t_m[n] = split_out(GA[:, u, 0, :], MH[:, n, :], ML[:, n, :], a, t_old)
            gaf[u] = t_m[n]

        run(chain(*[merge_tile(n) for n in range(8)]))

        t_h = {}

        def ev_wout(c):
            def f(t, ps, tok):
                cs = slice(c * 512, c * 512 + 512)
                r = dve.do(lambda e: e.tensor_tensor(H[:, t, cs], ps[:, :], H[:, t, cs], ALU.add), tok, t_x[t],
                           t_xs)
                t_h[t] = [*t_h.get(t, []), r]
                return [r]
            return f

        for c in range(2):
            drain(tm(SLOT_WOUT + 4 * c, 512, 8, ev_wout(c), MH, ML, t_m))
        t_pe_wout = t_used[SLOT_WOUT + 7]
        p1.close()
        if dbg == 1:
            sp.dma(out.rearrange("(t p) d -> p t d", p=P), H[:, :, :], s_out, 16, [t_h[t] for t in range(4)])
            sp.wait((s_out, 16))

        if dbg is None or dbg > 1:
            pv = ExitStack()
            OH = sb("OH", [32, S], F, pv)
            RB = sb("RB", [32, 6], F, pv)
            RBB = sb("RBB", [32, 6, P], F, pv)
            VE = sb("VE", [P, 6, 1024], F, pv)
            t_old = [t_pe_wout, [t_m[n] for n in range(8)]]
            act.wait(t_old)
            dve.wait(t_old)
            sp.dma(OH[:, :], oneh, s_misc[2], 16, t_old)
            t_rb = sp.dma(RB[:, :], relb, s_misc[2], 32)
            t_rbb = dve.do(lambda e: e.tensor_copy(RBB[:, :, :], RB[:, :].rearrange("b (h o) -> b h o", o=1).to_broadcast([32, 6, P])), t_rb)
            v = [dve.do(lambda e: e.memset(VE[:, :, 512:1024], NEG))]
            for h in range(6):
                bk = AB[h % 4]
                tk = pe.do(lambda e, h=h, bk=bk: e.matmul(bk.ap[:, :], RBB[:, h, :], OH[:, :], start=True, stop=True), t_rbb, bk.free)
                v.append(act.do(lambda e, h=h, bk=bk: e.copy(VE[:, h, 0:512], bk.ap[:, :]), tk))
                bk.free = [v[-1]]
            t_v = sp.dma(vec_dram, VE[:, :, :], s_misc[6], 16, v)
            p2 = ExitStack()
            junk = sb("junk2", [P, D], F, p2)
            XS2 = sb("XS2", [P, 4, D], F, p2)
            t_r = rms_cols(t_h, 4, 1e-5, junk[:, :])
            t_xs = []
            for t in range(4):
                f = lambda e, t=t: e.tensor_scalar(XS2[:, t, :], H[:, t, :], st[:, 4 + t:5 + t], None, ALU.mult)
                g = lambda e, t=t: e.activation(XS2[:, t, :], H[:, t, :], ACT.Identity, scale=st[:, 4 + t:5 + t])
                t_xs.append(dve.do(f, t_r) if t % 2 else act.do(g, t_r))
            xt = to_XT(XS2, t_xs, WB + AB, t_used[SLOT_GATE + 23], PP_G2)
            p2.close()
            p2 = ExitStack()
            t_old = [xt[k] for k in range(8)]
            GH = sb("GH", [P, 11, S], FR, p2)
            GL = sb("GL", [P, 11, S], FR, p2)
            UA = sb("UA", [P, 2, 2, S], F, p2)
            uf = [None, None]
            act.wait(t_old)
            dve.wait(t_old)
            g_free = [None]

            def up_tile(hf, j):
                f_ = hf * 11 + j
                u = f_ % 2
                s = {}

                def ev(g):
                    def f(ps, tok):
                        wc = PP_FW + 3 * (f_ + NF * g)
                        A = UA[:, u, g, :]
                        a = act.do(lambda e: e.activation(A, ps[:, :], ACT.Identity, scale=par(wc + 2)), tok, uf[u])
                        b = dve.do(lambda e: e.scalar_tensor_tensor(A[:, 1:S], ps[:, 0:S - 1], par(wc + 1), A[:, 1:S],
                                                                    ALU.mult, ALU.add), a)
                        c = dve.do(lambda e: e.scalar_tensor_tensor(A[:, 2:S], ps[:, 0:S - 2], par(wc), A[:, 2:S],
                                                                    ALU.mult, ALU.add), b)
                        s[g] = c
                        if g == 0:
                            s[0] = act.do(lambda e: e.activation(A, A, ACT.Silu), c)
                        return [c]
                    return f

                i = SLOT_FFN + hf * N_HALF + 2 * j
                yield from fm(i, WB, ev(0), x_tok=xt if f_ == 0 else None)
                yield from fm(i + 1, WB, ev(1))
                m = dve.do(lambda e: e.tensor_tensor(UA[:, u, 0, :], UA[:, u, 0, :], UA[:, u, 1, :], ALU.mult),
                           s[0], s[1])
                t_g[j] = split_out(UA[:, u, 0, :], GH[:, j, :], GL[:, j, :], m, g_free[0])
                uf[u] = t_g[j]

            for hf in range(2):
                t_g = {}
                run(chain(*[up_tile(hf, j) for j in range(11)]))
                t_h2 = {}

                def ev_down(c):
                    def f(t, ps, tok):
                        cs = slice(c * 512, c * 512 + 512)
                        r = dve.do(lambda e: e.tensor_tensor(H[:, t, cs], ps[:, :], H[:, t, cs], ALU.add), tok, t_xs,
                                   t_h[t])
                        t_h2[t] = [*t_h2.get(t, []), r]
                        return [r]
                    return f

                for c in range(2):
                    drain(tm(SLOT_FFN + hf * N_HALF + 22 + 6 * c, 512, 11, ev_down(c), GH, GL, t_g))
                t_h = t_h2
                g_free[0] = t_used[SLOT_FFN + hf * N_HALF + 33]
            t_old = [g_free[0], [t_g[j] for j in range(11)], t_v]
            p2.close()
            pv.close()
        if dbg == 2:
            sp.dma(out.rearrange("(t p) d -> p t d", p=P), H[:, :, :], s_out, 16, [t_h[t] for t in range(4)])
            sp.wait((s_out, 16))

        if dbg is None or dbg > 2:
            p3 = ExitStack()
            act.wait(t_old)
            dve.wait(t_old)
            O = sb("O", [P, 4, D], F, p3)
            SZ = sb("SZ", [P, 4, D], F, p3)
            HI = sb("HI", [P, 4, 402], F, p3)
            AV = sb("AV", [P, 4, S], F, p3)
            LN = sb("LN", [P, 2, D], F, p3)
            sm2 = sb("sm2", [P, 320], F, p3)
            pz = ExitStack()
            SQ = sb("SQ", [P, 2, S], F, pz)
            SK = sb("SK", [P, 2, S], F, pz)
            ph = ExitStack()
            FN = sb("FN", [P, D], F, ph)
            junk = sb("junk3", [P, D], F, ph)
            t_fn = sp.dma(FN[:, :], brow[0, :].partition_broadcast(P), s_misc[0], 16, t_old)
            t_ln = sp.dma(LN[:, :, :], brow[1:3, :].partition_broadcast(P), s_misc[1], 16, t_old)
            t_r = rms_cols(t_h, 8, 1e-5, junk[:, :])
            t_xs = []
            for t in range(4):
                t_xs.append(dve.do(lambda e, t=t: e.scalar_tensor_tensor(
                    H[:, t, :], H[:, t, :], st[:, 8 + t:9 + t], FN[:, :], ALU.mult, ALU.mult), t_r, t_fn))
            ph.close()
            xt = to_XT(H, t_xs, WB + AB, t_used[SLOT_FFN + N_HALF + 21])

            ph = ExitStack()
            HQ = sb("HQ", [P, 3, S], F, ph)
            HK = sb("HK", [P, 3, S], F, ph)
            HB = sb("HB", [P, 3, S], F, ph)
            T1 = sb("T1", [P, 2, S], F, ph)
            QU = sb("QU", [P, 2, 256], F, ph)
            KL = sb("KL", [P, 2, S], F, ph)
            Q1 = sb("Q1", [P, S], F, ph)
            K1 = sb("K1", [P, S], F, ph)
            K2 = sb("K2", [P, 3, 128], F, ph)
            TA = sb("TA", [P, 2, 1280], F, ph)
            act.wait(t_xs)
            dve.wait(t_xs)
            LB = sm2[:, 0:3]
            OML = sm2[:, 3:6]
            LBF = sm2[:, 6:9]
            EX = sm2[:, 9:12]
            LM = sm2[:, 12:15]
            t = dve.do(lambda e: e.tensor_tensor(LM, PPt[:, PP_LB:PP_LB + 3], PPt[:, PP_LB:PP_LB + 3], ALU.subtract), t_par)
            t = act.do(lambda e: e.activation(EX, LM, ACT.Exp), t)
            t = dve.do(lambda e: e.tensor_tensor(LB, EX, EX, ALU.subtract), t)
            t_lb = [dve.do(lambda e: e.tensor_scalar(OML, LB, -1.0, 1.0, ALU.mult, ALU.add), t),
                    dve.do(lambda e: e.tensor_scalar(LBF, LB, 1e-30, None, ALU.max), t)]
            t_kl0 = [dve.do(lambda e, u=u: e.memset(KL[:, u, :], 0.0), t_xs) for u in range(2)]
            ones = sb("onesr", [P, 128], F, ph)
            t_one = dve.do(lambda e: e.memset(ones[:, :], 1.0), t_xs)

            base = SLOT_B2
            t_hb, t_hk, t_hq, t_hv, t_g, t_sq, t_sk, t_av = {}, {}, {}, [], [], {}, {}, []
            t1f = [None, None]

            def ev_f(i):
                def f(ps, tok):
                    u = i % 2
                    a = act.do(lambda e: e.activation(T1[:, u, :], ps[:, :], ACT.Sigmoid), tok, t1f[u])
                    b = act.do(lambda e: e.activation(HK[:, i, :], ps[:, :], ACT.Sigmoid, scale=-1.0), tok)
                    t_hk[i] = dve.do(lambda e: e.tensor_scalar(HK[:, i, :], HK[:, i, :], OML[:, i:i + 1], None, ALU.mult),
                                     b, t_lb)
                    c = act.do(lambda e: e.activation(T1[:, u, :], T1[:, u, :], ACT.Ln, bias=LBF[:, i:i + 1],
                                                      scale=OML[:, i:i + 1]), a, t_lb)
                    r = []
                    for q in range(4):
                        cs = slice(q * 128, q * 128 + 128)
                        r.append(dve.do(lambda e, cs=cs: e.tensor_tensor_scan(
                            HB[:, i, cs], ones[:, :], T1[:, u, cs], 0.0, ALU.mult, ALU.add), c, t_one))
                    t1f[u] = t_hb[i] = r
                    return [a, b]
                return f

            def ev_copy(dst, store, key, scale=None):
                def f(ps, tok):
                    if scale is None:
                        store[key] = act.do(lambda e: e.copy(dst, ps[:, :]), tok)
                    else:
                        store[key] = act.do(lambda e: e.mul(dst, ps[:, :], scale), tok)
                    return [store[key]]
                return f

            def ev_b(t, ps, tok):
                r = act.do(lambda e: e.copy(HI[:, t, 0:384], ps[:, 0:384]), tok)
                g = act.do(lambda e: e.activation(HI[:, t, 384:402], ps[:, 384:402], ACT.Sigmoid), tok)
                t_hv.append(r)
                t_g.append(g)
                return [r, g]

            def ev_a(t, ps, tok):
                t_av.append(act.do(lambda e: e.copy(AV[:, t, :], ps[:, :]), tok))
                return [t_av[-1]]

            PAIRS = [(0, 1), (1, 2), (2, 3), (0, 2), (1, 3), (0, 3)]
            t_ohg = []
            RS = sm2[:, 16:40]
            DEX = sm2[:, 40:52]

            def hgrn(p):
                q, kk_, b = HQ[:, p, :], HK[:, p, :], HB[:, p, :]
                c4 = lambda ap: ap.rearrange("p (c t) -> p c t", c=4)
                tot = c4(b)[:, :, 127:128]
                taf = hg["ta"]
                d = dve.do(lambda e: e.tensor_tensor(c4(T1[:, 0, :]), tot.to_broadcast([P, 4, 128]), c4(b), ALU.subtract),
                           t_hb[p], hg["t"][0])
                x1 = act.do(lambda e: e.activation(T1[:, 1, :], b, ACT.Exp), t_hb[p], hg["t"][1])
                x0 = act.do(lambda e: e.activation(T1[:, 0, :], T1[:, 0, :], ACT.Exp), d)
                s0 = dve.do(lambda e: e.tensor_tensor(DEX[:, 2:3], b[:, 255:256], b[:, 383:384], ALU.add), t_hb[p], hg["dex"])
                s1 = dve.do(lambda e: e.tensor_copy(DEX[:, 0:2], c4(b)[:, 1:3, 127]), t_hb[p], hg["dex"])
                s2 = act.do(lambda e: e.activation(DEX[:, 4:7], DEX[:, 0:3], ACT.Exp), s0, s1)
                q1 = dve.do(lambda e: e.tensor_tensor(Q1[:, :], q, T1[:, 1, :], ALU.mult), x1, t_hq[p], hg["q1"])
                k1 = dve.do(lambda e: e.tensor_tensor(K1[:, :], kk_, T1[:, 0, :], ALU.mult), x0, t_hk[p], hg["q1"])
                hg["t"] = [k1, q1]
                k2 = []
                for m, (blk, col) in enumerate(((0, 4), (1, 5), (0, 6))):
                    k2.append(dve.do(lambda e, m=m, blk=blk, col=col: e.tensor_scalar(
                        K2[:, m, :], K1[:, blk * 128:blk * 128 + 128], DEX[:, col:col + 1], None, ALU.mult), k1, s2, hg["q1"]))
                hg["dex"] = k2
                yield
                t_ta = [[], []]
                for j in range(2):
                    r = slice(64 * j, 64 * j + 64)
                    bk = AB[j]
                    pe.wait(bk.free, t_hk[p], t_hq[p])
                    for c in range(4):
                        cs = slice(c * 128, c * 128 + 128)
                        f = lambda e, r=r, cs=cs, bk=bk: e.matmul(bk.ap[:, cs], kk_[r, cs], q[r, cs], start=True, stop=True)
                        tk = pe.do(f)
                    a = dve.do(lambda e, j=j, bk=bk: e.tensor_tensor(
                        c4(TA[:, j, 0:512]), c4(bk.ap[:, :]),
                        ID.rearrange("p (o t) -> p o t", o=1).to_broadcast([P, 4, 128]), ALU.mult), tk, taf)
                    bk.free = [a]
                    t_ta[j] = [a]
                yield
                t_off = [[], []]
                last = None
                for half in range(2):
                    for j in range(2):
                        r = slice(64 * j, 64 * j + 64)
                        bk = AB[2 + j] if half == 0 else AB[j]
                        pe.wait(bk.free, q1, k1, k2)
                        for m in range(3):
                            ci, cj = PAIRS[3 * half + m]
                            ks = K1[r, ci * 128:ci * 128 + 128] if half == 0 else K2[r, m, :]
                            last = pe.do(lambda e, m=m, ks=ks, r=r, cj=cj, bk=bk: e.matmul(
                                bk.ap[:, m * 128:m * 128 + 128], ks, Q1[r, cj * 128:cj * 128 + 128], start=True, stop=True))
                        a = act.do(lambda e, j=j, half=half, bk=bk: e.copy(
                            TA[:, j, 512 + 384 * half:896 + 384 * half], bk.ap[:, 0:384]), last, taf)
                        bk.free = [a]
                        t_off[j].append(a)
                    yield
                hg["q1"] = last
                for n, L_ in enumerate(LEVELS):
                    u = n % 2
                    nb = S // (2 * L_)
                    v = lambda ap, l=L_: ap.rearrange("p (n h l) -> p n h l", h=2, l=l)
                    bv = v(b)
                    mid = bv[:, :, 0, L_ - 1:L_].to_broadcast([P, nb, L_])
                    tv = T1[:, u, :].rearrange("p (h n l) -> p h n l", h=2, l=L_)
                    d0 = dve.do(lambda e, tv=tv, bv=bv, mid=mid: e.tensor_tensor(tv[:, 0], bv[:, :, 1, :], mid, ALU.subtract),
                                t_hb[p], hg["t"][u])
                    d1 = dve.do(lambda e, tv=tv, bv=bv, mid=mid: e.tensor_tensor(tv[:, 1], mid, bv[:, :, 0, :], ALU.subtract),
                                t_hb[p], hg["t"][u])
                    x = act.do(lambda e, u=u: e.activation(T1[:, u, :], T1[:, u, :], ACT.Exp), d0, d1)
                    yield
                    qv = QU[:, u, :].rearrange("p (n l) -> p n l", l=L_)
                    kv = v(KL[:, u, :])
                    m0 = dve.do(lambda e, tv=tv, qv=qv, v=v: e.tensor_tensor(qv, v(q)[:, :, 1, :], tv[:, 0], ALU.mult),
                                x, hg["qu"][u])
                    m1 = dve.do(lambda e, tv=tv, kv=kv, v=v: e.tensor_tensor(kv[:, :, 0, :], v(kk_)[:, :, 0, :], tv[:, 1], ALU.mult),
                                x, hg["qu"][u], t_kl0)
                    hg["t"][u] = [m0, m1]
                    yield
                    for j in range(2):
                        r = slice(64 * j, 64 * j + 64)
                        bk = AB[2 * u + j]
                        pe.wait(bk.free, m0, m1)
                        for c in range(4):
                            tk = pe.do(lambda e, r=r, u=u, c=c, bk=bk: e.matmul(
                                bk.ap[:, c * 64:c * 64 + 64], KL[r, u, c * 128:c * 128 + 128],
                                QU[r, u, c * 64:c * 64 + 64], start=True, stop=True))
                        nc_ = 64 // L_
                        for c in range(4):
                            o_ = TA[:, j, c * 128:c * 128 + 128].rearrange("p (n h l) -> p n h l", h=2, l=L_)[:, :, 1, :]
                            msk = C[:, C_LEV + 64 * n:C_LEV + 64 * n + 64].bitcast(U32).rearrange("p (n l) -> p n l", l=L_)
                            dat = bk.ap[:, c * 64:c * 64 + 64].rearrange("p (n l) -> p n l", l=L_)
                            a = dve.do(lambda e, o_=o_, msk=msk, dat=dat: e.copy_predicated(o_, msk, dat), tk, t_ta[j])
                        bk.free = [a]
                        t_ta[j] = [a]
                    hg["qu"][u] = tk
                    yield
                bk = AB[0] if p % 2 == 0 else AB[2]
                pe.wait(bk.free, t_ta[0], t_ta[1], t_off[0], t_off[1], t_hv)
                for j in range(2):
                    h = 2 * p + j
                    for cj in range(4):
                        src = [(cj, cj * 128)] + [(ci, 512 + 128 * m) for m, (ci, c2_) in enumerate(PAIRS) if c2_ == cj]
                        for z, (ci, col) in enumerate(src):
                            tk = pe.do(lambda e, j=j, h=h, cj=cj, ci=ci, col=col, z=z, n_=len(src): e.matmul(
                                bk.ap[:, (cj * 2 + j) * 64:(cj * 2 + j) * 64 + 64], TA[:, j, col:col + 128],
                                HI[:, ci, h * 64:h * 64 + 64], start=(z == 0), stop=(z == n_ - 1)))
                hg["ta"] = tk
                ov = O[:, :, 640 + 128 * p:768 + 128 * p]
                bv_ = bk.ap[:, :].rearrange("p (t c) -> p t c", t=4)
                a = act.do(lambda e: e.copy(ov, bv_), tk)
                s = act.do(lambda e: e.activation(T1[:, 0, :], bk.ap[:, :], ACT.Square), tk, hg["t"][0])
                rs = dve.do(lambda e: e.tensor_reduce(
                    RS[:, 8 * p:8 * p + 8], T1[:, 0, :].rearrange("p (g d) -> p g d", d=64), AX.X, ALU.add), s)
                hg["t"][0] = rs
                bk.free = [a, s]
                t_ohg.append([a, rs])
                yield

            hg = {"ta": None, "t": [None, None], "q1": None, "qu": [None, None], "dex": None}
            main = chain(*[fm(base + i, b2, ev_f(i), x_tok=xt if i == 0 else None) for i in range(3)],
                         *[fm(base + 3 + i, b2, ev_copy(HQ[:, i, :], t_hq, i)) for i in range(3)],
                         tm(base + 6, 402, 8, ev_b))
            run(main)
            hg["t"] = [t1f[0], t1f[1]]
            act.quiet(lambda e: e.preload_act_table_set("natural_log_exp_and_others"))
            main = chain(*[fm(base + 10 + i, b2, ev_copy(SQ[:, i, :], t_sq, i, 0.125)) for i in range(2)],
                         *[fm(base + 12 + i, b2, ev_copy(SK[:, i, :], t_sk, i)) for i in range(2)],
                         tm(base + 14, 512, 8, ev_a))
            run(main, chain(*[hgrn(p) for p in range(3)]))
            r = dve.do(lambda e: e.tensor_scalar(RS, RS, 1.0 / 64, 1e-6, ALU.mult, ALU.add), t_ohg)
            r = act.do(lambda e: e.activation(RS, RS, ACT.Sqrt), r)
            r = dve.do(lambda e: e.reciprocal(RS, RS), r)
            t_hgo = []
            for p in range(3):
                for t in range(4):
                    ov = O[:, t, 640 + 128 * p:768 + 128 * p].rearrange("p (j d) -> p j d", d=64)
                    sc = RS[:, 8 * p + 2 * t:8 * p + 2 * t + 2].rearrange("p (j o) -> p j o", o=1).to_broadcast([P, 2, 64])
                    t_hgo.append(dve.do(lambda e, ov=ov, sc=sc: e.tensor_tensor(ov, ov, sc, ALU.mult), r))
            for t in range(4):
                ov = O[:, t, 640:1024]
                t_hgo.append(dve.do(lambda e, ov=ov: e.tensor_tensor(ov, ov, RW[:, R_HG:R_HG + 384], ALU.mult), t_hgo[:12]))
            t_old = [hg["ta"], t_ohg, hg["t"], hg["qu"], hg["dex"], hg["q1"], (dve.sem, dve.count)]
            ph.close()

            ph = ExitStack()
            SPb = sb("SPb", [P, 2, 4, S], F, ph)
            AA = sb("AA", [P, 2, 4, S], F, ph)
            EE = sb("EE", [P, 2, S], F, ph)
            act.wait(t_old)
            dve.wait(t_old)
            STR = C[:, C_STRICT:C_STRICT + 128]
            sf = {"sp": [None, None], "aa": [None, None], "ee": [None, None], "n": 0}
            t_osb = []
            ZB, OB = AB[0:3], AB[3]

            def stick(h):
                u = h % 2
                r = slice(64 * u, 64 * u + 64)
                t_spk, t_a, t_cs = {}, {}, []

                def first(kb):
                    c0 = kb * 128
                    cs = slice(c0, S)
                    zb = ZB[sf["n"] % 3]
                    w = sf["n"] % 2
                    sf["n"] += 1
                    tz = pe.do(lambda e: e.matmul(zb.ap[:, cs], SK[r, h // 2, c0:c0 + 128], SQ[r, h // 2, cs],
                                                  start=True, stop=False, skip_group_check=True),
                               zb.free, t_sq[h // 2], t_sk[h // 2])
                    ee = EE[:, w, cs]
                    a = act.do(lambda e: e.activation(ee, zb.ap[:, cs], ACT.Abs), tz, sf["ee"][w])
                    b = act.do(lambda e: e.activation(ee, ee, ACT.Exp, scale=-1.0), a)
                    c = act.do(lambda e: e.activation(ee, ee, ACT.Ln, bias=1.0), b)
                    d = dve.do(lambda e: e.scalar_tensor_tensor(SPb[:, u, kb, cs], zb.ap[:, cs], 0.0, ee, ALU.max, ALU.add),
                               c, sf["sp"][u])
                    sf["ee"][w] = d
                    dg = SPb[:, u, kb, c0:c0 + 128]
                    t_spk[kb] = [d, dve.do(lambda e: e.tensor_tensor(dg, dg, STR, ALU.mult), d)]
                    return zb

                def second(kb, zb):
                    c0 = kb * 128
                    cs = slice(c0, S)
                    pe.wait(t_spk[kb])
                    f = lambda e: e.matmul(zb.ap[:, cs], C[:, C_NTRI:C_NTRI + 128], SPb[:, u, kb, cs],
                                           start=False, stop=(kb == 3), skip_group_check=True)
                    t_c = pe.do(f)
                    for k2 in range(kb + 1, 4):
                        c2 = slice(k2 * 128, S)
                        t_c = pe.do(lambda e, k2=k2, c2=c2: e.matmul(zb.ap[:, c2], C[:, C_ONE:C_ONE + 128],
                                                                     SPb[:, u, k2, c2], start=False, stop=(k2 == 3),
                                                                     skip_group_check=True))
                    t_cs.append(t_c)
                    a = act.do(lambda e: e.activation(AA[:, u, kb, cs], zb.ap[:, cs], ACT.Exp), t_c, sf["aa"][u])
                    zb.free = [a]
                    dg = AA[:, u, kb, c0:c0 + 128]
                    t_a[kb] = [a, dve.do(lambda e: e.tensor_tensor(dg, dg, STR, ALU.mult), a)]

                zbs = {}
                for kb in (3, 2, 1, 0):
                    zbs[kb] = first(kb)
                    yield
                    if kb < 3:
                        second(kb + 1, zbs[kb + 1])
                        yield
                second(0, zbs[0])
                sf["sp"][u] = t_cs
                yield
                pe.wait(OB.free if u == 0 else None, t_av)
                for qb in range(4):
                    for kb in range(qb + 1):
                        pe.wait(t_a[kb])
                        tk = pe.do(lambda e, qb=qb, kb=kb: e.matmul(
                            OB.ap[:, (qb * 2 + u) * 64:(qb * 2 + u) * 64 + 64], AA[:, u, kb, qb * 128:qb * 128 + 128],
                            AV[:, kb, 256 + h * 64:320 + h * 64], start=(kb == 0), stop=(kb == qb)))
                sf["aa"][u] = tk
                if u == 1:
                    c = 384 + 64 * (h - 1)
                    t_osb.append(act.do(lambda e: e.copy(O[:, :, c:c + 128], OB.ap[:, :].rearrange("p (t c) -> p t c", t=4)), tk))
                    OB.free = [t_osb[-1]]
                yield

            t_sz = {}

            def ev_z(c):
                def f(t, ps, tok):
                    t_sz[c, t] = act.do(lambda e: e.activation(SZ[:, t, c * 512:c * 512 + 512], ps[:, :], ACT.Silu), tok)
                    return [t_sz[c, t]]
                return f

            drain(chain(*[stick(h) for h in range(4)]))
            t_old = [sf["sp"], sf["aa"], sf["ee"]]
            ph.close()
            pz.close()

            ph = ExitStack()
            M = sb("M", [P, 6, U_N], F, ph)
            NQ = sb("NQ", [P, 3, S], F, ph)
            NK = sb("NK", [P, 2, S], F, ph)
            KCT = sb("KCT", [P, 31], F, ph)
            VC = sb("VC", [31, 2, 64], F, ph)
            pc = ExitStack()
            SRC = sb("SRC", [P, 2, S], F, pc)
            BLK = sb("BLK", [P, 32, 31], F, pc)
            W1 = sb("W1", [P, 2, 2048], F, pc)
            W2 = sb("W2", [P, 128], F, pc)
            PO = sb("PO", [P, 32], F, pc)
            HC = sb("HC", [P, 4, 31], F, pc)
            act.wait(t_old)
            dve.wait(t_old)
            sp.dma(W2[:, :], w2c, s_misc[3], 16, t_old)
            t_po = sp.dma(PO[:, :], posT, s_misc[3], 32)
            t_w1 = [sp.dma(W1[:, i, :], w1c[i, :, :], s_misc[4 + i], 16) for i in range(2)]
            src = bass.AP(tensor=vec_dram.tensor, offset=vec_dram.offset + 127, ap=[[6 * 1024 - 1, P], [1024, 6], [1, U_N]])
            t_M = sp.dma(M[:, :, :], src, s_misc[7], 16, t_v)

            t_src, t_nk, t_nq = {}, {}, {}

            def compress():
                w1u = {}
                bk = AB[0]
                done = None
                t_hc = []
                for s in range(2):
                    r = []
                    for a in range(2):
                        sv = SRC[:, s, :].rearrange("p (m b) -> p b m", b=16)[:, :, a:a + 31]
                        pv = PO[:, 16 * a:16 * a + 16].rearrange("p (b o) -> p b o", o=1).to_broadcast([P, 16, 31])
                        r.append(dve.do(lambda e, a=a, sv=sv, pv=pv: e.tensor_tensor(
                            BLK[:, 16 * a:16 * a + 16, :], sv, pv, ALU.add), t_src[s], t_po, done))
                    yield
                    for g in range(2):
                        rr = slice(64 * g, 64 * g + 64)
                        oc = slice((2 * s + g) * 31, (2 * s + g) * 31 + 31)
                        bb = AB[g]
                        pe.wait(bb.free if s == 0 else t_hc, r)
                        for l in range(32):
                            w = (2 * s + l // 16) % 2
                            pe.wait(w1t[2 * s + l // 16])
                            f = lambda e, rr=rr, oc=oc, l=l, w=w, bb=bb: e.matmul(
                                bb.ap[:, oc], W1[rr, w, (l % 16) * 128:(l % 16) * 128 + 128], BLK[rr, l, :],
                                start=(l == 0), stop=(l == 31))
                            tk = pe.do(f)
                            if g == 1 and s == 0 and l % 16 == 15:
                                i = 2 + l // 16
                                w1t[i] = sp.dma(W1[:, i % 2, :], w1c[i, :, :], s_misc[4 + i % 2], 32, tk)
                            if l % 8 == 7:
                                yield
                        h_ = act.do(lambda e, oc=oc, s=s, g=g, bb=bb: e.activation(
                            HC[:, 2 * s + g, :], bb.ap[:, oc], ACT.Gelu_apprx_tanh), tk)
                        t_hc.append(h_)
                    done = tk
                AB[0].free = t_hc
                AB[1].free = t_hc
                bk = AB[2]
                pe.wait(bk.free, t_hc)
                for g in range(2):
                    tk = pe.do(lambda e, g=g: e.matmul(bk.ap[64 * g:64 * g + 64, 0:31], W2[:, 0:64], HC[:, g, :],
                                                       start=True, stop=True))
                a = act.do(lambda e: e.copy(KCT[:, :], bk.ap[:, 0:31]), tk)
                pe.wait(AB[3].free)
                for g in range(2):
                    tk = pe.do(lambda e, g=g: e.matmul(AB[3].ap[0:31, 64 * g:64 * g + 64], HC[:, 2 + g, :], W2[:, 64:128],
                                                       start=True, stop=True))
                b = act.do(lambda e: e.copy(VC[:, :, :], AB[3].ap[0:31, 0:128].rearrange("p (g d) -> p g d", g=2)), tk)
                bk.free = [a]
                AB[3].free = [b]
                t_cmp.extend([a, b])
                yield

            w1t = {0: t_w1[0], 1: t_w1[1]}
            t_cmp = []
            drain(chain(fm(base + 18, b2, ev_copy(SRC[:, 0, :], t_src, 0)), fm(base + 19, b2, ev_copy(SRC[:, 1, :], t_src, 1))))
            run(chain(fm(base + 20, b2, ev_copy(NK[:, 0, :], t_nk, 0)), fm(base + 21, b2, ev_copy(NK[:, 1, :], t_nk, 1)),
                      *[fm(base + 22 + i, b2, ev_copy(NQ[:, i, :], t_nq, i)) for i in range(3)],
                      tm(base + 25, 512, 8, ev_z(0)), tm(base + 29, 512, 8, ev_z(1))),
                compress())
            t_old = [t_cmp]
            pc.close()
            DEP = 3
            SC2 = sb("SC2", [P, DEP, S], F, ph)
            PB2 = sb("PB2", [P, DEP, S], F, ph)
            PT2 = sb("PT2", [P, DEP, S], F, ph)
            OT = sb("OT", [P, 2, 384], F, ph)
            act.wait(t_old)
            dve.wait(t_old)
            NMn = sm2[:, 64:136]
            Ln_ = sm2[:, 136:208]
            CF = sm2[:, 208:280]
            idx = lambda br, qb, h: (br * 4 + qb) * 6 + h
            fr = {"sc": [None] * DEP, "pb": [None] * DEP, "pt": [None] * DEP, "n": 0, "ot": [None, None]}
            SBK, TBK, OBK = WB[0:3], [WB[3], AB[0], AB[1]], [AB[2], AB[3]]
            t_pv, t_ex = {}, {}
            t_onsa = {}
            t_mx, t_mt = {}, [[] for _ in range(4)]

            def inst(br, qb, h):
                u = fr["n"] % DEP
                fr["n"] += 1
                g, i = h // 3, h % 3
                r = slice(64 * g, 64 * g + 64)
                sbk, tbk = SBK[u], TBK[u]
                if br == 0:
                    w, kT, tks = 31, KCT[r, :], t_cmp
                    u0 = 384 - 128 * qb + 31
                    bias = M[:, h, u0:u0 + 16 * 30 + 1:16]
                else:
                    w, kT, tks = 128 * qb + 128, NK[r, br - 1, 0:128 * qb + 128], t_nk[br - 1]
                    bias = M[:, h, 384 - 128 * qb:512]
                n = idx(br, qb, h)
                ts = pe.do(lambda e: e.matmul(sbk.ap[:, 0:w], NQ[r, i, qb * 128:qb * 128 + 128], kT, start=True, stop=True),
                           sbk.free, t_nq[i], tks)
                tt = dve.do(lambda e: e.tensor_tensor_reduce(SC2[:, u, 0:w], sbk.ap[:, 0:w], bias, -0.125, BIG,
                                                             ALU.add, ALU.min, NMn[:, n:n + 1]), ts, t_M, fr["sc"][u])
                sbk.free = [tt]
                ex = act.do(lambda e: e.activation(PB2[:, u, 0:w], SC2[:, u, 0:w], ACT.Exp, bias=NMn[:, n:n + 1], scale=-1.0,
                                                   accum_out=Ln_[:, n:n + 1]), tt, fr["pb"][u])
                fr["sc"][u] = ex
                t_ex[br, qb, h] = ex
                yield
                yield
                nb = max(w // 128, 1)
                pe.wait(tbk.free, ex)
                if br == 0:
                    tp = pe.do(lambda e: e.transpose(tbk.ap[0:31, 0:128], PB2[:, u, 0:31], ID))
                    cp = dve.do(lambda e: e.tensor_copy(PT2[0:31, u, 0:128], tbk.ap[0:31, 0:128]), tp, fr["pt"][u])
                else:
                    for c in range(nb):
                        tp = pe.do(lambda e, c=c: e.transpose(tbk.ap[:, c * 128:c * 128 + 128], PB2[:, u, c * 128:c * 128 + 128], ID))
                    if h % 2:
                        cp = dve.do(lambda e: e.tensor_copy(PT2[:, u, 0:w], tbk.ap[:, 0:w]), tp, fr["pt"][u])
                    else:
                        cp = act.do(lambda e: e.copy(PT2[:, u, 0:w], tbk.ap[:, 0:w]), tp, fr["pt"][u])
                fr["pb"][u] = tp
                tbk.free = [cp]
                yield
                ob = OBK[(qb * 3 + br) % 2]
                pe.wait(cp, ob.free if h == 0 else None, t_av)
                for c in range(nb):
                    if br == 0:
                        f = lambda e: e.matmul(ob.ap[:, h * 64:h * 64 + 64], PT2[0:31, u, 0:128], VC[:, g, :], start=True, stop=True)
                    else:
                        vs = AV[:, c, 128 * (br - 1) + 64 * g:128 * (br - 1) + 64 * g + 64]
                        f = lambda e, c=c, vs=vs: e.matmul(ob.ap[:, h * 64:h * 64 + 64], PT2[:, u, c * 128:c * 128 + 128], vs,
                                                           start=(c == 0), stop=(c == nb - 1))
                    tk = pe.do(f)
                fr["pt"][u] = tk
                if h == 5:
                    m = idx(br, qb, 0)
                    cf = CF[:, m:m + 6]
                    a = dve.do(lambda e: e.reciprocal(cf, Ln_[:, m:m + 6]), [t_ex[br, qb, k] for k in range(6)])
                    gt = HI[:, qb, 384 + br:402:3]
                    a = dve.do(lambda e: e.tensor_tensor(cf, cf, gt, ALU.mult), a, t_g)
                    if br == 0 and qb == 0:
                        a = dve.do(lambda e: e.tensor_scalar(cf, cf, C[:, C_ROW:C_ROW + 1], None, ALU.mult), a)
                    o3 = ob.ap[:, 0:384].rearrange("p (h d) -> p h d", d=64)
                    cb = cf.rearrange("p (h o) -> p h o", o=1).to_broadcast([P, 6, 64])
                    ov = O[:, qb, 0:384]
                    if br == 0:
                        t_onsa[qb] = dve.do(lambda e: e.tensor_tensor(ov.rearrange("p (h d) -> p h d", d=64), o3, cb, ALU.mult), a, tk)
                        ob.free = [t_onsa[qb]]
                    else:
                        w_ = br % 2
                        b = dve.do(lambda e: e.tensor_tensor(OT[:, w_, :].rearrange("p (h d) -> p h d", d=64), o3, cb, ALU.mult),
                                   a, tk, fr["ot"][w_])
                        ob.free = [b]
                        t_onsa[qb] = fr["ot"][w_] = dve.do(lambda e: e.tensor_tensor(ov, ov, OT[:, w_, :], ALU.add), b, t_onsa[qb])
                yield

            def mix(qb, lo, hi, *toks):
                return dve.do(lambda e: e.tensor_tensor(O[:, qb, lo:hi], O[:, qb, lo:hi], SZ[:, qb, lo:hi], ALU.mult), *toks)

            def turn(qb, half, bk, *toks):
                pe.wait(bk.free, *toks)
                for k in range(4):
                    kt = 4 * half + k
                    tk = pe.do(lambda e, k=k, kt=kt: e.transpose(bk.ap[:, k * 128:k * 128 + 128], O[:, qb, kt * 128:kt * 128 + 128], ID))
                cs = slice(qb * 128, qb * 128 + 128)
                r = split_out(bk.ap[:, :].rearrange("p (k t) -> p k t", k=4), XH[:, 4 * half:4 * half + 4, cs],
                              XL[:, 4 * half:4 * half + 4, cs], tk)
                bk.free = r
                t_mt[qb] += r

            def flight(specs, depth):
                live = []
                specs = list(specs)
                while specs or live:
                    if specs and len(live) < depth:
                        live.append(inst(*specs.pop(0)))
                    for g_ in list(live):
                        try:
                            next(g_)
                        except StopIteration:
                            live.remove(g_)
                    yield

            for qb in range(4):
                t_mx[qb] = mix(qb, 384, 1024, t_osb, t_hgo, t_sz[0, qb], t_sz[1, qb])
            for qb in range(4):
                drain(flight([(br, qb, h) for br in range(3) for h in range(6)], DEP))
                m = mix(qb, 0, 384, t_onsa[qb], t_sz[0, qb])
                turn(qb, 0, TBK[0], m, t_mx[qb])
                turn(qb, 1, TBK[1], t_mx[qb])
            ph.close()

            t_y = {}
            STt = sm2[:, 280:320]
            bst = sm2[:, 64:112]
            mv = sm2[:, 112:120]

            def ev_out(c):
                def f(t, ps, tok):
                    hs = H[:, t, c * 512:c * 512 + 512]
                    y = dve.do(lambda e: e.scalar_tensor_tensor(hs, hs, 2.0 ** 0.25, ps[:, :], ALU.mult, ALU.add), tok, t_xs)
                    s = dve.do(lambda e: e.bn_stats(bst[:, 12 * t + 6 * c:12 * t + 6 * c + 6], hs), y)
                    t_y[t] = [*t_y.get(t, []), y, s]
                    if c == 1:
                        m2 = mv[:, 2 * t:2 * t + 2]
                        a = dve.do(lambda e: e.bn_aggr(m2, bst[:, 12 * t:12 * t + 12]), t_y[t])
                        a = dve.do(lambda e: e.tensor_scalar(m2[:, 1:2], m2[:, 1:2], 1e-5, None, ALU.add), a)
                        a = act.do(lambda e: e.activation(m2[:, 1:2], m2[:, 1:2], ACT.Sqrt), a)
                        a = dve.do(lambda e: e.reciprocal(m2[:, 1:2], m2[:, 1:2]), a)
                        a = dve.do(lambda e: e.tensor_scalar(H[:, t, :], H[:, t, :], m2[:, 0:1], m2[:, 1:2], ALU.subtract, ALU.mult), a)
                        a = dve.do(lambda e: e.tensor_tensor(H[:, t, :], H[:, t, :], LN[:, 0, :], ALU.mult), a, t_ln)
                        a = dve.do(lambda e: e.tensor_tensor(H[:, t, :], H[:, t, :], LN[:, 1, :], ALU.add), a)
                        sp.dma(out[t * P:(t + 1) * P, :], H[:, t, :], s_out, 16 * (t + 1), a)
                    return [y]
                return f

            dve.wait(t_mt)
            for c in range(2):
                drain(tm(SLOT_WOUT2 + 4 * c, 512, 8, ev_out(c), x_tok=[t_mt] * 8))
            sp.wait((s_out, 64))
            p3.close()

        block = ctx.enter_context(nc.Block())

        @block.sync
        def _(e):
            sp.play(e)

        @block.tensor
        def _(e):
            pe.play(e)

        @block.scalar
        def _(e):
            act.play(e)

        @block.vector
        def _(e):
            dve.play(e)

        @block.gpsimd
        def _(e):
            pool.play(e)


def constants():
    c = np.zeros((P, C_N), np.float32)
    p = np.arange(P)
    c[:, C_ID:C_ID + 128] = np.eye(P)
    dist = p[:, None] + 128 - np.arange(256)[None]
    c[:, C_BAND:C_BAND + 256] = np.where((dist >= 0) & (dist < 128), 0.0, NEG)
    c[:, C_STRICT:C_STRICT + 128] = p[:, None] < p[None]
    c[:, C_NTRI:C_NTRI + 128] = -(p[:, None] >= p[None]).astype(np.float32)
    for n, L in enumerate(LEVELS):
        t = np.arange(P).reshape(-1, 2, L)[:, 1].reshape(-1)
        same = p[:, None] // (2 * L) == t[None] // (2 * L)
        c[:, C_LEV + 64 * n:C_LEV + 64 * n + 64] = same & ((p[:, None] // L) % 2 == 0)
    c[:, C_ROW] = p >= 31
    c[:, C_ONE:C_ONE + 128] = -1.0
    r = np.arange(S)
    big = np.maximum(r, 1).astype(np.float32) / np.float32(16)
    large = 16 + (np.log(big) / np.float32(np.log(128 / 16)) * np.float32(16)).astype(np.int32)
    bucket = np.where(r < 16, r, np.clip(large, 0, 31))
    oneh = np.zeros((32, S), np.float32)
    oneh[bucket, 511 - r] = 8.0
    return c, oneh


def fm_slot(w, cols):
    return w[:, cols].reshape(-1, P, len(cols)).transpose(1, 0, 2).reshape(P, -1)


def kernel(**inputs):
    import concourse.bacc as bacc
    from concourse.bass_utils import run_bass_kernel_spmd

    a = {k: np.asarray(v) for k, v in inputs.items()}
    cst, oneh = constants()
    w_in, w_up, w_dn, w_out = a["w_in"][0], a["w_up"][0], a["w_down"][0], a["w_out"][0]
    wa, wc = a["w_attn_branch"][0], a["w_conv_branch"][0]
    w2, wo2 = a["w_in_2"][0], a["w_out_2"][0]
    ar = np.arange
    qcols = np.concatenate([np.concatenate([ar(i * 64, i * 64 + 64), ar((i + 4) * 64, (i + 4) * 64 + 64)])
                            for i in range(4)])
    cols1 = np.concatenate([qcols, ar(512, 4352)])
    tiles1 = cols1.reshape(34, P)
    slots = []

    def fms(w, t):
        slots.append(fm_slot(w, t))

    def tms(w, cols, per=2):
        b = w[:, cols].reshape(-1, P, len(cols))
        for s0 in range(0, b.shape[0], per):
            slots.append(b[s0:s0 + per].transpose(1, 0, 2).reshape(P, -1))

    for i in range(6):
        fms(w_in, tiles1[i])
    for c in range(4):
        for j in (10, 14, 6):
            fms(w_in, tiles1[j + c])
    for n in range(8):
        fms(w_in, tiles1[18 + n])
        fms(w_in, tiles1[26 + n])
        cs = ar(n * P, n * P + P)
        slots.append(np.concatenate([fm_slot(wa, cs), fm_slot(wc, cs)], axis=1))
    for c in range(2):
        tms(w_out, ar(c * 512, c * 512 + 512))
    for hf in range(2):
        for j in range(11):
            f = hf * 11 + j
            fms(w_up, ar(f * P, f * P + P))
            fms(w_up, ar((NF + f) * P, (NF + f) * P + P))
        for c in range(2):
            tms(w_dn[hf * 1408:hf * 1408 + 1408], ar(c * 512, c * 512 + 512))
    o = np.cumsum([0, 384, 128, 128, 128, 128, 128, 128, 18, 384, 256, 256, 256, 256, 384, 384, 384, 384])
    (nq, nkc, nvc, nks, nvs, nkw, nvw, ng, nz, sq, sk, sv, sz, hq, hf_, hi_, hz, _) = o
    for i in range(3):
        fms(w2, ar(hf_ + i * P, hf_ + i * P + P))
    for i in range(3):
        fms(w2, ar(hq + i * P, hq + i * P + P))
    tms(w2, np.concatenate([ar(hi_, hi_ + 384), ar(ng, ng + 18)]))
    for b in (sq, sk):
        for i in range(2):
            fms(w2, ar(b + i * P, b + i * P + P))
    tms(w2, np.concatenate([ar(nvs, nvs + 128), ar(nvw, nvw + 128), ar(sv, sv + 256)]))
    for b in (nkc, nvc, nks, nkw):
        fms(w2, ar(b, b + P))
    for i in range(3):
        fms(w2, np.concatenate([ar(nq + i * 64, nq + i * 64 + 64), ar(nq + (i + 3) * 64, nq + (i + 3) * 64 + 64)]))
    tms(w2, np.concatenate([ar(nz, nz + 384), ar(sz, sz + 128)]))
    tms(w2, np.concatenate([ar(sz + 128, sz + 256), ar(hz, hz + 384)]))
    for c in range(2):
        tms(wo2, ar(c * 512, c * 512 + 512))
    assert len(slots) == N_SLOTS, (len(slots), N_SLOTS)
    wp = np.zeros((N_SLOTS, P, 1024), np.float32)
    for i, s in enumerate(slots):
        wp[i, :, :s.shape[1]] = s

    pp = np.zeros((P, PP_N), np.float32)
    pp[:, PP_B:PP_B + 34] = a["b_in"][0][tiles1].T
    pp[:, PP_G1:PP_G1 + 8] = a["mix_norm"][0].reshape(8, P).T
    pp[:, PP_G2:PP_G2 + 8] = a["ffn_norm"][0].reshape(8, P).T
    pp[:, PP_CW:PP_CW + 12] = a["conv_w"][0].reshape(3, 4, P).transpose(2, 1, 0).reshape(P, 12)
    pp[:, PP_FW:PP_FW + 132] = a["ffn_conv_w"][0].reshape(3, 44, P).transpose(2, 1, 0).reshape(P, 132)
    pp[:, PP_LB:PP_LB + 3] = a["hg_lb_2"][0].reshape(3, P).T
    rows = np.concatenate([a["b_in"][0][640:768], a["sinks"][0], a["hg_norm_w_2"][0]])
    brow = np.stack([a["final_norm"], a["ln_g_2"][0], a["ln_b_2"][0]])
    w1c = np.stack([a[n][0][hh * 1024:hh * 1024 + 1024].reshape(16, 64, P).transpose(1, 0, 2).reshape(64, 2048)
                    for n in ("w_ck1_2", "w_cv1_2") for hh in range(2)])
    w1c = np.concatenate([w1c, w1c], axis=1)
    w2c = np.concatenate([a["w_ck2_2"][0], a["w_cv2_2"][0]], axis=1)
    posT = np.ascontiguousarray(np.concatenate([a["cmp_pos_2"][0].T] * 2, axis=0))
    arrays = dict(wp=wp, x=a["x"][0], pp=pp, cst=cst, rows=rows, brow=brow, relb=a["rel_bias_2"], oneh=oneh,
                  w1c=w1c, w2c=w2c, posT=posT)
    arrays = {k: np.ascontiguousarray(v) for k, v in arrays.items()}
    nc = bacc.Bacc("TRN2", target_bir_lowering=False, num_devices=1)
    args = [nc.dram_tensor(k, v.shape, mybir.dt.from_np(v.dtype), kind="ExternalInput").ap() for k, v in arrays.items()]
    out = nc.dram_tensor("y", (S, D), F, kind="ExternalOutput").ap()
    program(nc, *args, out)
    r = run_bass_kernel_spmd(nc, [arrays], core_ids=[0])
    return r.results[0]["y"].reshape(1, S, D)
```

```python
from contextlib import ExitStack

import numpy as np
import concourse.bass as bass
from concourse import mybir

F = mybir.dt.float32
FR = mybir.dt.float32r
U32 = mybir.dt.uint32
ALU = mybir.AluOpType
ACT = mybir.ActivationFunctionType
AX = mybir.AxisListType

P = 128
S = 512
D = 1024
NEG = -1e30
BIG = 3e38

NF = 22
W1 = 0
SLOT_Q = [0, 1, 2, 3]
SLOT_K = 4
SLOT_V = 5
SLOT_CONV = 6
SLOT_GATE = 18
SLOT_WOUT = 42
SLOT_FFN = 50
N_HALF = 22 + 12
SLOT_B2 = SLOT_FFN + 2 * N_HALF
B2_HGF, B2_HGQ, B2_HGI = 0, 3, 6
B2_C, B2_K, B2_Q, B2_V, B2_SQ, B2_SK, B2_Z, N_B2 = 10, 12, 14, 17, 21, 23, 25, 33
SLOT_WOUT2 = SLOT_B2 + N_B2
N_SLOTS = SLOT_WOUT2 + 8

PP_B = 0
PP_G1 = 34
PP_G2 = 42
PP_CW = 50
PP_FW = 62
PP_LB = 194
PP_HG = 197
PP_N = 200
C_ID = 0
C_BAND = 128
C_STRICT = 384
C_NTRI = 512
C_LEV = 640
C_ROW = 640 + 1792
C_ONE = C_ROW + 1
C_N = C_ONE + 128
LEVELS = [64, 32, 16, 8, 4, 2, 1]
R_VB = 0
R_SINK = 128
R_N = 136
SLACK = 3.0


class Queue:

    def __init__(self, sem, us, when):
        self.sem, self.count, self.items, self.seen = sem, 0, [], {}
        self.us, self.when, self.now = us, when, 0.0

    def wait(self, *toks):
        for t in toks:
            if t is None:
                continue
            if isinstance(t, dict):
                t = list(t.values())
            if isinstance(t, list):
                self.wait(*t)
                continue
            sem, value = t
            self.now = max(self.now, self.when[sem.name, value])
            if self.seen.get(sem.name, 0) < value:
                self.seen[sem.name] = value
                self.items.append(lambda e, sem=sem, value=value: e.wait_ge(sem, value))

    def do(self, fn, *waits, us=None):
        self.wait(*waits)
        self.count += 1
        self.items.append(lambda e: fn(e).then_inc(self.sem, 1))
        self.now += us or self.us
        self.when[self.sem.name, self.count] = self.now + 0.2
        return (self.sem, self.count)

    def quiet(self, fn, *waits, us=None):
        self.wait(*waits)
        self.now += us or self.us
        self.items.append(fn)

    def dma(self, out, in_, sem, value, *waits, us=4.0):
        self.wait(*waits)
        self.items.append(lambda e: e.dma_start(out, in_).then_inc(sem, 16))
        self.when[sem.name, value] = self.now + us
        return (sem, value)

    def play(self, e):
        for f in self.items:
            f(e)


class Bank:

    def __init__(self, ap):
        self.ap, self.free = ap, []


class Banks:

    def __init__(self, banks):
        self.idle = list(banks)

    def get(self):
        return self.idle.pop(0) if self.idle else None

    def give(self, bank, toks):
        bank.free = toks
        self.idle.append(bank)


def take(banks):
    yield from until(lambda: banks.idle)
    return banks.get()


def until(cond):
    while not cond():
        yield cond


def leaves(toks):
    if toks is None:
        return []
    if isinstance(toks, dict):
        toks = list(toks.values())
    if isinstance(toks, list):
        return [x for t in toks for x in leaves(t)]
    return [toks]


class Sides:

    def __init__(self, pe, others, when):
        self.pe, self.others, self.when, self.lanes = pe, others, when, []

    def add(self, makers, depth):
        self.lanes.append((list(makers), [], depth))

    def ready_at(self, need):
        if callable(need):
            return 0.0 if need() else None
        return max([self.when[s.name, v] for s, v in leaves(need)], default=0.0)

    def step(self, force=False):
        best = None
        for makers, active, depth in self.lanes:
            while active and active[0][0] is None:
                active.pop(0)
            while makers and len(active) < depth:
                active.append([makers.pop(0)(), None])
            for a in active:
                if a[0] is not None:
                    r = self.ready_at(a[1])
                    if r is not None and (best is None or r < best[0] and best[0] > self.pe.now):
                        best = (r, a)
        if best is None or (best[0] > self.pe.now and not force):
            return False
        try:
            best[1][1] = next(best[1][0])
        except StopIteration:
            best[1][0] = None
        return True

    def run(self, main, slack):
        before = -1.0
        for _ in main:
            stuck = self.pe.now == before
            while max(q.now for q in self.others) < self.pe.now + slack and self.step():
                stuck = False
            if stuck:
                assert self.step(True)
            before = self.pe.now

    def finish(self):
        while self.step(True):
            pass


def program(nc, wp, x, pp, cst, rows, brow, relb, oneh, w1c, w2c, posT, out, dbg=None):
    ctx = ExitStack()
    with ctx:
        def sem(name):
            return ctx.enter_context(nc.semaphore(name))

        def sb(name, shape, dt=F, c=ctx):
            return c.enter_context(nc.sbuf_tensor(name, shape, dt))

        when = {}
        pe, act, dve, pool, sp = (Queue(sem("q_" + n), us, when) for n, us in (
            ("pe", 0.12), ("act", 0.7), ("dve", 0.6), ("pool", 0.5), ("sp", 0.1)))
        NR = NH = 3
        s_w = [sem(f"s_w{i}") for i in range(NR)]
        s_par = sem("s_par")
        s_x = [sem(f"s_x{i}") for i in range(4)]
        s_misc = [sem(f"s_m{i}") for i in range(10)]
        s_out = sem("s_out")

        psum = [ctx.enter_context(nc.psum_tensor(f"ps{i}", [P, S], F)) for i in range(8)]
        banks = Banks([Bank(p) for p in psum])
        sides = Sides(pe, (act, dve), when)

        raw = [sb(f"raw{i}", [P, 1024]) for i in range(NR)]
        whi = [sb(f"whi{i}", [P, 1024], FR) for i in range(NH)]
        wlo = [sb(f"wlo{i}", [P, 1024], FR) for i in range(NH)]
        XH = sb("XH", [P, 8, S], FR)
        XL = sb("XL", [P, 8, S], FR)
        H = sb("H", [P, 4, D])
        PPt = sb("PPt", [P, PP_N])
        C = sb("C", [P, C_N])
        RW = sb("RW", [P, R_N])
        st = sb("st", [P, 64])
        ID = C[:, C_ID:C_ID + 128]
        x2_dram = nc.dram_tensor("x2_dram", [S, D], F, kind="Internal").ap()
        vec_dram = nc.dram_tensor("vec_dram", [P, 6, 1024], F, kind="Internal").ap()

        t_x = []
        for t in range(4):
            t_x.append(act.dma(H[:, t, :], x[t * P:(t + 1) * P, :], s_x[t], 16))
        act.dma(C[:, :], cst, s_par, 16)
        act.dma(PPt[:, :], pp, s_par, 32)
        t_par = act.dma(RW[:, :], rows.partition_broadcast(P), s_par, 48)

        widths = [1024] * N_SLOTS
        for hf in range(2):
            for c in range(2):
                widths[SLOT_FFN + hf * N_HALF + 22 + 6 * c + 5] = 512
        for i in range(4):
            widths[SLOT_B2 + 6 + i] = 804
        t_w, t_hi, t_lo, t_used = {}, {}, {}, {}

        def load(i):
            if i < N_SLOTS:
                w = widths[i]
                t_w[i] = sp.dma(raw[i % NR][:, 0:w], wp[i, :, 0:w], s_w[i % NR], 16 * (i // NR + 1),
                                t_hi.get(i - NR), t_lo.get(i - NR))

        def split(i):
            if i < N_SLOTS and i not in t_hi:
                w = widths[i]
                r, h, lo = raw[i % NR][:, 0:w], whi[i % NH][:, 0:w], wlo[i % NH][:, 0:w]
                t_hi[i] = act.do(lambda e: e.copy(h, r), t_w[i], t_used.get(i - NH), us=1.1)
                t_lo[i] = dve.do(lambda e: e.tensor_tensor(lo, r, h.bitcast(F), ALU.subtract),
                                 t_hi[i], t_used.get(i - NH), us=1.1)
                load(i + NR)

        for i in range(NR):
            load(i)

        def slot(i):
            for j in range(i, i + NH):
                if j - NH < 0 or (j - NH) in t_used:
                    split(j)
            pe.wait(t_hi[i], t_lo[i])
            return whi[i % NH], wlo[i % NH]

        def mm3(out_, ah, al, bh, bl, start, stop_):
            pe.quiet(lambda e: e.matmul(out_, ah, bh, start=start, stop=False), us=0.21)
            pe.quiet(lambda e: e.matmul(out_, ah, bl, start=False, stop=False), us=0.21)
            return lambda e: e.matmul(out_, al, bh, start=False, stop=stop_)

        def fm(i, evac, Xh=None, Xl=None, x_tok=None, nk=8, wk=0, last=True):
            Xh, Xl = Xh or XH, Xl or XL
            b = yield from take(banks)
            wh, wl = slot(i)
            pe.wait(b.free, None if isinstance(x_tok, dict) else x_tok)
            for k in range(nk):
                if isinstance(x_tok, dict):
                    pe.wait(x_tok[k])
                cs = slice((wk + k) * P, (wk + k + 1) * P)
                f = mm3(b.ap[:, :], wh[:, cs], wl[:, cs], Xh[:, k, :], Xl[:, k, :], k == 0, k == nk - 1)
                if k == nk - 1:
                    tok = pe.do(f, us=0.21)
                else:
                    pe.quiet(f, us=0.21)
                    yield
            if last:
                t_used[i] = tok
            banks.give(b, evac(b.ap, tok))
            yield

        def tm(i0, width, nk, evac, Xh=None, Xl=None, x_tok=None, per=2):
            Xh, Xl = Xh or XH, Xl or XL
            bs = []
            for t in range(4):
                bs.append((yield from take(banks)))
            for s0 in range(0, nk, per):
                i = i0 + s0 // per
                ks = range(s0, min(s0 + per, nk))
                wh, wl = slot(i)
                for t in range(4):
                    b = bs[t]
                    if s0 == 0:
                        pe.wait(b.free)
                    for k in ks:
                        if x_tok is not None:
                            pe.wait(x_tok[k])
                        ws = slice((k - s0) * width, (k - s0 + 1) * width)
                        ts = slice(t * P, (t + 1) * P)
                        f = mm3(b.ap[:, 0:width], Xh[:, k, ts], Xl[:, k, ts], wh[:, ws], wl[:, ws],
                                k == 0, k == nk - 1)
                        if k == ks[-1]:
                            tok = pe.do(f, us=0.21 * width / 512)
                        else:
                            pe.quiet(f, us=0.21 * width / 512)
                            yield
                    if t == 3:
                        t_used[i] = tok
                    if ks[-1] == nk - 1:
                        banks.give(b, evac(t, b.ap, tok))
                    yield

        def drain(g):
            for _ in g:
                pass

        def chain(*gs):
            for g in gs:
                yield from g

        def par(col, n=1):
            return PPt[:, col:col + n]

        def split_out(src, hi, lo, *waits, scale=None, bias=None):
            if scale is not None:
                a = act.do(lambda e: e.activation(hi, src, ACT.Identity, scale=scale), *waits)
                d = dve.do(lambda e: e.scalar_tensor_tensor(lo, src, scale, hi.bitcast(F), ALU.mult, ALU.subtract), a, *waits)
            elif bias is not None:
                a = act.do(lambda e: e.activation(hi, src, ACT.Identity, bias=bias), *waits)
                d = dve.do(lambda e: e.scalar_tensor_tensor(lo, src, bias, hi.bitcast(F), ALU.add, ALU.subtract), a, *waits)
            else:
                a = act.do(lambda e: e.copy(hi, src), *waits)
                d = dve.do(lambda e: e.tensor_tensor(lo, src, hi.bitcast(F), ALU.subtract), a, *waits)
            return [a, d]

        def rms_cols(t_h, base, eps, junk):
            sq = []
            for t in range(4):
                sq.append(act.do(lambda e, t=t: e.activation(junk, H[:, t, :], ACT.Square,
                                                             accum_out=st[:, base + t:base + t + 1]),
                                 t_h[t], sq[-1] if sq else None))
            cs = slice(base, base + 4)
            e0 = dve.do(lambda e: e.tensor_scalar(st[:, cs], st[:, cs], 1.0 / D, eps, ALU.mult, ALU.add), sq)
            a = act.do(lambda e: e.activation(st[:, cs], st[:, cs], ACT.Sqrt), e0)
            return dve.do(lambda e: e.reciprocal(st[:, cs], st[:, cs]), a)

        def to_XT(src, t_src, x_free, gcol=None):
            toks = {}
            for k in range(8):
                b = banks.get()
                pe.wait(b.free, t_src)
                for t in range(4):
                    f = lambda e, b=b, k=k, t=t: e.transpose(b.ap[:, t * P:(t + 1) * P], src[:, t, k * P:(k + 1) * P], ID)
                    if t == 3:
                        tok = pe.do(f)
                    else:
                        pe.quiet(f)
                toks[k] = split_out(b.ap[:, :], XH[:, k, :], XL[:, k, :], tok, x_free,
                                    scale=None if gcol is None else par(gcol + k))
                banks.give(b, toks[k])
            return toks

        p1 = ExitStack()
        junk = sb("junk", [P, D], F, p1)
        XS = sb("XS", [P, 4, D], F, p1)
        t_r = rms_cols(t_x, 0, 1e-5, junk[:, :])
        t_xs = []
        for t in range(4):
            f = lambda e, t=t: e.tensor_scalar(XS[:, t, :], H[:, t, :], st[:, t:t + 1], None, ALU.mult)
            g = lambda e, t=t: e.activation(XS[:, t, :], H[:, t, :], ACT.Identity, scale=st[:, t:t + 1])
            t_xs.append(dve.do(f, t_r, t_x[t]) if t % 2 else act.do(g, t_r, t_x[t]))
        split(0)
        xt = to_XT(XS, [t_xs, t_par], None, PP_G1)
        t_all = [xt[k] for k in range(8)]
        p1.close()

        p1 = ExitStack()
        Q = sb("Q", [P, 4, S], F, p1)
        K = sb("K", [P, S], F, p1)
        V = sb("V", [P, 4, 128], F, p1)
        SC = sb("SC", [P, 3, 2, 256], F, p1)
        PT = sb("PT", [P, 3, 512], F, p1)
        AT = sb("AT", [P, 4, S], F, p1)
        CA = sb("CA", [P, S], F, p1)
        CB = sb("CB", [P, S], F, p1)
        CC = sb("CC", [P, S], F, p1)
        GA = sb("GA", [P, 2, 2, S], F, p1)
        small = sb("small", [P, 4, 4, 8], F, p1)
        ATH = sb("ATH", [P, 4, S], FR, p1)
        ATL = sb("ATL", [P, 4, S], FR, p1)
        CVH = sb("CVH", [P, 4, S], FR, p1)
        CVL = sb("CVL", [P, 4, S], FR, p1)
        MH = sb("MH", [P, 8, S], FR, p1)
        ML = sb("ML", [P, 8, S], FR, p1)
        nsink = small[:, 3, 3, :]
        t_old = t_all

        t_q, t_v = {}, []

        def ev_q(i):
            def f(ps, tok):
                t_q[i] = act.do(lambda e: e.activation(Q[:, i, :], ps[:, :], ACT.Identity, bias=par(PP_B + i)), tok, t_old)
                return [t_q[i]]
            return f

        def ev_k(ps, tok):
            t_q["k"] = act.do(lambda e: e.activation(K[:, :], ps[:, :], ACT.Identity, bias=par(PP_B + 4)), tok, t_old)
            return [t_q["k"]]

        def ev_v(t, ps, tok):
            t_v.append(dve.do(lambda e: e.tensor_tensor(V[:, t, :], ps[:, 0:128], RW[:, R_VB:R_VB + 128], ALU.add),
                              tok, t_par, t_old))
            return [t_v[-1]]

        t_ns = dve.do(lambda e: e.tensor_scalar(nsink, RW[:, R_SINK:R_SINK + 8], -1.0, None, ALU.mult), t_par, t_old)
        drain(chain(
            *[fm(i, ev_q(i), x_tok=xt if i == 0 else None) for i in range(4)],
            fm(SLOT_K, ev_k),
            tm(SLOT_V, 128, 8, ev_v, per=8)))

        nm = lambda qb, h: small[:, 0, qb, h:h + 1]
        ls = lambda qb, h: small[:, 1, qb, h:h + 1]
        t_ath = []
        a1 = {"n": 0, "sc": [None] * 3, "pt": [None] * 3, "l": {}, "o": None, "seq": []}

        def attn1(qb, i):
            u = a1["n"] % 3
            a1["n"] += 1
            k0, kn = (0, 128) if qb == 0 else ((qb - 1) * 128, 256)
            nb = kn // 128
            w = 2 * nb * 128
            sbk = []
            for j in range(2):
                b = yield from take(banks)
                sbk.append(b)
                r = slice(64 * j, 64 * j + 64)
                t_s = pe.do(lambda e, r=r, b=b: e.matmul(b.ap[:, 0:kn], Q[r, i, qb * 128:qb * 128 + 128],
                                                         K[r, k0:k0 + kn], start=True, stop=True),
                            b.free, t_q[i], t_q["k"])
                h = i + 4 * j
                band = C[:, C_BAND + 256 - kn:C_BAND + 256]
                tt = dve.do(lambda e, j=j, h=h, b=b: e.tensor_tensor_reduce(
                    SC[:, u, j, 0:kn], b.ap[:, 0:kn], band, -0.125, nsink[:, h:h + 1],
                    ALU.add, ALU.min, nm(qb, h)), t_s, t_ns, a1["sc"][u])
                banks.give(b, [tt])
                a1["l"][qb, h] = act.do(lambda e, j=j, h=h: e.activation(
                    SC[:, u, j, 0:kn], SC[:, u, j, 0:kn], ACT.Exp, bias=nm(qb, h), scale=-1.0,
                    accum_out=ls(qb, h)), tt)
            yield [a1["l"][qb, i], a1["l"][qb, i + 4]]
            b = yield from take(banks)
            pe.wait(b.free, a1["l"][qb, i], a1["l"][qb, i + 4])
            for j in range(2):
                for c in range(nb):
                    t_t = pe.do(lambda e, j=j, c=c, b=b: e.transpose(
                        b.ap[:, (j * nb + c) * 128:(j * nb + c + 1) * 128], SC[:, u, j, c * 128:(c + 1) * 128], ID))
            a1["sc"][u] = t_t
            t_c = dve.do(lambda e, b=b: e.tensor_copy(PT[:, u, 0:w], b.ap[:, 0:w]), t_t, a1["pt"][u])
            banks.give(b, [t_c])
            yield t_c
            yield from until(lambda: len(a1["seq"]) == qb * 4 + i)
            if i == 0:
                a1["o"] = yield from take(banks)
            bo = a1["o"]
            pe.wait(t_c, t_v[max(qb - 1, 0):qb + 1], bo.free)
            for j in range(2):
                h = i + 4 * j
                for c in range(nb):
                    kb = k0 // 128 + c
                    t_p = pe.do(lambda e, j=j, c=c, h=h, kb=kb: e.matmul(
                        bo.ap[:, h * 64:h * 64 + 64], PT[:, u, (j * nb + c) * 128:(j * nb + c + 1) * 128],
                        V[:, kb, j * 64:j * 64 + 64], start=(c == 0), stop=(c == nb - 1)))
            a1["pt"][u] = t_p
            a1["seq"].append((qb, i))
            assert a1["seq"] == sorted(a1["seq"])
            if i < 3:
                return
            t_l = [a1["l"][qb, h] for h in range(8)]
            sk = small[:, 2, qb, :]
            a = dve.do(lambda e: e.tensor_tensor(sk, small[:, 0, qb, :], nsink, ALU.subtract), t_l)
            a = act.do(lambda e: e.activation(sk, sk, ACT.Exp), a)
            a = dve.do(lambda e: e.tensor_tensor(sk, sk, small[:, 1, qb, :], ALU.add), a)
            a = dve.do(lambda e: e.reciprocal(sk, sk), a)
            o3 = bo.ap[:, :].rearrange("p (h d) -> p h d", d=64)
            a3 = AT[:, qb, :].rearrange("p (h d) -> p h d", d=64)
            g = dve.do(lambda e: e.tensor_tensor(
                a3, o3, sk.rearrange("p (h o) -> p h o", o=1).to_broadcast([P, 8, 64]), ALU.mult), a, t_p)
            banks.give(bo, [g])
            yield
            b = yield from take(banks)
            pe.wait(b.free, g)
            for k in range(4):
                t_t = pe.do(lambda e, k=k, b=b: e.transpose(b.ap[:, k * 128:(k + 1) * 128],
                                                            AT[:, qb, k * 128:(k + 1) * 128], ID))
            src = b.ap[:, :].rearrange("p (k t) -> p k t", k=4)
            r = split_out(src, ATH[:, :, qb * 128:(qb + 1) * 128], ATL[:, :, qb * 128:(qb + 1) * 128], t_t)
            banks.give(b, r)
            t_ath.append(r)
            yield

        t_cv = []
        cv = {"a": None, "b": None, "c": None, "hi": None}

        def conv_tile(c):
            s = {}

            def ev_cc(ps, tok):
                s["cc"] = act.do(lambda e: e.activation(CA[:, :], ps[:, :], ACT.Identity, bias=par(PP_B + 10 + c)),
                                 tok, cv["a"], t_old)
                return [s["cc"]]

            def ev_cx(ps, tok):
                s["p"] = dve.do(lambda e: e.scalar_tensor_tensor(CB[:, :], ps[:, :], par(PP_B + 14 + c), CA[:, :],
                                                                 ALU.add, ALU.mult), tok, s["cc"], cv["b"])
                cv["a"] = s["p"]
                wc = PP_CW + 3 * c
                y2 = act.do(lambda e: e.activation(CC[:, :], CB[:, :], ACT.Identity, scale=par(wc + 2)), s["p"], cv["c"])
                y1 = dve.do(lambda e: e.scalar_tensor_tensor(CC[:, 1:S], CB[:, 0:S - 1], par(wc + 1), CC[:, 1:S],
                                                             ALU.mult, ALU.add), y2)
                s["y"] = dve.do(lambda e: e.scalar_tensor_tensor(CC[:, 2:S], CB[:, 0:S - 2], par(wc), CC[:, 2:S],
                                                                 ALU.mult, ALU.add), y1)
                return [s["p"]]

            def ev_cb(ps, tok):
                z = dve.do(lambda e: e.scalar_tensor_tensor(CB[:, :], ps[:, :], par(PP_B + 6 + c), CC[:, :],
                                                            ALU.add, ALU.mult), tok, s["y"])
                cv["c"] = z
                t_cv.append(split_out(CB[:, :], CVH[:, c, :], CVL[:, c, :], z, t_old))
                cv["b"] = t_cv[-1]
                return [z]

            i = SLOT_CONV + 3 * c
            return chain(fm(i, ev_cc), fm(i + 1, ev_cx), fm(i + 2, ev_cb))

        sides.add([lambda qb=qb, i=i: attn1(qb, i) for qb in range(4) for i in range(4)], 3)
        sides.run(chain(*[conv_tile(c) for c in range(4)]), SLACK)

        t_m = {}
        gaf = [None, None]

        def merge_tile(n):
            u = n % 2
            s = {}

            def ev_g(j):
                def f(ps, tok):
                    s[j] = act.do(lambda e: e.activation(GA[:, u, j, :], ps[:, :], ACT.Sigmoid,
                                                         bias=par(PP_B + 18 + 8 * j + n)), tok, gaf[u], t_old)
                    return [s[j]]
                return f

            def ev_br(j):
                def f(ps, tok):
                    s[2 + j] = dve.do(lambda e: e.tensor_tensor(GA[:, u, j, :], ps[:, :], GA[:, u, j, :], ALU.mult),
                                      tok, s[j])
                    return [s[2 + j]]
                return f

            i = SLOT_GATE + 3 * n
            yield from fm(i, ev_g(0))
            yield from fm(i + 1, ev_g(1))
            yield from until(lambda: len(t_ath) == 4)
            yield from fm(i + 2, ev_br(0), ATH, ATL, t_ath, 4, 0, last=False)
            yield from fm(i + 2, ev_br(1), CVH, CVL, t_cv, 4, 4)
            a = dve.do(lambda e: e.tensor_tensor(GA[:, u, 0, :], GA[:, u, 0, :], GA[:, u, 1, :], ALU.add), s[2], s[3])
            t_m[n] = split_out(GA[:, u, 0, :], MH[:, n, :], ML[:, n, :], a, t_old)
            gaf[u] = t_m[n]

        sides.run(chain(*[merge_tile(n) for n in range(8)]), SLACK)

        t_h = {}

        def ev_wout(c):
            def f(t, ps, tok):
                cs = slice(c * 512, c * 512 + 512)
                r = dve.do(lambda e: e.tensor_tensor(H[:, t, cs], ps[:, :], H[:, t, cs], ALU.add), tok, t_x[t],
                           t_xs)
                t_h[t] = [*t_h.get(t, []), r]
                return [r]
            return f

        for c in range(2):
            drain(tm(SLOT_WOUT + 4 * c, 512, 8, ev_wout(c), MH, ML, t_m))
        t_pe_wout = t_used[SLOT_WOUT + 7]
        p1.close()
        if dbg == 1:
            sp.dma(out.rearrange("(t p) d -> p t d", p=P), H[:, :, :], s_out, 16, [t_h[t] for t in range(4)])
            sp.wait((s_out, 16))

        if dbg is None or dbg > 1:
            pv = ExitStack()
            OH = sb("OH", [32, S], F, pv)
            RB = sb("RB", [32, 6], F, pv)
            RBB = sb("RBB", [32, 6, P], F, pv)
            VE = sb("VE", [P, 6, 1024], F, pv)
            t_old = [t_pe_wout, [t_m[n] for n in range(8)]]
            act.wait(t_old)
            dve.wait(t_old)
            sp.dma(OH[:, :], oneh, s_misc[2], 16, t_old)
            t_rb = sp.dma(RB[:, :], relb, s_misc[2], 32)
            t_rbb = dve.do(lambda e: e.tensor_copy(RBB[:, :, :], RB[:, :].rearrange("b (h o) -> b h o", o=1).to_broadcast([32, 6, P])), t_rb)
            v = [dve.do(lambda e: e.memset(VE[:, :, 512:1024], NEG))]
            for h in range(6):
                bk = banks.get()
                tk = pe.do(lambda e, h=h, bk=bk: e.matmul(bk.ap[:, :], RBB[:, h, :], OH[:, :], start=True, stop=True), t_rbb, bk.free)
                v.append(act.do(lambda e, h=h, bk=bk: e.copy(VE[:, h, 0:512], bk.ap[:, :]), tk))
                banks.give(bk, [v[-1]])
            t_v = sp.dma(vec_dram, VE[:, :, :], s_misc[6], 16, v)
            p2 = ExitStack()
            junk = sb("junk2", [P, D], F, p2)
            XS2 = sb("XS2", [P, 4, D], F, p2)
            t_r = rms_cols(t_h, 4, 1e-5, junk[:, :])
            t_xs = []
            for t in range(4):
                f = lambda e, t=t: e.tensor_scalar(XS2[:, t, :], H[:, t, :], st[:, 4 + t:5 + t], None, ALU.mult)
                g = lambda e, t=t: e.activation(XS2[:, t, :], H[:, t, :], ACT.Identity, scale=st[:, 4 + t:5 + t])
                t_xs.append(dve.do(f, t_r) if t % 2 else act.do(g, t_r))
            xt = to_XT(XS2, t_xs, t_used[SLOT_GATE + 23], PP_G2)
            p2.close()
            p2 = ExitStack()
            t_old = [xt[k] for k in range(8)]
            GH = sb("GH", [P, 11, S], FR, p2)
            GL = sb("GL", [P, 11, S], FR, p2)
            UA = sb("UA", [P, 2, 2, S], F, p2)
            uf = [None, None]
            act.wait(t_old)
            dve.wait(t_old)
            g_free = [None]

            def up_tile(hf, j):
                f_ = hf * 11 + j
                u = f_ % 2
                s = {}

                def ev(g):
                    def f(ps, tok):
                        wc = PP_FW + 3 * (f_ + NF * g)
                        A = UA[:, u, g, :]
                        a = act.do(lambda e: e.activation(A, ps[:, :], ACT.Identity, scale=par(wc + 2)), tok, uf[u])
                        b = dve.do(lambda e: e.scalar_tensor_tensor(A[:, 1:S], ps[:, 0:S - 1], par(wc + 1), A[:, 1:S],
                                                                    ALU.mult, ALU.add), a)
                        c = dve.do(lambda e: e.scalar_tensor_tensor(A[:, 2:S], ps[:, 0:S - 2], par(wc), A[:, 2:S],
                                                                    ALU.mult, ALU.add), b)
                        s[g] = c
                        if g == 0:
                            s[0] = act.do(lambda e: e.activation(A, A, ACT.Silu), c)
                        return [c]
                    return f

                i = SLOT_FFN + hf * N_HALF + 2 * j
                yield from fm(i, ev(0), x_tok=xt if f_ == 0 else None)
                yield from fm(i + 1, ev(1))
                m = dve.do(lambda e: e.tensor_tensor(UA[:, u, 0, :], UA[:, u, 0, :], UA[:, u, 1, :], ALU.mult),
                           s[0], s[1])
                t_g[j] = split_out(UA[:, u, 0, :], GH[:, j, :], GL[:, j, :], m, g_free[0])
                uf[u] = t_g[j]

            for hf in range(2):
                t_g = {}
                drain(chain(*[up_tile(hf, j) for j in range(11)]))
                t_h2 = {}

                def ev_down(c):
                    def f(t, ps, tok):
                        cs = slice(c * 512, c * 512 + 512)
                        r = dve.do(lambda e: e.tensor_tensor(H[:, t, cs], ps[:, :], H[:, t, cs], ALU.add), tok, t_xs,
                                   t_h[t])
                        t_h2[t] = [*t_h2.get(t, []), r]
                        return [r]
                    return f

                for c in range(2):
                    drain(tm(SLOT_FFN + hf * N_HALF + 22 + 6 * c, 512, 11, ev_down(c), GH, GL, t_g))
                t_h = t_h2
                g_free[0] = t_used[SLOT_FFN + hf * N_HALF + 33]
            t_old = [g_free[0], [t_g[j] for j in range(11)], t_v]
            p2.close()
            pv.close()
        if dbg == 2:
            sp.dma(out.rearrange("(t p) d -> p t d", p=P), H[:, :, :], s_out, 16, [t_h[t] for t in range(4)])
            sp.wait((s_out, 16))

        if dbg is None or dbg > 2:
            p3 = ExitStack()
            act.wait(t_old)
            dve.wait(t_old)
            A = sb("A", [P, 28248], F, p3)
            sm2 = sb("sm2", [P, 320], F, p3)

            def region(at, *shape, parts=P):
                v = A[0:parts, at:at + int(np.prod(shape))]
                if len(shape) > 1:
                    names = "abcd"[:len(shape)]
                    v = v.rearrange(f"p ({' '.join(names)}) -> p {' '.join(names)}",
                                    **dict(zip(names[1:], shape[1:])))
                return v

            HI = region(0, 4, 402)
            AV = region(1608, 4, S)
            NK = region(3656, 2, S)
            NQ = region(4680, 3, S)
            M = region(6216, 6, 512)
            MC = region(9288, 6, 4, 31)
            KCT = region(10032, 31)
            VC = region(10063, 2, 64, parts=31)
            SRC = region(10200, 2, S)
            BLK = region(11224, 16, 2, 31)
            W1 = region(12216, 2048)
            W2 = region(14264, P)
            PO = region(14392, 16)
            HC = region(14424, 2, 62)
            ME = region(14560, 6, 384)
            DEP = 4
            SC2 = region(10200, DEP, S)
            PT2 = region(12248, DEP, S)
            OT = region(14296, 2, 384)
            SQ = region(15064, 2, S)
            SK = region(16088, 2, S)
            G0 = 17112
            HG = region(G0, 3, 3, S)
            G1 = G0 + 4608
            T1 = region(G1, 2, S)
            SRX = region(G1 + 1024, S)
            KL = region(G1 + 1536, 2, S)
            Q1 = region(G1 + 2560, S)
            K1 = region(G1 + 3072, S)
            K2 = region(G1 + 3584, 3, 128)
            TA = region(G1 + 3968, 2, 1280)
            SZT = region(G0, 8, S)
            SPb = region(G1, 1280)
            AA = region(G1 + 1280, 1280)
            EE = region(G1 + 2560, 2, S)
            MX = region(G1 + 3584, 2, S)
            Y = region(3656, 4, D)
            LN = region(3656 + 4096, 2, D)
            FN = region(G1, D)
            junk = region(G1 + 1024, D)
            O = H
            QU = [H[:, 2 * u:2 * u + 2, 384:640] for u in range(2)]

            t_fn = pool.dma(FN, brow[0, :].partition_broadcast(P), s_misc[0], 16, t_old)
            t_r = rms_cols(t_h, 8, 1e-5, junk)
            t_xs = []
            for t in range(4):
                t_xs.append(dve.do(lambda e, t=t: e.scalar_tensor_tensor(
                    H[:, t, :], H[:, t, :], st[:, 8 + t:9 + t], FN, ALU.mult, ALU.mult), t_r, t_fn))
            xt = to_XT(H, t_xs, t_used[SLOT_FFN + N_HALF + 21])
            t_x2 = pool.dma(x2_dram.rearrange("(t p) d -> p t d", p=P), H[:, :, :], s_misc[8], 16, t_xs)
            t_turned = [xt[k] for k in range(8)]

            LB = sm2[:, 0:3]
            OML = sm2[:, 3:6]
            LBF = sm2[:, 6:9]
            EX = sm2[:, 9:12]
            LM = sm2[:, 12:15]
            RS = sm2[:, 16:40]
            DEX = sm2[:, 40:52]
            NMn = sm2[:, 64:136]
            Ln_ = sm2[:, 136:208]
            CF = sm2[:, 208:280]
            lbp = PPt[:, PP_LB:PP_LB + 3]
            t = dve.do(lambda e: e.tensor_tensor(LM, lbp, lbp, ALU.subtract), t_par)
            t = act.do(lambda e: e.activation(EX, LM, ACT.Exp), t)
            t = dve.do(lambda e: e.tensor_tensor(LB, EX, EX, ALU.subtract), t)
            t_lb = [dve.do(lambda e: e.tensor_scalar(OML, LB, -1.0, 1.0, ALU.mult, ALU.add), t),
                    dve.do(lambda e: e.tensor_scalar(LBF, LB, 1e-30, None, ALU.max), t)]
            t_kl0 = [dve.do(lambda e: e.memset(KL, 0.0), t_xs),
                     dve.do(lambda e: e.memset(H[:, :, 384:640], 0.0), t_x2, t_turned)]
            ones = TA[:, 0, 0:128]
            t_one = dve.do(lambda e: e.memset(ones, 1.0), t_xs)

            base = SLOT_B2
            t_hb, t_hk, t_hq, t_hv, t_g, t_sq, t_sk, t_av = {}, {}, {}, [], [], {}, {}, []
            t_src, t_nk, t_nq, t_sz = {}, {}, {}, {}
            t1f = [None, None]
            LNEXP = "natural_log_exp_and_others"

            def ev_f(i):
                def f(ps, tok):
                    u = i % 2
                    hk, hb = HG[:, i, 1, :], HG[:, i, 2, :]
                    a = act.do(lambda e: e.activation(T1[:, u, :], ps[:, :], ACT.Sigmoid), tok, t1f[u])
                    b = act.do(lambda e: e.activation(hk, ps[:, :], ACT.Sigmoid, scale=-1.0), tok)
                    t_hk[i] = dve.do(lambda e: e.tensor_scalar(hk, hk, OML[:, i:i + 1], None, ALU.mult), b, t_lb)
                    c = act.do(lambda e: e.activation(T1[:, u, :], T1[:, u, :], ACT.Ln, bias=LBF[:, i:i + 1],
                                                      scale=OML[:, i:i + 1]), a, t_lb)
                    r = []
                    for q in range(4):
                        cs = slice(q * 128, q * 128 + 128)
                        r.append(dve.do(lambda e, cs=cs: e.tensor_tensor_scan(
                            hb[:, cs], ones, T1[:, u, cs], 0.0, ALU.mult, ALU.add), c, t_one))
                    t1f[u] = t_hb[i] = r
                    return [a, b]
                return f

            def ev_copy(dst, store, key, scale=None, after=()):
                def f(ps, tok):
                    if scale is None:
                        store[key] = act.do(lambda e: e.copy(dst, ps[:, :]), tok, *after)
                    else:
                        store[key] = act.do(lambda e: e.mul(dst, ps[:, :], scale), tok, *after)
                    return [store[key]]
                return f

            def ev_b(t, ps, tok):
                g = act.do(lambda e: e.activation(HI[:, t, 384:402], ps[:, 384:402], ACT.Sigmoid), tok)
                r = act.do(lambda e: e.copy(HI[:, t, 0:384], ps[:, 0:384]), tok)
                t_hv.append(r)
                t_g.append(g)
                return [r, g]

            def ev_a(t, ps, tok):
                t_av.append(act.do(lambda e: e.copy(AV[:, t, :], ps[:, :]), tok))
                return [t_av[-1]]

            PAIRS = [(0, 1), (1, 2), (2, 3), (0, 2), (1, 3), (0, 3)]
            t_ohg = {}
            hg = {"ta": None, "t": [None, None], "q1": None, "qu": [None, None], "dex": None}
            c4 = lambda ap: ap.rearrange("p (c t) -> p c t", c=4)

            def hgrn(p):
                q, kk_, b = HG[:, p, 0, :], HG[:, p, 1, :], HG[:, p, 2, :]
                tot = c4(b)[:, :, 127:128]
                taf = hg["ta"]
                d = dve.do(lambda e: e.tensor_tensor(c4(T1[:, 0, :]), tot.to_broadcast([P, 4, 128]), c4(b), ALU.subtract),
                           t_hb[p], hg["t"][0])
                x1 = act.do(lambda e: e.activation(T1[:, 1, :], b, ACT.Exp), t_hb[p], hg["t"][1])
                x0 = act.do(lambda e: e.activation(T1[:, 0, :], T1[:, 0, :], ACT.Exp), d)
                s0 = dve.do(lambda e: e.tensor_tensor(DEX[:, 2:3], b[:, 255:256], b[:, 383:384], ALU.add), t_hb[p], hg["dex"])
                s1 = dve.do(lambda e: e.tensor_copy(DEX[:, 0:2], c4(b)[:, 1:3, 127]), t_hb[p], hg["dex"])
                s2 = act.do(lambda e: e.activation(DEX[:, 4:7], DEX[:, 0:3], ACT.Exp), s0, s1)
                t_ta = [None, None]
                yield [t_hk[p], t_hq[p]]
                for j in range(2):
                    r = slice(64 * j, 64 * j + 64)
                    bk = yield from take(banks)
                    pe.wait(bk.free, t_hk[p], t_hq[p])
                    for c in range(4):
                        cs = slice(c * 128, c * 128 + 128)
                        tk = pe.do(lambda e, r=r, cs=cs, bk=bk: e.matmul(bk.ap[:, cs], kk_[r, cs], q[r, cs],
                                                                         start=True, stop=True))
                    t_ta[j] = dve.do(lambda e, j=j, bk=bk: e.tensor_tensor(
                        c4(TA[:, j, 0:512]), c4(bk.ap[:, :]),
                        ID.rearrange("p (o t) -> p o t", o=1).to_broadcast([P, 4, 128]), ALU.mult), tk, taf, t_hb)
                    banks.give(bk, [t_ta[j]])
                q1 = dve.do(lambda e: e.tensor_tensor(Q1, q, T1[:, 1, :], ALU.mult), x1, t_hq[p], hg["q1"])
                k1 = dve.do(lambda e: e.tensor_tensor(K1, kk_, T1[:, 0, :], ALU.mult), x0, t_hk[p], hg["q1"])
                hg["t"] = [k1, q1]
                k2 = []
                for m, (blk, col) in enumerate(((0, 4), (1, 5), (0, 6))):
                    k2.append(dve.do(lambda e, m=m, blk=blk, col=col: e.tensor_scalar(
                        K2[:, m, :], K1[:, blk * 128:blk * 128 + 128], DEX[:, col:col + 1], None, ALU.mult), k1, s2, hg["q1"]))
                hg["dex"] = k2
                t_off = []

                def off(half):
                    for j in range(2):
                        r = slice(64 * j, 64 * j + 64)
                        bk = yield from take(banks)
                        pe.wait(bk.free, q1, k1, k2)
                        for m in range(3):
                            ci, cj = PAIRS[3 * half + m]
                            ks = K1[r, ci * 128:ci * 128 + 128] if half == 0 else K2[r, m, :]
                            hg["q1"] = pe.do(lambda e, m=m, ks=ks, r=r, cj=cj, bk=bk: e.matmul(
                                bk.ap[:, m * 128:m * 128 + 128], ks, Q1[r, cj * 128:cj * 128 + 128], start=True, stop=True))
                        a = act.do(lambda e, j=j, bk=bk: e.copy(
                            TA[:, j, 512 + 384 * half:896 + 384 * half], bk.ap[:, 0:384]), hg["q1"], taf, t_hb)
                        banks.give(bk, [a])
                        t_off.append(a)

                v = lambda ap, l: ap.rearrange("p (n h l) -> p n h l", h=2, l=l)
                tv = lambda u, l: T1[:, u, :].rearrange("p (h n l) -> p h n l", h=2, l=l)

                def prep(n):
                    l, u = LEVELS[n], n % 2
                    bv, o_ = v(b, l), tv(u, l)
                    mid = bv[:, :, 0, l - 1:l].to_broadcast([P, S // (2 * l), l])
                    d0 = dve.do(lambda e: e.tensor_tensor(o_[:, 0], bv[:, :, 1, :], mid, ALU.subtract), t_hb[p], hg["t"][u])
                    d1 = dve.do(lambda e: e.tensor_tensor(o_[:, 1], mid, bv[:, :, 0, :], ALU.subtract), t_hb[p], hg["t"][u])
                    return act.do(lambda e: e.activation(T1[:, u, :], T1[:, u, :], ACT.Exp), d0, d1)

                def mult(n, x):
                    l, u = LEVELS[n], n % 2
                    kv, qs, ks, t_ = v(KL[:, u, :], l), v(q, l), v(kk_, l), tv(u, l)
                    m0 = [dve.do(lambda e, r=slice(64 * j, 64 * j + 64), j=j: e.tensor_tensor(
                        QU[u][r, j].rearrange("p (n l) -> p n l", l=l), qs[r, :, 1, :], t_[r, 0], ALU.mult),
                        x, hg["qu"][u], t_kl0) for j in range(2)]
                    m1 = dve.do(lambda e: e.tensor_tensor(kv[:, :, 0, :], ks[:, :, 0, :], t_[:, 1], ALU.mult),
                                x, hg["qu"][u], t_kl0)
                    hg["t"][u] = [m0, m1]
                    return [m0, m1]

                def prod(n, m):
                    l, u = LEVELS[n], n % 2
                    bk = yield from take(banks)
                    pe.wait(bk.free, m)
                    bj = bk.ap[:, :].rearrange("p (j q) -> p j q", j=2)
                    for c in range(4):
                        tk = pe.do(lambda e, c=c: e.matmul(
                            bj[:, :, c * 64:c * 64 + 64], KL[:, u, c * 128:c * 128 + 128],
                            QU[u][:, :, c * 64:c * 64 + 64], start=True, stop=True), us=0.22)
                    for j in range(2):
                        o_ = TA[:, j, 0:512].rearrange("p (n h l) -> p n h l", h=2, l=l)[:, :, 1, :]
                        msk = C[:, C_LEV + 256 * n:C_LEV + 256 * n + 256].bitcast(U32).rearrange("p (n l) -> p n l", l=l)
                        dat = bj[:, j, :].rearrange("p (n l) -> p n l", l=l)
                        t_ta[j] = dve.do(lambda e, o_=o_, msk=msk, dat=dat: e.copy_predicated(o_, msk, dat), tk, t_ta[j])
                    banks.give(bk, list(t_ta))
                    hg["qu"][u] = tk

                xs, ms = {}, {}
                xs[0] = prep(0)
                yield [q1, k1, k2]
                yield from off(0)
                xs[1] = prep(1)
                ms[0] = mult(0, xs[0])
                yield from off(1)
                for n in range(len(LEVELS)):
                    if n + 2 < len(LEVELS):
                        xs[n + 2] = prep(n + 2)
                    if n + 1 < len(LEVELS):
                        ms[n + 1] = mult(n + 1, xs[n + 1])
                    yield ms[n]
                    yield from prod(n, ms[n])
                yield [t_ta, t_off]
                bk = yield from take(banks)
                pe.wait(bk.free, t_ta, t_off, t_hv)
                for j in range(2):
                    h = 2 * p + j
                    for cj in range(4):
                        src = [(cj, cj * 128)] + [(ci, 512 + 128 * m) for m, (ci, c2_) in enumerate(PAIRS) if c2_ == cj]
                        for z, (ci, col) in enumerate(src):
                            tk = pe.do(lambda e, j=j, h=h, cj=cj, ci=ci, col=col, z=z, n_=len(src): e.matmul(
                                bk.ap[:, (cj * 2 + j) * 64:(cj * 2 + j) * 64 + 64], TA[:, j, col:col + 128],
                                HI[:, ci, h * 64:h * 64 + 64], start=(z == 0), stop=(z == n_ - 1)))
                hg["ta"] = tk
                ov = O[:, :, 640 + 128 * p:768 + 128 * p]
                a = act.do(lambda e: e.copy(ov, bk.ap[:, :].rearrange("p (t c) -> p t c", t=4)), tk, t_x2, t_turned)
                s = act.do(lambda e: e.activation(T1[:, 0, :], bk.ap[:, :], ACT.Square), tk, hg["t"][0])
                rs = dve.do(lambda e: e.tensor_reduce(
                    RS[:, 8 * p:8 * p + 8], T1[:, 0, :].rearrange("p (g d) -> p g d", d=64), AX.X, ALU.add), s)
                hg["t"][0] = rs
                banks.give(bk, [a, s])
                t_ohg[p] = [a, rs]
                yield

            t_hgo = []

            def hgrn_norm():
                r = dve.do(lambda e: e.tensor_scalar(RS, RS, 1.0 / 64, 1e-6, ALU.mult, ALU.add), list(t_ohg.values()))
                r = act.do(lambda e: e.activation(RS, RS, ACT.Sqrt), r)
                act.quiet(lambda e: e.preload_act_table_set(LNEXP))
                r = dve.do(lambda e: e.reciprocal(RS, RS), r)
                done = []
                for p in range(3):
                    for t in range(4):
                        ov = O[:, t, 640 + 128 * p:768 + 128 * p].rearrange("p (j d) -> p j d", d=64)
                        sc = RS[:, 8 * p + 2 * t:8 * p + 2 * t + 2].rearrange("p (j o) -> p j o", o=1).to_broadcast([P, 2, 64])
                        done.append(dve.do(lambda e, ov=ov, sc=sc: e.tensor_tensor(ov, ov, sc, ALU.mult), r))
                    yield
                t_hgo.extend(done)

            STR = C[:, C_STRICT:C_STRICT + 128]
            OFF = [0, 512, 896, 1152]
            sf = {"sp": None, "aa": None, "ee": [None, None], "n": 0, "o": None}
            t_osb = []

            def stick(h):
                yield from until(lambda: h // 2 in t_sk and len(t_av) == 4)
                u = h % 2
                r = slice(64 * u, 64 * u + 64)
                t_spk, t_a, t_cs, zbs = {}, {}, [], {}
                kc = lambda T, kb, c0: T[:, OFF[kb] + c0 - 128 * kb:OFF[kb] + S - 128 * kb]

                def first(kb):
                    c0 = kb * 128
                    cs = slice(c0, S)
                    zb = yield from take(banks)
                    zbs[kb] = zb
                    w = sf["n"] % 2
                    sf["n"] += 1
                    tz = pe.do(lambda e: e.matmul(zb.ap[:, cs], SK[r, h // 2, c0:c0 + 128], SQ[r, h // 2, cs],
                                                  start=True, stop=False, skip_group_check=True),
                               zb.free, t_sq[h // 2], t_sk[h // 2])
                    ee = EE[:, w, cs]
                    a = act.do(lambda e: e.activation(ee, zb.ap[:, cs], ACT.Abs), tz, sf["ee"][w], t_hgdone)
                    b = act.do(lambda e: e.activation(ee, ee, ACT.Exp, scale=-1.0), a)
                    c = act.do(lambda e: e.activation(ee, ee, ACT.Ln, bias=1.0), b)
                    sp_ = kc(SPb, kb, c0)
                    d = dve.do(lambda e: e.scalar_tensor_tensor(sp_, zb.ap[:, cs], 0.0, ee, ALU.max, ALU.add),
                               c, sf["sp"], t_hgdone)
                    sf["ee"][w] = d
                    dg = SPb[:, OFF[kb]:OFF[kb] + 128]
                    t_spk[kb] = [d, dve.do(lambda e: e.tensor_tensor(dg, dg, STR, ALU.mult), d)]

                def second(kb):
                    c0 = kb * 128
                    cs = slice(c0, S)
                    zb = zbs[kb]
                    pe.wait(t_spk[kb])
                    sp_, aa = kc(SPb, kb, c0), kc(AA, kb, c0)
                    t_c = pe.do(lambda e: e.matmul(zb.ap[:, cs], C[:, C_NTRI:C_NTRI + 128], sp_,
                                                   start=False, stop=(kb == 3), skip_group_check=True))
                    for k2 in range(kb + 1, 4):
                        c2 = slice(k2 * 128, S)
                        t_c = pe.do(lambda e, k2=k2, c2=c2: e.matmul(zb.ap[:, c2], C[:, C_ONE:C_ONE + 128],
                                                                     kc(SPb, k2, k2 * 128), start=False, stop=(k2 == 3),
                                                                     skip_group_check=True))
                    t_cs.append(t_c)
                    a = act.do(lambda e: e.activation(aa, zb.ap[:, cs], ACT.Exp), t_c, sf["aa"])
                    banks.give(zb, [a])
                    dg = AA[:, OFF[kb]:OFF[kb] + 128]
                    t_a[kb] = [a, dve.do(lambda e: e.tensor_tensor(dg, dg, STR, ALU.mult), a)]

                for kb in (3, 2, 1, 0):
                    yield from first(kb)
                    if kb < 3:
                        yield t_spk[kb + 1]
                        second(kb + 1)
                yield t_spk[0]
                second(0)
                sf["sp"] = t_cs
                yield t_a
                if u == 0:
                    sf["o"] = yield from take(banks)
                    pe.wait(sf["o"].free)
                ob = sf["o"]
                pe.wait(t_av)
                for qb in range(4):
                    for kb in range(qb + 1):
                        pe.wait(t_a[kb])
                        at = OFF[kb] + 128 * (qb - kb)
                        tk = pe.do(lambda e, qb=qb, kb=kb, at=at: e.matmul(
                            ob.ap[:, (qb * 2 + u) * 64:(qb * 2 + u) * 64 + 64], AA[:, at:at + 128],
                            AV[:, kb, 256 + h * 64:320 + h * 64], start=(kb == 0), stop=(kb == qb)))
                sf["aa"] = tk
                if u == 1:
                    c = 384 + 64 * (h - 1)
                    t_osb.append(act.do(lambda e: e.copy(O[:, :, c:c + 128], ob.ap[:, :].rearrange("p (t c) -> p t c", t=4)),
                                        tk, t_x2, t_turned, t_hgdone))
                    banks.give(ob, [t_osb[-1]])
                yield

            t_cmp, t_mc = [], []

            def compress():
                w1t = t_w1
                t_hc, done, t_blk = [], None, None
                for s in range(2):
                    yield from until(lambda: s in t_src)
                    pool.dma(SRX[0:64, :], SRC[64:128, s, :], s_misc[5], 32 * s + 16, t_src[s], t_xs, t_blk)
                    t_x = pool.dma(SRX[64:128, :], SRC[0:64, s, :], s_misc[5], 32 * s + 32)
                    t_blk = []
                    for j in range(2):
                        rr = slice(64 * j, 64 * j + 64)
                        for g in range(2):
                            src = SRC[rr, s, :] if g == j else SRX[rr, :]
                            for a in range(2):
                                sv = src.rearrange("p (m b k) -> p b k m", b=8, k=2)[:, :, j, a:a + 31]
                                pv_ = PO[rr, 8 * a:8 * a + 8].rearrange("p (b o) -> p b o", o=1).to_broadcast([64, 8, 31])
                                t_blk.append(dve.do(lambda e, rr=rr, g=g, a=a, sv=sv, pv_=pv_: e.tensor_tensor(
                                    BLK[rr, 8 * a:8 * a + 8, g, :], sv, pv_, ALU.add), t_src[s], t_x, t_po, done, us=0.35))
                    yield [t_blk, w1t]
                    bk = yield from take(banks)
                    pe.wait(bk.free, t_blk, w1t)
                    for l in range(16):
                        tk = pe.do(lambda e, l=l, bk=bk: e.matmul(
                            bk.ap[:, 0:62], W1[:, l * 128:l * 128 + 128], BLK[:, l, :, :].rearrange("p g n -> p (g n)"),
                            start=(l == 0), stop=(l == 15)), us=0.22)
                        if l % 4 == 3:
                            yield
                    if s == 0:
                        w1t = pool.dma(W1, w1c[1, :, :], s_misc[4], 32, tk, us=6.0)
                    t_hc.append(act.do(lambda e, s=s, bk=bk: e.activation(
                        HC[:, s, :], bk.ap[:, 0:62], ACT.Gelu_apprx_tanh), tk))
                    banks.give(bk, [t_hc[-1]])
                    act.quiet(lambda e: e.preload_act_table_set(LNEXP))
                    done = tk
                yield t_hc
                bk = yield from take(banks)
                pe.wait(bk.free, t_hc)
                for g in range(2):
                    tk = pe.do(lambda e, g=g: e.matmul(bk.ap[64 * g:64 * g + 64, 0:31], W2[:, 0:64], HC[:, 0, 31 * g:31 * g + 31],
                                                       start=True, stop=True))
                a = act.do(lambda e: e.copy(KCT, bk.ap[:, 0:31]), tk)
                banks.give(bk, [a])
                b2 = yield from take(banks)
                pe.wait(b2.free)
                for g in range(2):
                    tk = pe.do(lambda e, g=g: e.matmul(b2.ap[0:31, 64 * g:64 * g + 64], HC[:, 1, 31 * g:31 * g + 31], W2[:, 64:128],
                                                       start=True, stop=True))
                b = act.do(lambda e: e.copy(VC, b2.ap[0:31, 0:128].rearrange("p (g d) -> p g d", g=2)), tk)
                banks.give(b2, [b])
                for qb in range(4):
                    u0 = 415 - 128 * qb
                    n0 = min(31, (512 - u0 + 15) // 16)
                    if n0:
                        mc, ms_ = MC[:, :, qb, 0:n0], M[:, :, u0:u0 + 16 * n0 - 15:16]
                        t_mc.append(dve.do(lambda e, mc=mc, ms_=ms_: e.tensor_copy(mc, ms_), t_M))
                    if n0 < 31:
                        u1 = u0 + 16 * n0 - 512
                        mc, ms_ = MC[:, :, qb, n0:31], ME[:, :, u1:u1 + 16 * (31 - n0) - 15:16]
                        t_mc.append(dve.do(lambda e, mc=mc, ms_=ms_: e.tensor_copy(mc, ms_), t_M))
                t_cmp.extend([a, b])
                yield

            idx = lambda br, qb, h: (br * 4 + qb) * 6 + h
            fr = {"sc": [None] * DEP, "pt": [None] * DEP, "n": 0, "ot": [None, None], "o": None, "seq": []}
            t_ex, t_onsa, nsa_done = {}, {}, []

            def inst(qb, br, h):
                u = fr["n"] % DEP
                fr["n"] += 1
                g, i = h // 3, h % 3
                r = slice(64 * g, 64 * g + 64)
                if br == 0:
                    w, kT, tks = 31, KCT[r, :], t_cmp
                    bias = MC[:, h, qb, :]
                else:
                    w, kT, tks = 128 * qb + 128, NK[r, br - 1, 0:128 * qb + 128], t_nk[br - 1]
                    bias = M[:, h, 384 - 128 * qb:512]
                n = idx(br, qb, h)
                sbk = yield from take(banks)
                ts = pe.do(lambda e: e.matmul(sbk.ap[:, 0:w], NQ[r, i, qb * 128:qb * 128 + 128], kT, start=True, stop=True),
                           sbk.free, t_nq[i], tks)
                sc = SC2[:, u, 0:w]
                tt = dve.do(lambda e: e.tensor_tensor_reduce(sc, sbk.ap[:, 0:w], bias, -0.125, BIG,
                                                             ALU.add, ALU.min, NMn[:, n:n + 1]),
                            ts, t_M, t_mc, fr["sc"][u], t_cmp)
                banks.give(sbk, [tt])
                ex = act.do(lambda e: e.activation(sc, sc, ACT.Exp, bias=NMn[:, n:n + 1], scale=-1.0,
                                                   accum_out=Ln_[:, n:n + 1]), tt)
                t_ex[br, qb, h] = ex
                yield ex
                nb = max(w // 128, 1)
                tbk = yield from take(banks)
                pe.wait(tbk.free, ex)
                if br == 0:
                    tp = pe.do(lambda e: e.transpose(tbk.ap[0:31, 0:128], SC2[:, u, 0:31], ID))
                    cp = dve.do(lambda e: e.tensor_copy(PT2[0:31, u, 0:128], tbk.ap[0:31, 0:128]), tp, fr["pt"][u], t_cmp)
                else:
                    for c in range(nb):
                        tp = pe.do(lambda e, c=c: e.transpose(tbk.ap[:, c * 128:c * 128 + 128], SC2[:, u, c * 128:c * 128 + 128], ID))
                    if h % 2:
                        cp = dve.do(lambda e: e.tensor_copy(PT2[:, u, 0:w], tbk.ap[:, 0:w]), tp, fr["pt"][u], t_cmp)
                    else:
                        cp = act.do(lambda e: e.copy(PT2[:, u, 0:w], tbk.ap[:, 0:w]), tp, fr["pt"][u], t_cmp)
                fr["sc"][u] = tp
                banks.give(tbk, [cp])
                yield cp
                yield from until(lambda: len(fr["seq"]) == (qb * 3 + br) * 6 + h)
                if h == 0:
                    fr["o"] = yield from take(banks)
                    pe.wait(fr["o"].free)
                ob = fr["o"]
                pe.wait(cp, t_av)
                for c in range(nb):
                    if br == 0:
                        f = lambda e: e.matmul(ob.ap[:, h * 64:h * 64 + 64], PT2[0:31, u, 0:128], VC[:, g, :], start=True, stop=True)
                    else:
                        vs = AV[:, c, 128 * (br - 1) + 64 * g:128 * (br - 1) + 64 * g + 64]
                        f = lambda e, c=c, vs=vs: e.matmul(ob.ap[:, h * 64:h * 64 + 64], PT2[:, u, c * 128:c * 128 + 128], vs,
                                                           start=(c == 0), stop=(c == nb - 1))
                    tk = pe.do(f)
                fr["pt"][u] = tk
                fr["seq"].append((qb, br, h))
                assert fr["seq"] == sorted(fr["seq"])
                if h < 5:
                    return
                m = idx(br, qb, 0)
                cf = CF[:, m:m + 6]
                a = dve.do(lambda e: e.reciprocal(cf, Ln_[:, m:m + 6]), [t_ex[br, qb, k] for k in range(6)])
                gt = HI[:, qb, 384 + br:402:3]
                a = dve.do(lambda e: e.tensor_tensor(cf, cf, gt, ALU.mult), a, t_g)
                if br == 0 and qb == 0:
                    a = dve.do(lambda e: e.tensor_scalar(cf, cf, C[:, C_ROW:C_ROW + 1], None, ALU.mult), a)
                o3 = ob.ap[:, 0:384].rearrange("p (h d) -> p h d", d=64)
                cb = cf.rearrange("p (h o) -> p h o", o=1).to_broadcast([P, 6, 64])
                ov = O[:, qb, 0:384]
                if br == 0:
                    t_onsa[qb] = dve.do(lambda e: e.tensor_tensor(ov.rearrange("p (h d) -> p h d", d=64), o3, cb, ALU.mult),
                                        a, tk, t_x2, t_turned)
                    banks.give(ob, [t_onsa[qb]])
                else:
                    w_ = br % 2
                    b = dve.do(lambda e: e.tensor_tensor(OT[:, w_, :].rearrange("p (h d) -> p h d", d=64), o3, cb, ALU.mult),
                               a, tk, fr["ot"][w_], t_mc)
                    banks.give(ob, [b])
                    t_onsa[qb] = fr["ot"][w_] = dve.do(lambda e: e.tensor_tensor(ov, ov, OT[:, w_, :], ALU.add), b, t_onsa[qb])
                if br == 2:
                    nsa_done.append(tk)

            def ev_z(n):
                def f(ps, tok):
                    z = SZT[:, n, :]
                    a = act.do(lambda e: e.activation(z, ps[:, :], ACT.Silu), tok, t_ohg[n // 3])
                    act.quiet(lambda e: e.preload_act_table_set(LNEXP))
                    t_sz[n] = a
                    if n >= 5:
                        t_sz[n] = dve.do(lambda e: e.tensor_scalar(z, z, par(PP_HG + n - 5), None, ALU.mult), a)
                    return [a]
                return f

            t_mt = [[] for _ in range(4)]
            mxf = [None, None]

            def turn(qb, half):
                yield from until(lambda: len(nsa_done) > qb and len(t_osb) == 2 and t_hgo and main_done)
                bk = yield from take(banks)
                pe.wait(bk.free, t_onsa[qb], t_osb, t_hgo)
                for k in range(4):
                    kt = 4 * half + k
                    tk = pe.do(lambda e, k=k, kt=kt: e.transpose(bk.ap[:, k * 128:k * 128 + 128], O[:, qb, kt * 128:kt * 128 + 128], ID))
                cs = slice(qb * 128, qb * 128 + 128)
                mx = MX[:, half, :].rearrange("p (k t) -> p k t", k=4)
                m = dve.do(lambda e: e.tensor_tensor(mx, bk.ap[:, :].rearrange("p (k t) -> p k t", k=4),
                                                     SZT[:, 4 * half:4 * half + 4, cs], ALU.mult),
                           tk, list(t_sz.values()), mxf[half], t_hgdone)
                banks.give(bk, [m])
                yield
                r = split_out(mx, XH[:, 4 * half:4 * half + 4, cs], XL[:, 4 * half:4 * half + 4, cs], m, t_zmain)
                mxf[half] = r
                t_mt[qb] += r
                yield

            w2_after = [xt[k] for k in range(8)]
            pool.dma(W2, w2c, s_misc[3], 16, w2_after)
            t_po = pool.dma(PO, posT, s_misc[3], 32)
            t_w1 = pool.dma(W1, w1c[0, :, :], s_misc[4], 16)
            row = lambda off_: vec_dram.offset + off_
            pool.dma(M, bass.AP(tensor=vec_dram.tensor, offset=row(127), ap=[[6 * 1024 - 1, P], [1024, 6], [1, 512]]),
                     s_misc[7], 16, t_v)
            t_M = pool.dma(ME, bass.AP(tensor=vec_dram.tensor, offset=row(127 + 512), ap=[[6 * 1024 - 1, P], [1024, 6], [1, 384]]),
                           s_misc[7], 32)
            t_hgdone, main_done, t_zmain = [], [], []

            def note(f):
                f()
                return
                yield

            drain(chain(*[fm(base + B2_HGF + i, ev_f(i), x_tok=xt if i == 0 else None) for i in range(3)],
                        *[fm(base + B2_HGQ + i, ev_copy(HG[:, i, 0, :], t_hq, i)) for i in range(3)],
                        tm(base + B2_HGI, 402, 8, ev_b)))
            hg["t"] = [t1f[0], t1f[1]]
            act.quiet(lambda e: e.preload_act_table_set(LNEXP))

            def hg_end():
                yield from hgrn_norm()
                t_hgdone.extend([hg["ta"], hg["t"], hg["qu"], hg["dex"], hg["q1"]])

            sides.add([lambda p=p: hgrn(p) for p in range(3)] + [hg_end] + [lambda h=h: stick(h) for h in range(4)], 1)
            sides.add([compress], 1)
            sides.run(chain(*[fm(base + B2_C + i, ev_copy(SRC[:, i, :], t_src, i)) for i in range(2)],
                            *[fm(base + B2_K + i, ev_copy(NK[:, i, :], t_nk, i)) for i in range(2)],
                            *[fm(base + B2_Q + i, ev_copy(NQ[:, i, :], t_nq, i)) for i in range(3)],
                            tm(base + B2_V, 512, 8, ev_a),
                            until(lambda: len(t_cmp) > 0)), SLACK)
            sides.add([lambda a=(qb, br, h): inst(*a) for qb in range(4) for br in range(3) for h in range(6)], DEP)
            sides.add([lambda a=(qb, h): turn(*a) for qb in range(4) for h in range(2)], 2)

            def z_tile(n):
                yield from until(lambda: n // 3 in t_ohg)
                yield from fm(base + B2_Z + n, ev_z(n))

            sides.run(chain(*[fm(base + B2_SQ + i, ev_copy(SQ[:, i, :], t_sq, i, 0.125, [t_mc])) for i in range(2)],
                            *[fm(base + B2_SK + i, ev_copy(SK[:, i, :], t_sk, i, None, [t_mc])) for i in range(2)],
                            *[z_tile(n) for n in range(8)]), SLACK)
            main_done.append(True)
            t_zmain.append(t_used[base + B2_Z + 7])
            sides.finish()

            t_end = [nsa_done, t_onsa[3], t_mt, fr["ot"], fr["sc"], fr["pt"]]
            t_Y = pool.dma(Y, x2_dram.rearrange("(t p) d -> p t d", p=P), s_misc[9], 16, t_end)
            t_ln = pool.dma(LN, brow[1:3, :].partition_broadcast(P), s_misc[1], 16)
            t_y = {}
            bst = sm2[:, 64:112]
            mv = sm2[:, 112:120]

            def ev_out(c):
                def f(t, ps, tok):
                    hs = Y[:, t, c * 512:c * 512 + 512]
                    y = dve.do(lambda e: e.scalar_tensor_tensor(hs, hs, 2.0 ** 0.25, ps[:, :], ALU.mult, ALU.add), tok, t_Y)
                    s = dve.do(lambda e: e.bn_stats(bst[:, 12 * t + 6 * c:12 * t + 6 * c + 6], hs), y)
                    t_y[t] = [*t_y.get(t, []), y, s]
                    if c == 1:
                        m2 = mv[:, 2 * t:2 * t + 2]
                        yt = Y[:, t, :]
                        a = dve.do(lambda e: e.bn_aggr(m2, bst[:, 12 * t:12 * t + 12]), t_y[t])
                        a = dve.do(lambda e: e.tensor_scalar(m2[:, 1:2], m2[:, 1:2], 1e-5, None, ALU.add), a)
                        a = act.do(lambda e: e.activation(m2[:, 1:2], m2[:, 1:2], ACT.Sqrt), a)
                        a = dve.do(lambda e: e.reciprocal(m2[:, 1:2], m2[:, 1:2]), a)
                        a = dve.do(lambda e: e.tensor_scalar(yt, yt, m2[:, 0:1], m2[:, 1:2], ALU.subtract, ALU.mult), a)
                        a = dve.do(lambda e: e.tensor_tensor(yt, yt, LN[:, 0, :], ALU.mult), a, t_ln)
                        a = dve.do(lambda e: e.tensor_tensor(yt, yt, LN[:, 1, :], ALU.add), a)
                        sp.dma(out[t * P:(t + 1) * P, :], yt, s_out, 16 * (t + 1), a)
                    return [y]
                return f

            for c in range(2):
                drain(tm(SLOT_WOUT2 + 4 * c, 512, 8, ev_out(c), x_tok=[t_mt] * 8))
            sp.wait((s_out, 64))
            p3.close()

        block = ctx.enter_context(nc.Block())

        @block.sync
        def _(e):
            sp.play(e)

        @block.tensor
        def _(e):
            pe.play(e)

        @block.scalar
        def _(e):
            act.play(e)

        @block.vector
        def _(e):
            dve.play(e)

        @block.gpsimd
        def _(e):
            pool.play(e)


def constants():
    c = np.zeros((P, C_N), np.float32)
    p = np.arange(P)
    c[:, C_ID:C_ID + 128] = np.eye(P)
    dist = p[:, None] + 128 - np.arange(256)[None]
    c[:, C_BAND:C_BAND + 256] = np.where((dist >= 0) & (dist < 128), 0.0, NEG)
    c[:, C_STRICT:C_STRICT + 128] = p[:, None] < p[None]
    c[:, C_NTRI:C_NTRI + 128] = -(p[:, None] >= p[None]).astype(np.float32)
    for n, L in enumerate(LEVELS):
        t = np.arange(P).reshape(-1, 2, L)[:, 1].reshape(-1)
        same = p[:, None] // (2 * L) == t[None] // (2 * L)
        c[:, C_LEV + 256 * n:C_LEV + 256 * n + 256] = np.tile(same & ((p[:, None] // L) % 2 == 0), (1, 4))
    c[:, C_ROW] = p >= 31
    c[:, C_ONE:C_ONE + 128] = -1.0
    r = np.arange(S)
    big = np.maximum(r, 1).astype(np.float32) / np.float32(16)
    large = 16 + (np.log(big) / np.float32(np.log(128 / 16)) * np.float32(16)).astype(np.int32)
    bucket = np.where(r < 16, r, np.clip(large, 0, 31))
    oneh = np.zeros((32, S), np.float32)
    oneh[bucket, 511 - r] = 8.0
    return c, oneh


def fm_slot(w, cols):
    return w[:, cols].reshape(-1, P, len(cols)).transpose(1, 0, 2).reshape(P, -1)


def kernel(**inputs):
    import concourse.bacc as bacc
    from concourse.bass_utils import run_bass_kernel_spmd

    a = {k: np.asarray(v) for k, v in inputs.items()}
    cst, oneh = constants()
    w_in, w_up, w_dn, w_out = a["w_in"][0], a["w_up"][0], a["w_down"][0], a["w_out"][0]
    wa, wc = a["w_attn_branch"][0], a["w_conv_branch"][0]
    w2, wo2 = a["w_in_2"][0], a["w_out_2"][0]
    ar = np.arange
    qcols = np.concatenate([np.concatenate([ar(i * 64, i * 64 + 64), ar((i + 4) * 64, (i + 4) * 64 + 64)])
                            for i in range(4)])
    cols1 = np.concatenate([qcols, ar(512, 4352)])
    tiles1 = cols1.reshape(34, P)
    slots = []

    def fms(w, t):
        slots.append(fm_slot(w, t))

    def tms(w, cols, per=2):
        b = w[:, cols].reshape(-1, P, len(cols))
        for s0 in range(0, b.shape[0], per):
            slots.append(b[s0:s0 + per].transpose(1, 0, 2).reshape(P, -1))

    for i in range(6):
        fms(w_in, tiles1[i])
    for c in range(4):
        for j in (10, 14, 6):
            fms(w_in, tiles1[j + c])
    for n in range(8):
        fms(w_in, tiles1[18 + n])
        fms(w_in, tiles1[26 + n])
        cs = ar(n * P, n * P + P)
        slots.append(np.concatenate([fm_slot(wa, cs), fm_slot(wc, cs)], axis=1))
    for c in range(2):
        tms(w_out, ar(c * 512, c * 512 + 512))
    for hf in range(2):
        for j in range(11):
            f = hf * 11 + j
            fms(w_up, ar(f * P, f * P + P))
            fms(w_up, ar((NF + f) * P, (NF + f) * P + P))
        for c in range(2):
            tms(w_dn[hf * 1408:hf * 1408 + 1408], ar(c * 512, c * 512 + 512))
    o = np.cumsum([0, 384, 128, 128, 128, 128, 128, 128, 18, 384, 256, 256, 256, 256, 384, 384, 384, 384])
    (nq, nkc, nvc, nks, nvs, nkw, nvw, ng, nz, sq, sk, sv, sz, hq, hf_, hi_, hz, _) = o
    for i in range(3):
        fms(w2, ar(hf_ + i * P, hf_ + i * P + P))
    for i in range(3):
        fms(w2, ar(hq + i * P, hq + i * P + P))
    tms(w2, np.concatenate([ar(hi_, hi_ + 384), ar(ng, ng + 18)]))
    for b in (nkc, nvc, nks, nkw):
        fms(w2, ar(b, b + P))
    for i in range(3):
        fms(w2, np.concatenate([ar(nq + i * 64, nq + i * 64 + 64), ar(nq + (i + 3) * 64, nq + (i + 3) * 64 + 64)]))
    tms(w2, np.concatenate([ar(nvs, nvs + 128), ar(nvw, nvw + 128), ar(sv, sv + 256)]))
    for b in (sq, sk):
        for i in range(2):
            fms(w2, ar(b + i * P, b + i * P + P))
    zc = np.concatenate([ar(nz, nz + 384), ar(sz, sz + 256), ar(hz, hz + 384)])
    for i in range(8):
        fms(w2, zc[i * P:i * P + P])
    for c in range(2):
        tms(wo2, ar(c * 512, c * 512 + 512))
    assert len(slots) == N_SLOTS, (len(slots), N_SLOTS)
    wp = np.zeros((N_SLOTS, P, 1024), np.float32)
    for i, s in enumerate(slots):
        wp[i, :, :s.shape[1]] = s

    pp = np.zeros((P, PP_N), np.float32)
    pp[:, PP_B:PP_B + 34] = a["b_in"][0][tiles1].T
    pp[:, PP_G1:PP_G1 + 8] = a["mix_norm"][0].reshape(8, P).T
    pp[:, PP_G2:PP_G2 + 8] = a["ffn_norm"][0].reshape(8, P).T
    pp[:, PP_CW:PP_CW + 12] = a["conv_w"][0].reshape(3, 4, P).transpose(2, 1, 0).reshape(P, 12)
    pp[:, PP_FW:PP_FW + 132] = a["ffn_conv_w"][0].reshape(3, 44, P).transpose(2, 1, 0).reshape(P, 132)
    pp[:, PP_LB:PP_LB + 3] = a["hg_lb_2"][0].reshape(3, P).T
    pp[:, PP_HG:PP_HG + 3] = a["hg_norm_w_2"][0].reshape(3, P).T
    rows = np.concatenate([a["b_in"][0][640:768], a["sinks"][0]])
    brow = np.stack([a["final_norm"], a["ln_g_2"][0], a["ln_b_2"][0]])
    w1c = np.stack([a[n][0].reshape(16, P, P).transpose(1, 0, 2).reshape(P, 2048) for n in ("w_ck1_2", "w_cv1_2")])
    w2c = np.concatenate([a["w_ck2_2"][0], a["w_cv2_2"][0]], axis=1)
    posT = a["cmp_pos_2"][0].reshape(16, P).T
    arrays = dict(wp=wp, x=a["x"][0], pp=pp, cst=cst, rows=rows, brow=brow, relb=a["rel_bias_2"], oneh=oneh,
                  w1c=w1c, w2c=w2c, posT=posT)
    arrays = {k: np.ascontiguousarray(v) for k, v in arrays.items()}
    nc = bacc.Bacc("TRN2", target_bir_lowering=False, num_devices=1)
    args = [nc.dram_tensor(k, v.shape, mybir.dt.from_np(v.dtype), kind="ExternalInput").ap() for k, v in arrays.items()]
    out = nc.dram_tensor("y", (S, D), F, kind="ExternalOutput").ap()
    program(nc, *args, out)
    r = run_bass_kernel_spmd(nc, [arrays], core_ids=[0])
    return r.results[0]["y"].reshape(1, S, D)
```

```python
from contextlib import ExitStack

import numpy as np
import concourse.bass as bass
from concourse import mybir

F = mybir.dt.float32
FR = mybir.dt.float32r
U32 = mybir.dt.uint32
ALU = mybir.AluOpType
ACT = mybir.ActivationFunctionType
AX = mybir.AxisListType

P = 128
S = 512
D = 1024
NEG = -1e30
BIG = 3e38

NF = 22
SLOT_K = 4
SLOT_V = 5
SLOT_CONV = 6
SLOT_GATE = 18
SLOT_WOUT = 42
SLOT_FFN = 50
N_HALF = 22 + 12
SLOT_B2 = SLOT_FFN + 2 * N_HALF
B2_HGF, B2_HGQ, B2_HGI = 0, 3, 6
B2_C, B2_K, B2_Q, B2_V, B2_SQ, B2_SK, B2_Z, N_B2 = 10, 12, 14, 17, 21, 23, 25, 33
SLOT_WOUT2 = SLOT_B2 + N_B2
N_SLOTS = SLOT_WOUT2 + 8

PP_B = 0
PP_CW = 34
PP_FW = 46
PP_LB = 178
PP_HG = 181
PP_N = 184
C_ID = 0
C_BAND = 128
C_STRICT = 384
C_NTRI = 512
C_LEV = 640
C_ROW = 640 + 1792
C_ONE = C_ROW + 1
C_N = C_ONE + 128
LEVELS = [64, 32, 16, 8, 4, 2, 1]
R_VB = 0
R_SINK = 128
R_N = 136
DEPTHS = (3, 6)
SLACK = (3.0, 3.0, 3.0, 3.0, 5.0)


class Queue:

    def __init__(self, sem, us, when):
        self.sem, self.count, self.items, self.seen = sem, 0, [], {}
        self.us, self.when, self.now = us, when, 0.0

    def wait(self, *toks):
        for t in toks:
            if t is None:
                continue
            if isinstance(t, dict):
                t = list(t.values())
            if isinstance(t, list):
                self.wait(*t)
                continue
            sem, value = t
            self.now = max(self.now, self.when[sem.name, value])
            if self.seen.get(sem.name, 0) < value:
                self.seen[sem.name] = value
                self.items.append(lambda e, sem=sem, value=value: e.wait_ge(sem, value))

    def do(self, fn, *waits, us=None):
        self.wait(*waits)
        self.count += 1
        self.items.append(lambda e: fn(e).then_inc(self.sem, 1))
        self.now += us or self.us
        self.when[self.sem.name, self.count] = self.now + 0.2
        return (self.sem, self.count)

    def quiet(self, fn, *waits, us=None):
        self.wait(*waits)
        self.now += us or self.us
        self.items.append(fn)

    def dma(self, out, in_, sem, value, *waits, us=4.0):
        self.wait(*waits)
        self.items.append(lambda e: e.dma_start(out, in_).then_inc(sem, 16))
        self.when[sem.name, value] = self.now + us
        return (sem, value)

    def play(self, e):
        for f in self.items:
            f(e)


class Bank:

    def __init__(self, ap):
        self.ap, self.free = ap, []


class Banks:

    def __init__(self, banks):
        self.idle = list(banks)

    def get(self):
        return self.idle.pop(0) if self.idle else None

    def give(self, bank, toks):
        bank.free = toks
        self.idle.append(bank)


def take(banks):
    yield from until(lambda: banks.idle)
    b = banks.get()
    yield b.free
    return b


def until(cond):
    while not cond():
        yield cond


def leaves(toks):
    if toks is None:
        return []
    if isinstance(toks, dict):
        toks = list(toks.values())
    if isinstance(toks, list):
        return [x for t in toks for x in leaves(t)]
    return [toks]


class Sides:

    def __init__(self, pe, others, when):
        self.pe, self.others, self.when, self.lanes = pe, others, when, []

    def add(self, makers, depth):
        self.lanes.append((list(makers), [], depth))

    def ready_at(self, need):
        if callable(need):
            return 0.0 if need() else None
        return max([self.when[s.name, v] for s, v in leaves(need)], default=0.0)

    def step(self, force=False):
        best = None
        for makers, active, depth in self.lanes:
            while active and active[0][0] is None:
                active.pop(0)
            while makers and len(active) < depth:
                active.append([makers.pop(0)(), None])
            for a in active:
                if a[0] is not None:
                    r = self.ready_at(a[1])
                    if r is not None and (best is None or r < best[0] and best[0] > self.pe.now):
                        best = (r, a)
        if best is None or (best[0] > self.pe.now and not force):
            return False
        try:
            best[1][1] = next(best[1][0])
        except StopIteration:
            best[1][0] = None
        return True

    def run(self, main, slack):
        before = -1.0
        for _ in main:
            stuck = self.pe.now == before
            while max(q.now for q in self.others) < self.pe.now + slack and self.step():
                stuck = False
            if stuck:
                self.step(True)
            before = self.pe.now

    def finish(self):
        while self.step(True):
            pass


def program(nc, wp, x, pp, cst, rows, brow, relb, oneh, w1c, w2c, posT, out, dbg=None):
    ctx = ExitStack()
    with ctx:
        def sem(name):
            return ctx.enter_context(nc.semaphore(name))

        def sb(name, shape, dt=F, c=ctx):
            return c.enter_context(nc.sbuf_tensor(name, shape, dt))

        when = {}
        pe, act, dve, pool, sp = (Queue(sem("q_" + n), us, when) for n, us in (
            ("pe", 0.12), ("act", 0.5), ("dve", 0.6), ("pool", 0.5), ("sp", 0.1)))
        NR = NH = 3
        s_w = [sem(f"s_w{i}") for i in range(NR)]
        s_par = sem("s_par")
        s_x = [sem(f"s_x{i}") for i in range(4)]
        s_misc = [sem(f"s_m{i}") for i in range(13)]
        s_out = sem("s_out")

        psum = [ctx.enter_context(nc.psum_tensor(f"ps{i}", [P, S], F)) for i in range(8)]
        banks = Banks([Bank(p) for p in psum])
        sides = Sides(pe, (act, dve), when)

        raw = [sb(f"raw{i}", [P, 1024]) for i in range(NR)]
        whi = [sb(f"whi{i}", [P, 1024], FR) for i in range(NH)]
        wlo = [sb(f"wlo{i}", [P, 1024], FR) for i in range(NH)]
        XH = sb("XH", [P, 8, S], FR)
        XL = sb("XL", [P, 8, S], FR)
        H = sb("H", [P, 4, D])
        PPt = sb("PPt", [P, PP_N])
        C = sb("C", [P, C_N])
        RW = sb("RW", [P, R_N])
        st = sb("st", [P, 64])
        ID = C[:, C_ID:C_ID + 128]
        x2_dram = nc.dram_tensor("x2_dram", [S, D], F, kind="Internal").ap()
        vec_dram = nc.dram_tensor("vec_dram", [P, 6, 1024], F, kind="Internal").ap()

        p1 = ExitStack()
        XS = sb("XS", [P, 4, D], F, p1)
        GR = sb("GR", [P, D], F, p1)
        t_x = [act.dma(H[:, 0, :], x[0:P, :], s_x[0], 16)]
        t_gr = act.dma(GR[:, :], brow[3, :].partition_broadcast(P), s_misc[10], 16)
        t_id = act.dma(ID, cst[:, C_ID:C_ID + 128], s_misc[11], 16)
        for t in range(1, 4):
            t_x.append(act.dma(H[:, t, :], x[t * P:(t + 1) * P, :], s_x[t], 16))
        act.dma(PPt[:, :], pp, s_par, 16)
        act.dma(RW[:, :], rows.partition_broadcast(P), s_par, 32)
        t_par = act.dma(C[:, 128:], cst[:, 128:], s_par, 48)

        widths = [1024] * N_SLOTS
        for hf in range(2):
            for c in range(2):
                widths[SLOT_FFN + hf * N_HALF + 22 + 6 * c + 5] = 512
        for i in range(4):
            widths[SLOT_B2 + 6 + i] = 804
        t_w, t_hi, t_lo, t_used = {}, {}, {}, {}

        def load(i):
            if i < N_SLOTS:
                w = widths[i]
                t_w[i] = sp.dma(raw[i % NR][:, 0:w], wp[i, :, 0:w], s_w[i % NR], 16 * (i // NR + 1),
                                t_hi.get(i - NR), t_lo.get(i - NR))

        def split(i):
            if i < N_SLOTS and i not in t_hi:
                w = widths[i]
                r, h, lo = raw[i % NR][:, 0:w], whi[i % NH][:, 0:w], wlo[i % NH][:, 0:w]
                t_hi[i] = act.do(lambda e: e.copy(h, r), t_w[i], t_used.get(i - NH), us=1.1)
                t_lo[i] = dve.do(lambda e: e.tensor_tensor(lo, r, h.bitcast(F), ALU.subtract),
                                 t_hi[i], t_used.get(i - NH), us=1.1)
                load(i + NR)

        load(0)
        sp.wait(t_x[2])
        load(1)
        load(2)

        def slot(i):
            for j in range(i, i + NH):
                if j - NH < 0 or (j - NH) in t_used:
                    split(j)
            pe.wait(t_hi[i], t_lo[i])
            return whi[i % NH], wlo[i % NH]

        def mm3(out_, ah, al, bh, bl, start, stop_):
            pe.quiet(lambda e: e.matmul(out_, ah, bh, start=start, stop=False), us=0.21)
            pe.quiet(lambda e: e.matmul(out_, ah, bl, start=False, stop=False), us=0.21)
            return lambda e: e.matmul(out_, al, bh, start=False, stop=stop_)

        def fm(i, evac, Xh=None, Xl=None, x_tok=None, nk=8, wk=0, last=True):
            Xh, Xl = Xh or XH, Xl or XL
            b = yield from take(banks)
            wh, wl = slot(i)
            pe.wait(b.free, None if isinstance(x_tok, dict) else x_tok)
            for k in range(nk):
                if isinstance(x_tok, dict):
                    pe.wait(x_tok[k])
                cs = slice((wk + k) * P, (wk + k + 1) * P)
                f = mm3(b.ap[:, :], wh[:, cs], wl[:, cs], Xh[:, k, :], Xl[:, k, :], k == 0, k == nk - 1)
                if k == nk - 1:
                    tok = pe.do(f, us=0.21)
                else:
                    pe.quiet(f, us=0.21)
                    yield
            if last:
                t_used[i] = tok
            banks.give(b, evac(b.ap, tok))
            yield

        def tm(i0, width, nk, evac, Xh=None, Xl=None, x_tok=None, per=2, tail=False):
            Xh, Xl = Xh or XH, Xl or XL
            bs = []
            for t in range(4):
                bs.append((yield from take(banks)))
            groups = [[s0] for s0 in range(0, nk, per)]
            if tail:
                groups[-2:] = [groups[-2] + groups[-1]]
            for grp in groups:
                held = [slot(i0 + s0 // per) for s0 in grp]
                for t in range(4):
                    b = bs[t]
                    if grp[0] == 0:
                        pe.wait(b.free)
                    for s0, (wh, wl) in zip(grp, held):
                        ks = range(s0, min(s0 + per, nk))
                        for k in ks:
                            if callable(x_tok):
                                yield from until(lambda: x_tok(t))
                                pe.wait(x_tok(t))
                            elif x_tok is not None:
                                pe.wait(x_tok[k])
                            ws = slice((k - s0) * width, (k - s0 + 1) * width)
                            ts = slice(t * P, (t + 1) * P)
                            f = mm3(b.ap[:, 0:width], Xh[:, k, ts], Xl[:, k, ts], wh[:, ws], wl[:, ws],
                                    k == 0, k == nk - 1)
                            if k == ks[-1]:
                                tok = pe.do(f, us=0.21 * width / 512)
                            else:
                                pe.quiet(f, us=0.21 * width / 512)
                                yield
                        if t == 3:
                            t_used[i0 + s0 // per] = tok
                        if ks[-1] == nk - 1:
                            banks.give(b, evac(t, b.ap, tok))
                        yield

        def drain(g):
            for _ in g:
                pass

        def chain(*gs):
            for g in gs:
                yield from g

        def par(col, n=1):
            return PPt[:, col:col + n]

        def split_out(src, hi, lo, *waits, scale=None, bias=None):
            if scale is not None:
                a = act.do(lambda e: e.activation(hi, src, ACT.Identity, scale=scale), *waits)
                d = dve.do(lambda e: e.scalar_tensor_tensor(lo, src, scale, hi.bitcast(F), ALU.mult, ALU.subtract), a, *waits)
            elif bias is not None:
                a = act.do(lambda e: e.activation(hi, src, ACT.Identity, bias=bias), *waits)
                d = dve.do(lambda e: e.scalar_tensor_tensor(lo, src, bias, hi.bitcast(F), ALU.add, ALU.subtract), a, *waits)
            else:
                a = act.do(lambda e: e.copy(hi, src), *waits)
                d = dve.do(lambda e: e.tensor_tensor(lo, src, hi.bitcast(F), ALU.subtract), a, *waits)
            return [a, d]

        def norm(base, eps, dst, t_g, grow):
            sums = {}

            def half(t, c, junk, *waits):
                cs = slice(c * 512, c * 512 + 512)
                at = base + 2 * t + c
                sums[t, c] = act.do(lambda e: e.activation(junk, H[:, t, cs], ACT.Square, accum_out=st[:, at:at + 1]), *waits)
                if c == 0:
                    a = st[:, at:at + 1]
                    sums[t, 0] = dve.do(lambda e: e.tensor_scalar(a, a, 1.0 / D, eps, ALU.mult, ALU.add), sums[t, 0], us=0.1)
                    return [sums[t, 0]]
                return sums[t, c]

            def rest(t, *waits):
                at = base + 2 * t
                a, b = st[:, at:at + 1], st[:, at + 1:at + 2]
                k = act.do(lambda e: e.activation(b, b, ACT.Sqrt, bias=a, scale=1.0 / D), sums[t, 0], sums[t, 1], us=0.2)
                k = dve.do(lambda e: e.reciprocal(b, b), k, us=0.1)
                lo_, hi_ = slice(0, 512), slice(512, 1024)
                g = pool.do(lambda e: e.tensor_tensor(dst[:, t, hi_], H[:, t, hi_], grow[:, hi_], ALU.mult),
                            sums[t, 1], t_g, *waits)
                return [dve.do(lambda e: e.scalar_tensor_tensor(
                            dst[:, t, lo_], H[:, t, lo_], b, grow[:, lo_], ALU.mult, ALU.mult), k, t_g, *waits),
                        act.do(lambda e: e.activation(dst[:, t, hi_], dst[:, t, hi_], ACT.Identity, scale=b), k, g)]
            return half, rest

        def turn_rows(src, t_src, x_free, toks):
            for k in range(8):
                toks[k] = []

            def f(t):
                for c in range(2):
                    b = banks.get()
                    pe.wait(b.free, t_src[t][c], t_id)
                    for k in range(4):
                        f = lambda e, b=b, k=k, t=t, c=c: e.transpose(
                            b.ap[:, k * P:(k + 1) * P], src[:, t, (4 * c + k) * P:(4 * c + k + 1) * P], ID)
                        if k == 3:
                            tok = pe.do(f)
                        else:
                            pe.quiet(f)
                    ts = slice(t * P, (t + 1) * P)
                    o = split_out(b.ap[:, :].rearrange("p (k t) -> p k t", k=4), XH[:, 4 * c:4 * c + 4, ts],
                                  XL[:, 4 * c:4 * c + 4, ts], tok, x_free)
                    banks.give(b, o)
                    for k in range(4 * c, 4 * c + 4):
                        toks[k] += o
            return f

        def first_two(i, evs, turn_x, toks):
            bs = [banks.get(), banks.get()]

            def part(s, half):
                j = i + s
                wh, wl = whi[j % NH], wlo[j % NH]
                ts = slice(256 * half, 256 * half + 256)
                pe.wait(bs[s].free, t_hi[j], t_lo[j])
                for k in range(8):
                    pe.wait(toks[k])
                    cs = slice(k * P, (k + 1) * P)
                    f = mm3(bs[s].ap[:, ts], wh[:, cs], wl[:, cs], XH[:, k, ts], XL[:, k, ts], k == 0, k == 7)
                    if k == 7:
                        t_used[j] = pe.do(f, us=0.11)
                    else:
                        pe.quiet(f, us=0.11)

            part(0, 0)
            turn_x(2)
            turn_x(3)
            split(i + 1)
            part(0, 1)
            banks.give(bs[0], evs[0](bs[0].ap, t_used[i]))
            split(i + 2)
            part(1, 0)
            part(1, 1)
            banks.give(bs[1], evs[1](bs[1].ap, t_used[i + 1]))

        act.quiet(lambda e: e.preload_act_table_set("sqrt_and_others"))
        n_half, n_rest = norm(0, 1e-5, XS, t_gr, GR)
        t_xs, xt = [], {}
        turn_x = turn_rows(XS, t_xs, None, xt)
        for t in range(4):
            for c in range(2):
                n_half(t, c, XS[:, t, c * 512:c * 512 + 512], t_x[t])
            t_xs.append(n_rest(t))
            if t in (1, 2):
                turn_x(t - 1)
            if t == 2:
                split(0)
        p1.close()

        p1 = ExitStack()
        Q = sb("Q", [P, 4, S], F, p1)
        K = sb("K", [P, S], F, p1)
        V = sb("V", [P, 4, 128], F, p1)
        SC = sb("SC", [P, DEPTHS[0], 2, 256], F, p1)
        AT = sb("AT", [P, 4, S], F, p1)
        CA = sb("CA", [P, S], F, p1)
        CB = sb("CB", [P, S], F, p1)
        CC = sb("CC", [P, S], F, p1)
        GA = sb("GA", [P, 2, 2, S], F, p1)
        small = sb("small", [P, 4, 4, 8], F, p1)
        ATH = sb("ATH", [P, 4, S], FR, p1)
        ATL = sb("ATL", [P, 4, S], FR, p1)
        CVH = sb("CVH", [P, 4, S], FR, p1)
        CVL = sb("CVL", [P, 4, S], FR, p1)
        MH = sb("MH", [P, 8, S], FR, p1)
        ML = sb("ML", [P, 8, S], FR, p1)
        nsink = small[:, 3, 3, :]
        t_old = [t_par]

        t_q, t_v = {}, []

        def ev_q(i):
            def f(ps, tok):
                t_q[i] = act.do(lambda e: e.activation(Q[:, i, :], ps[:, :], ACT.Identity, bias=par(PP_B + i)), tok, t_old)
                return [t_q[i]]
            return f

        def ev_k(ps, tok):
            t_q["k"] = act.do(lambda e: e.activation(K[:, :], ps[:, :], ACT.Identity, bias=par(PP_B + 4)), tok, t_old)
            return [t_q["k"]]

        def ev_v(t, ps, tok):
            t_v.append(dve.do(lambda e: e.tensor_tensor(V[:, t, :], ps[:, 0:128], RW[:, R_VB:R_VB + 128], ALU.add),
                              tok, t_par, t_old))
            return [t_v[-1]]

        t_ns = dve.do(lambda e: e.tensor_scalar(nsink, RW[:, R_SINK:R_SINK + 8], -1.0, None, ALU.mult), t_par, t_old)
        first_two(0, (ev_q(0), ev_q(1)), turn_x, xt)
        drain(chain(
            *[fm(i, ev_q(i)) for i in (2, 3)],
            fm(SLOT_K, ev_k),
            tm(SLOT_V, 128, 8, ev_v, per=8)))

        nm = lambda qb, h: small[:, 0, qb, h:h + 1]
        ls = lambda qb, h: small[:, 1, qb, h:h + 1]
        t_ath = []
        a1 = {"n": 0, "pt": [None] * DEPTHS[0], "l": {}, "o": None, "seq": []}

        def attn1(qb, i):
            u = a1["n"] % DEPTHS[0]
            a1["n"] += 1
            k0, kn = (0, 128) if qb == 0 else ((qb - 1) * 128, 256)
            nb = kn // 128
            w = 2 * nb * 128
            sbk = []
            for j in range(2):
                b = yield from take(banks)
                sbk.append(b)
                r = slice(64 * j, 64 * j + 64)
                t_s = pe.do(lambda e, r=r, b=b: e.matmul(b.ap[:, 0:kn], Q[r, i, qb * 128:qb * 128 + 128],
                                                         K[r, k0:k0 + kn], start=True, stop=True),
                            b.free, t_q[i], t_q["k"])
                h = i + 4 * j
                band = C[:, C_BAND + 256 - kn:C_BAND + 256]
                tt = dve.do(lambda e, j=j, h=h, b=b: e.tensor_tensor_reduce(
                    SC[:, u, j, 0:kn], b.ap[:, 0:kn], band, -0.125, nsink[:, h:h + 1],
                    ALU.add, ALU.min, nm(qb, h)), t_s, t_ns, a1["pt"][u])
                banks.give(b, [tt])
                a1["l"][qb, h] = act.do(lambda e, j=j, h=h: e.activation(
                    SC[:, u, j, 0:kn], SC[:, u, j, 0:kn], ACT.Exp, bias=nm(qb, h), scale=-1.0,
                    accum_out=ls(qb, h)), tt)
            yield [a1["l"][qb, i], a1["l"][qb, i + 4]]
            b = yield from take(banks)
            pe.wait(b.free, a1["l"][qb, i], a1["l"][qb, i + 4])
            for j in range(2):
                for c in range(nb):
                    t_t = pe.do(lambda e, j=j, c=c, b=b: e.transpose(
                        b.ap[:, (j * nb + c) * 128:(j * nb + c + 1) * 128], SC[:, u, j, c * 128:(c + 1) * 128], ID))
            pt = SC[:, u, :, :].rearrange("p j k -> p (j k)")
            t_c = dve.do(lambda e, b=b: e.tensor_copy(pt[:, 0:w], b.ap[:, 0:w]), t_t)
            banks.give(b, [t_c])
            yield t_c
            yield from until(lambda: len(a1["seq"]) == qb * 4 + i)
            if i == 0:
                a1["o"] = yield from take(banks)
            bo = a1["o"]
            pe.wait(t_c, t_v[max(qb - 1, 0):qb + 1], bo.free)
            for j in range(2):
                h = i + 4 * j
                for c in range(nb):
                    kb = k0 // 128 + c
                    t_p = pe.do(lambda e, j=j, c=c, h=h, kb=kb: e.matmul(
                        bo.ap[:, h * 64:h * 64 + 64], pt[:, (j * nb + c) * 128:(j * nb + c + 1) * 128],
                        V[:, kb, j * 64:j * 64 + 64], start=(c == 0), stop=(c == nb - 1)))
            a1["pt"][u] = t_p
            a1["seq"].append((qb, i))
            assert a1["seq"] == sorted(a1["seq"])
            if i < 3:
                return
            t_l = [a1["l"][qb, h] for h in range(8)]
            sk = small[:, 2, qb, :]
            a = dve.do(lambda e: e.tensor_tensor(sk, small[:, 0, qb, :], nsink, ALU.subtract), t_l)
            a = act.do(lambda e: e.activation(sk, sk, ACT.Exp), a)
            a = dve.do(lambda e: e.tensor_tensor(sk, sk, small[:, 1, qb, :], ALU.add), a)
            a = dve.do(lambda e: e.reciprocal(sk, sk), a)
            o3 = bo.ap[:, :].rearrange("p (h d) -> p h d", d=64)
            a3 = AT[:, qb, :].rearrange("p (h d) -> p h d", d=64)
            g = dve.do(lambda e: e.tensor_tensor(
                a3, o3, sk.rearrange("p (h o) -> p h o", o=1).to_broadcast([P, 8, 64]), ALU.mult), a, t_p)
            banks.give(bo, [g])
            yield
            b = yield from take(banks)
            pe.wait(b.free, g)
            for k in range(4):
                t_t = pe.do(lambda e, k=k, b=b: e.transpose(b.ap[:, k * 128:(k + 1) * 128],
                                                            AT[:, qb, k * 128:(k + 1) * 128], ID))
            src = b.ap[:, :].rearrange("p (k t) -> p k t", k=4)
            r = split_out(src, ATH[:, :, qb * 128:(qb + 1) * 128], ATL[:, :, qb * 128:(qb + 1) * 128], t_t)
            banks.give(b, r)
            t_ath.append(r)
            yield

        t_cv = []
        cv = {"a": None, "b": None, "c": None, "hi": None}

        def conv_tile(c):
            s = {}

            def ev_cc(ps, tok):
                s["cc"] = act.do(lambda e: e.activation(CA[:, :], ps[:, :], ACT.Identity, bias=par(PP_B + 10 + c)),
                                 tok, cv["a"], t_old)
                return [s["cc"]]

            def ev_cx(ps, tok):
                s["p"] = dve.do(lambda e: e.scalar_tensor_tensor(CB[:, :], ps[:, :], par(PP_B + 14 + c), CA[:, :],
                                                                 ALU.add, ALU.mult), tok, s["cc"], cv["b"])
                cv["a"] = s["p"]
                wc = PP_CW + 3 * c
                y2 = act.do(lambda e: e.activation(CC[:, :], CB[:, :], ACT.Identity, scale=par(wc + 2)), s["p"], cv["c"])
                y1 = dve.do(lambda e: e.scalar_tensor_tensor(CC[:, 1:S], CB[:, 0:S - 1], par(wc + 1), CC[:, 1:S],
                                                             ALU.mult, ALU.add), y2)
                s["y"] = dve.do(lambda e: e.scalar_tensor_tensor(CC[:, 2:S], CB[:, 0:S - 2], par(wc), CC[:, 2:S],
                                                                 ALU.mult, ALU.add), y1)
                return [s["p"]]

            def ev_cb(ps, tok):
                z = dve.do(lambda e: e.scalar_tensor_tensor(CB[:, :], ps[:, :], par(PP_B + 6 + c), CC[:, :],
                                                            ALU.add, ALU.mult), tok, s["y"])
                cv["c"] = z
                t_cv.append(split_out(CB[:, :], CVH[:, c, :], CVL[:, c, :], z, t_old))
                cv["b"] = t_cv[-1]
                return [z]

            i = SLOT_CONV + 3 * c
            return chain(fm(i, ev_cc), fm(i + 1, ev_cx), fm(i + 2, ev_cb))

        sides.add([lambda qb=qb, i=i: attn1(qb, i) for qb in range(4) for i in range(4)], DEPTHS[0])
        sides.run(chain(*[conv_tile(c) for c in range(4)]), SLACK[0])

        t_m = {}
        gaf = [None, None]

        def merge_tile(n):
            u = n % 2
            s = {}

            def ev_g(j):
                def f(ps, tok):
                    s[j] = act.do(lambda e: e.activation(GA[:, u, j, :], ps[:, :], ACT.Sigmoid,
                                                         bias=par(PP_B + 18 + 8 * j + n)), tok, gaf[u], t_old)
                    return [s[j]]
                return f

            def ev_br(j):
                def f(ps, tok):
                    s[2 + j] = dve.do(lambda e: e.tensor_tensor(GA[:, u, j, :], ps[:, :], GA[:, u, j, :], ALU.mult),
                                      tok, s[j])
                    return [s[2 + j]]
                return f

            i = SLOT_GATE + 3 * n
            yield from fm(i, ev_g(0))
            yield from fm(i + 1, ev_g(1))
            yield from until(lambda: len(t_ath) == 4)
            yield from fm(i + 2, ev_br(0), ATH, ATL, t_ath, 4, 0, last=False)
            yield from fm(i + 2, ev_br(1), CVH, CVL, t_cv, 4, 4)
            a = dve.do(lambda e: e.tensor_tensor(GA[:, u, 0, :], GA[:, u, 0, :], GA[:, u, 1, :], ALU.add), s[2], s[3])
            t_m[n] = split_out(GA[:, u, 0, :], MH[:, n, :], ML[:, n, :], a, t_old)
            gaf[u] = t_m[n]

        sides.run(chain(*[merge_tile(n) for n in range(8)]), SLACK[1])

        p1.close()
        pv = ExitStack()
        OH = sb("OH", [32, S], F, pv)
        RB = sb("RB", [32, 6], F, pv)
        RBB = sb("RBB", [32, 6, P], F, pv)
        VE = sb("VE", [P, 6, 1024], F, pv)
        p2 = ExitStack()
        XS2 = sb("XS2", [P, 4, D], F, p2)
        GR2 = sb("GR2", [P, D], F, p2)
        t_free = [t_used[SLOT_GATE + 23], [t_m[n] for n in range(8)]]
        t_gr = pool.dma(GR2[:, :], brow[4, :].partition_broadcast(P), s_misc[12], 16, t_free)
        t_h, t_xs2 = {}, {}
        n_half, n_rest = norm(8, 1e-5, XS2, t_gr, GR2)

        def ev_wout(c):
            def f(t, ps, tok):
                cs = slice(c * 512, c * 512 + 512)
                r = dve.do(lambda e: e.tensor_tensor(H[:, t, cs], ps[:, :], H[:, t, cs], ALU.add), tok, t_x[t],
                           t_xs)
                t_h[t] = [*t_h.get(t, []), r]
                q = n_half(t, c, ps[:, :], r)
                if c == 1:
                    if t > 1:
                        turn_x(t - 2)
                    t_xs2[t] = n_rest(t, t_free)
                return [r, q]
            return f

        act.quiet(lambda e: e.preload_act_table_set("sqrt_and_others"))

        xt = {}
        turn_x = turn_rows(XS2, t_xs2, t_used[SLOT_GATE + 23], xt)
        for c in range(2):
            drain(tm(SLOT_WOUT + 4 * c, 512, 8, ev_wout(c), MH, ML, t_m, tail=c == 1))
        t_pe_wout = t_used[SLOT_WOUT + 7]
        if dbg == 1:
            sp.dma(out.rearrange("(t p) d -> p t d", p=P), H[:, :, :], s_out, 16, [t_h[t] for t in range(4)])
            sp.wait((s_out, 16))

        if dbg is None or dbg > 1:
            t_xs = [t_xs2[t] for t in range(4)]
            sp.dma(OH[:, :], oneh, s_misc[2], 16, t_free)
            t_rb = sp.dma(RB[:, :], relb, s_misc[2], 32)
            t_ve = []

            def distances():
                t_rbb = dve.do(lambda e: e.tensor_copy(RBB[:, :, :], RB[:, :].rearrange("b (h o) -> b h o", o=1).to_broadcast([32, 6, P])), t_rb, t_free)
                t_ve.append(dve.do(lambda e: e.memset(VE[:, :, 512:1024], NEG), t_free, us=3.0))
                for h in range(6):
                    yield t_rbb
                    bk = yield from take(banks)
                    tk = pe.do(lambda e, h=h, bk=bk: e.matmul(bk.ap[:, :], RBB[:, h, :], OH[:, :], start=True, stop=True),
                               t_rbb, bk.free, us=0.85)
                    t_ve.append(act.do(lambda e, h=h, bk=bk: e.copy(VE[:, h, 0:512], bk.ap[:, :]), tk, t_free))
                    banks.give(bk, [t_ve[-1]])
                t_ve.append(sp.dma(vec_dram, VE[:, :, :], s_misc[6], 16, t_ve))

            p2.close()
            p2 = ExitStack()
            t_old = [t_pe_wout]
            GH = sb("GH", [P, 11, S], FR, p2)
            GL = sb("GL", [P, 11, S], FR, p2)
            UA = sb("UA", [P, 2, 2, S], F, p2)
            FN = sb("FN", [P, D], F, p2)
            t_fn = pool.dma(FN[:, :], brow[0, :].partition_broadcast(P), s_misc[0], 16, t_old)
            uf = [t_old, t_old]
            sides.add([distances], 1)
            LM, EX, LB, OML, LBF = (st[:, 32 + 3 * i:35 + 3 * i] for i in range(5))
            lbp = PPt[:, PP_LB:PP_LB + 3]
            t = dve.do(lambda e: e.tensor_tensor(LM, lbp, lbp, ALU.subtract), t_par)
            t = act.do(lambda e: e.activation(EX, LM, ACT.Exp), t)
            t = dve.do(lambda e: e.tensor_tensor(LB, EX, EX, ALU.subtract), t)
            t_lb = [dve.do(lambda e: e.tensor_scalar(OML, LB, -1.0, 1.0, ALU.mult, ALU.add), t),
                    dve.do(lambda e: e.tensor_scalar(LBF, LB, 1e-30, None, ALU.max), t)]
            g_free = [t_old]

            def up_tile(hf, j):
                f_ = hf * 11 + j
                u = f_ % 2
                s = {}

                def ev(g):
                    def f(ps, tok):
                        wc = PP_FW + 3 * (f_ + NF * g)
                        A = UA[:, u, g, :]
                        a = act.do(lambda e: e.activation(A, ps[:, :], ACT.Identity, scale=par(wc + 2)), tok, uf[u])
                        b = dve.do(lambda e: e.scalar_tensor_tensor(A[:, 1:S], ps[:, 0:S - 1], par(wc + 1), A[:, 1:S],
                                                                    ALU.mult, ALU.add), a)
                        c = dve.do(lambda e: e.scalar_tensor_tensor(A[:, 2:S], ps[:, 0:S - 2], par(wc), A[:, 2:S],
                                                                    ALU.mult, ALU.add), b)
                        s[g] = c
                        if g == 0:
                            s[0] = act.do(lambda e: e.activation(A, A, ACT.Silu), c)
                        return [c]
                    return f

                i = SLOT_FFN + hf * N_HALF + 2 * j
                if f_ == 0:
                    first_two(i, (ev(0), ev(1)), turn_x, xt)
                else:
                    yield from fm(i, ev(0))
                    yield from fm(i + 1, ev(1))
                m = dve.do(lambda e: e.tensor_tensor(UA[:, u, 0, :], UA[:, u, 0, :], UA[:, u, 1, :], ALU.mult),
                           s[0], s[1])
                t_g[j] = split_out(UA[:, u, 0, :], GH[:, j, :], GL[:, j, :], m, g_free[0])
                uf[u] = t_g[j]

            for hf in range(2):
                t_g = {}
                sides.run(chain(*[up_tile(hf, j) for j in range(11)]), SLACK[2])
                t_h2, t_x2s = {}, {}
                if hf == 1:
                    act.quiet(lambda e: e.preload_act_table_set("sqrt_and_others"))
                    n_half, n_rest = norm(16, 1e-5, H, t_fn, FN)

                def ev_down(c):
                    def f(t, ps, tok):
                        cs = slice(c * 512, c * 512 + 512)
                        r = dve.do(lambda e: e.tensor_tensor(H[:, t, cs], ps[:, :], H[:, t, cs], ALU.add), tok, t_xs,
                                   t_h[t])
                        t_h2[t] = [*t_h2.get(t, []), r]
                        if hf == 0:
                            return [r]
                        q = n_half(t, c, ps[:, :], r)
                        if c == 1:
                            if t > 1:
                                turn_x(t - 2)
                            t_x2s[t] = n_rest(t)
                        return [r, q]
                    return f

                if hf == 1:
                    xt = {}
                    turn_x = turn_rows(H, t_x2s, t_used[SLOT_FFN + N_HALF + 21], xt)
                for c in range(2):
                    drain(tm(SLOT_FFN + hf * N_HALF + 22 + 6 * c, 512, 11, ev_down(c), GH, GL, t_g,
                             tail=hf + c == 2))
                t_h = t_h2
                g_free[0] = t_used[SLOT_FFN + hf * N_HALF + 33]
            t_v = t_ve[-1]
            t_old = [g_free[0], [t_g[j] for j in range(11)], t_ve]
            p2.close()
            pv.close()
        if dbg == 2:
            sp.dma(out.rearrange("(t p) d -> p t d", p=P), H[:, :, :], s_out, 16, [t_h[t] for t in range(4)])
            sp.wait((s_out, 16))

        if dbg is None or dbg > 2:
            p3 = ExitStack()
            act.wait(t_old)
            dve.wait(t_old)
            A = sb("A", [P, 28248], F, p3)
            sm2 = sb("sm2", [P, 320], F, p3)

            def region(at, *shape, parts=P):
                v = A[0:parts, at:at + int(np.prod(shape))]
                if len(shape) > 1:
                    names = "abcd"[:len(shape)]
                    v = v.rearrange(f"p ({' '.join(names)}) -> p {' '.join(names)}",
                                    **dict(zip(names[1:], shape[1:])))
                return v

            HI = region(0, 4, 402)
            AV = region(1608, 4, S)
            NK = region(3656, 2, S)
            NQ = region(4680, 3, S)
            M = region(6216, 6, 512)
            MC = region(9288, 6, 4, 31)
            KCT = region(10032, 31)
            VC = region(10063, 2, 64, parts=31)
            SRC = region(10200, 2, S)
            BLK = region(11224, 16, 2, 31)
            W1 = region(12216, 2048)
            W2 = region(14264, P)
            PO = region(14392, 16)
            HC = region(14424, 2, 62)
            ME = region(14560, 6, 384)
            DEP = DEPTHS[1]
            SC2 = region(10200, DEP, S)
            PT2 = SC2
            OT = region(14296, 2, 384)
            SQ = region(15064, 2, S)
            SK = region(16088, 2, S)
            G0 = 17112
            HG = region(G0, 3, 3, S)
            G1 = G0 + 4608
            T1 = region(G1, 2, S)
            SRX = region(G1 + 1024, S)
            KL = region(G1 + 1536, 2, S)
            Q1 = region(G1 + 2560, S)
            K1 = region(G1 + 3072, S)
            K2 = region(G1 + 3584, 3, 128)
            TA = region(G1 + 3968, 2, 1280)
            SZT = region(G0, 8, S)
            SPb = region(G1, 1280)
            AA = region(G1 + 1280, 1280)
            EE = region(G1 + 2560, 2, S)
            MX = region(G1 + 3584, 2, S)
            Y = region(3656, 4, D)
            LN = region(3656 + 4096, 2, D)
            O = H
            QU = [H[:, 2 * u:2 * u + 2, 384:640] for u in range(2)]

            t_xs = [t_x2s[t] for t in range(4)]
            t_x2 = pool.dma(x2_dram.rearrange("(t p) d -> p t d", p=P), H[:, :, :], s_misc[8], 16, t_xs)

            RS = sm2[:, 16:40]
            DEX = sm2[:, 40:52]
            NMn = sm2[:, 64:136]
            Ln_ = sm2[:, 136:208]
            CF = sm2[:, 208:280]
            t_kl0 = [pool.do(lambda e: e.memset(KL, 0.0), t_old, t_xs)]
            ones = TA[:, 0, 0:128]
            t_one = pool.do(lambda e: e.memset(ones, 1.0), t_old, t_xs)

            base = SLOT_B2
            t_hb, t_hk, t_hq, t_hv, t_g, t_sq, t_sk, t_av = {}, {}, {}, [], [], {}, {}, []
            t_src, t_nk, t_nq, t_sz = {}, {}, {}, {}
            t1f = [None, None]
            LNEXP = "natural_log_exp_and_others"

            def ev_f(i):
                def f(ps, tok):
                    u = i % 2
                    hk, hb = HG[:, i, 1, :], HG[:, i, 2, :]
                    a = act.do(lambda e: e.activation(T1[:, u, :], ps[:, :], ACT.Sigmoid), tok, t1f[u])
                    b = act.do(lambda e: e.activation(hk, ps[:, :], ACT.Sigmoid, scale=-1.0), tok)
                    t_hk[i] = dve.do(lambda e: e.tensor_scalar(hk, hk, OML[:, i:i + 1], None, ALU.mult), b, t_lb)
                    c = act.do(lambda e: e.activation(T1[:, u, :], T1[:, u, :], ACT.Ln, bias=LBF[:, i:i + 1],
                                                      scale=OML[:, i:i + 1]), a, t_lb)
                    r = []
                    for q in range(4):
                        cs = slice(q * 128, q * 128 + 128)
                        r.append(dve.do(lambda e, cs=cs: e.tensor_tensor_scan(
                            hb[:, cs], ones, T1[:, u, cs], 0.0, ALU.mult, ALU.add), c, t_one))
                    t1f[u] = t_hb[i] = r
                    return [a, b]
                return f

            def ev_copy(dst, store, key, scale=None, after=()):
                def f(ps, tok):
                    if scale is None:
                        store[key] = act.do(lambda e: e.copy(dst, ps[:, :]), tok, *after)
                    else:
                        store[key] = act.do(lambda e: e.mul(dst, ps[:, :], scale), tok, *after)
                    return [store[key]]
                return f

            def ev_b(t, ps, tok):
                r = act.do(lambda e: e.copy(HI[:, t, :], ps[:, 0:402]), tok)
                t_hv.append(r)
                if t == 3:
                    t_g.append(act.do(lambda e: e.activation(HI[:, :, 384:402], HI[:, :, 384:402], ACT.Sigmoid), t_hv))
                return [r]

            def ev_a(t, ps, tok):
                t_av.append(act.do(lambda e: e.copy(AV[:, t, :], ps[:, :]), tok))
                return [t_av[-1]]

            PAIRS = [(0, 1), (1, 2), (2, 3), (0, 2), (1, 3), (0, 3)]
            t_ohg = {}
            hg = {"ta": None, "t": [None, None], "q1": None, "qu": [None, None], "dex": None}
            c4 = lambda ap: ap.rearrange("p (c t) -> p c t", c=4)

            def hgrn(p):
                q, kk_, b = HG[:, p, 0, :], HG[:, p, 1, :], HG[:, p, 2, :]
                tot = c4(b)[:, :, 127:128]
                taf = hg["ta"]
                d = dve.do(lambda e: e.tensor_tensor(c4(T1[:, 0, :]), tot.to_broadcast([P, 4, 128]), c4(b), ALU.subtract),
                           t_hb[p], hg["t"][0])
                x1 = act.do(lambda e: e.activation(T1[:, 1, :], b, ACT.Exp), t_hb[p], hg["t"][1])
                x0 = act.do(lambda e: e.activation(T1[:, 0, :], T1[:, 0, :], ACT.Exp), d)
                s0 = dve.do(lambda e: e.tensor_tensor(DEX[:, 2:3], b[:, 255:256], b[:, 383:384], ALU.add), t_hb[p], hg["dex"])
                s1 = dve.do(lambda e: e.tensor_copy(DEX[:, 0:2], c4(b)[:, 1:3, 127]), t_hb[p], hg["dex"])
                s2 = act.do(lambda e: e.activation(DEX[:, 4:7], DEX[:, 0:3], ACT.Exp), s0, s1)
                t_ta = [None, None]
                yield [t_hk[p], t_hq[p]]
                for j in range(2):
                    r = slice(64 * j, 64 * j + 64)
                    bk = yield from take(banks)
                    pe.wait(bk.free, t_hk[p], t_hq[p])
                    for c in range(4):
                        cs = slice(c * 128, c * 128 + 128)
                        tk = pe.do(lambda e, r=r, cs=cs, bk=bk: e.matmul(bk.ap[:, cs], kk_[r, cs], q[r, cs],
                                                                         start=True, stop=True))
                    t_ta[j] = dve.do(lambda e, j=j, bk=bk: e.tensor_tensor(
                        c4(TA[:, j, 0:512]), c4(bk.ap[:, :]),
                        ID.rearrange("p (o t) -> p o t", o=1).to_broadcast([P, 4, 128]), ALU.mult), tk, taf, t_hb)
                    banks.give(bk, [t_ta[j]])
                q1 = dve.do(lambda e: e.tensor_tensor(Q1, q, T1[:, 1, :], ALU.mult), x1, t_hq[p], hg["q1"])
                k1 = dve.do(lambda e: e.tensor_tensor(K1, kk_, T1[:, 0, :], ALU.mult), x0, t_hk[p], hg["q1"])
                hg["t"] = [k1, q1]
                k2 = []
                for m, (blk, col) in enumerate(((0, 4), (1, 5), (0, 6))):
                    k2.append(dve.do(lambda e, m=m, blk=blk, col=col: e.tensor_scalar(
                        K2[:, m, :], K1[:, blk * 128:blk * 128 + 128], DEX[:, col:col + 1], None, ALU.mult), k1, s2, hg["q1"]))
                hg["dex"] = k2
                t_off = []

                def off(half):
                    for j in range(2):
                        r = slice(64 * j, 64 * j + 64)
                        bk = yield from take(banks)
                        pe.wait(bk.free, q1, k1, k2)
                        for m in range(3):
                            ci, cj = PAIRS[3 * half + m]
                            ks = K1[r, ci * 128:ci * 128 + 128] if half == 0 else K2[r, m, :]
                            hg["q1"] = pe.do(lambda e, m=m, ks=ks, r=r, cj=cj, bk=bk: e.matmul(
                                bk.ap[:, m * 128:m * 128 + 128], ks, Q1[r, cj * 128:cj * 128 + 128], start=True, stop=True))
                        a = act.do(lambda e, j=j, bk=bk: e.copy(
                            TA[:, j, 512 + 384 * half:896 + 384 * half], bk.ap[:, 0:384]), hg["q1"], taf, t_hb)
                        banks.give(bk, [a])
                        t_off.append(a)

                v = lambda ap, l: ap.rearrange("p (n h l) -> p n h l", h=2, l=l)
                tv = lambda u, l: T1[:, u, :].rearrange("p (h n l) -> p h n l", h=2, l=l)

                def prep(n):
                    l, u = LEVELS[n], n % 2
                    bv, o_ = v(b, l), tv(u, l)
                    mid = bv[:, :, 0, l - 1:l].to_broadcast([P, S // (2 * l), l])
                    d0 = dve.do(lambda e: e.tensor_tensor(o_[:, 0], bv[:, :, 1, :], mid, ALU.subtract), t_hb[p], hg["t"][u])
                    d1 = dve.do(lambda e: e.tensor_tensor(o_[:, 1], mid, bv[:, :, 0, :], ALU.subtract), t_hb[p], hg["t"][u])
                    return act.do(lambda e: e.activation(T1[:, u, :], T1[:, u, :], ACT.Exp), d0, d1)

                def mult(n, x):
                    l, u = LEVELS[n], n % 2
                    kv, qs, ks, t_ = v(KL[:, u, :], l), v(q, l), v(kk_, l), tv(u, l)
                    m0 = [dve.do(lambda e, r=slice(64 * j, 64 * j + 64), j=j: e.tensor_tensor(
                        QU[u][r, j].rearrange("p (n l) -> p n l", l=l), qs[r, :, 1, :], t_[r, 0], ALU.mult),
                        x, hg["qu"][u], t_kl0) for j in range(2)]
                    m1 = dve.do(lambda e: e.tensor_tensor(kv[:, :, 0, :], ks[:, :, 0, :], t_[:, 1], ALU.mult),
                                x, hg["qu"][u], t_kl0)
                    hg["t"][u] = [m0, m1]
                    return [m0, m1]

                def prod(n, m):
                    l, u = LEVELS[n], n % 2
                    bk = yield from take(banks)
                    pe.wait(bk.free, m)
                    bj = bk.ap[:, :].rearrange("p (j q) -> p j q", j=2)
                    for c in range(4):
                        tk = pe.do(lambda e, c=c: e.matmul(
                            bj[:, :, c * 64:c * 64 + 64], KL[:, u, c * 128:c * 128 + 128],
                            QU[u][:, :, c * 64:c * 64 + 64], start=True, stop=True), us=0.22)
                    for j in range(2):
                        o_ = TA[:, j, 0:512].rearrange("p (n h l) -> p n h l", h=2, l=l)[:, :, 1, :]
                        msk = C[:, C_LEV + 256 * n:C_LEV + 256 * n + 256].bitcast(U32).rearrange("p (n l) -> p n l", l=l)
                        dat = bj[:, j, :].rearrange("p (n l) -> p n l", l=l)
                        t_ta[j] = dve.do(lambda e, o_=o_, msk=msk, dat=dat: e.copy_predicated(o_, msk, dat), tk, t_ta[j])
                    banks.give(bk, list(t_ta))
                    hg["qu"][u] = tk

                xs, ms = {}, {}
                xs[0] = prep(0)
                yield [q1, k1, k2]
                yield from off(0)
                xs[1] = prep(1)
                ms[0] = mult(0, xs[0])
                yield from off(1)
                for n in range(len(LEVELS)):
                    if n + 2 < len(LEVELS):
                        xs[n + 2] = prep(n + 2)
                    if n + 1 < len(LEVELS):
                        ms[n + 1] = mult(n + 1, xs[n + 1])
                    yield ms[n]
                    yield from prod(n, ms[n])
                yield [t_ta, t_off]
                bk = yield from take(banks)
                pe.wait(bk.free, t_ta, t_off, t_hv)
                for j in range(2):
                    h = 2 * p + j
                    for cj in range(4):
                        src = [(cj, cj * 128)] + [(ci, 512 + 128 * m) for m, (ci, c2_) in enumerate(PAIRS) if c2_ == cj]
                        for z, (ci, col) in enumerate(src):
                            tk = pe.do(lambda e, j=j, h=h, cj=cj, ci=ci, col=col, z=z, n_=len(src): e.matmul(
                                bk.ap[:, (cj * 2 + j) * 64:(cj * 2 + j) * 64 + 64], TA[:, j, col:col + 128],
                                HI[:, ci, h * 64:h * 64 + 64], start=(z == 0), stop=(z == n_ - 1)))
                hg["ta"] = tk
                ov = O[:, :, 640 + 128 * p:768 + 128 * p]
                a = act.do(lambda e: e.copy(ov, bk.ap[:, :].rearrange("p (t c) -> p t c", t=4)), tk, t_x2, t_turned)
                s = act.do(lambda e: e.activation(T1[:, 0, :], bk.ap[:, :], ACT.Square), tk, hg["t"][0])
                rs = dve.do(lambda e: e.tensor_reduce(
                    RS[:, 8 * p:8 * p + 8], T1[:, 0, :].rearrange("p (g d) -> p g d", d=64), AX.X, ALU.add), s)
                hg["t"][0] = rs
                banks.give(bk, [a, s])
                t_ohg[p] = [a, rs]
                yield

            t_hgo = []

            def hgrn_norm():
                r = dve.do(lambda e: e.tensor_scalar(RS, RS, 1.0 / 64, 1e-6, ALU.mult, ALU.add), list(t_ohg.values()))
                r = act.do(lambda e: e.activation(RS, RS, ACT.Sqrt), r)
                act.quiet(lambda e: e.preload_act_table_set(LNEXP), us=1.3)
                r = dve.do(lambda e: e.reciprocal(RS, RS), r)
                done = []
                for p in range(3):
                    for t in range(4):
                        ov = O[:, t, 640 + 128 * p:768 + 128 * p].rearrange("p (j d) -> p j d", d=64)
                        sc = RS[:, 8 * p + 2 * t:8 * p + 2 * t + 2].rearrange("p (j o) -> p j o", o=1).to_broadcast([P, 2, 64])
                        done.append(dve.do(lambda e, ov=ov, sc=sc: e.tensor_tensor(ov, ov, sc, ALU.mult), r))
                    yield
                t_hgo.extend(done)

            STR = C[:, C_STRICT:C_STRICT + 128]
            OFF = [0, 512, 896, 1152]
            sf = {"sp": None, "aa": None, "ee": [None, None], "n": 0, "o": None}
            t_osb = []

            def stick(h):
                yield from until(lambda: h // 2 in t_sk and len(t_av) == 4)
                u = h % 2
                r = slice(64 * u, 64 * u + 64)
                t_spk, t_a, t_cs, zbs = {}, {}, [], {}
                kc = lambda T, kb, c0: T[:, OFF[kb] + c0 - 128 * kb:OFF[kb] + S - 128 * kb]

                def first(kb):
                    c0 = kb * 128
                    cs = slice(c0, S)
                    zb = yield from take(banks)
                    zbs[kb] = zb
                    w = sf["n"] % 2
                    sf["n"] += 1
                    tz = pe.do(lambda e: e.matmul(zb.ap[:, cs], SK[r, h // 2, c0:c0 + 128], SQ[r, h // 2, cs],
                                                  start=True, stop=False, skip_group_check=True),
                               zb.free, t_sq[h // 2], t_sk[h // 2])
                    ee = EE[:, w, cs]
                    a = act.do(lambda e: e.activation(ee, zb.ap[:, cs], ACT.Abs), tz, sf["ee"][w], t_hgdone)
                    b = act.do(lambda e: e.activation(ee, ee, ACT.Exp, scale=-1.0), a)
                    c = act.do(lambda e: e.activation(ee, ee, ACT.Ln, bias=1.0), b)
                    sp_ = kc(SPb, kb, c0)
                    d = dve.do(lambda e: e.scalar_tensor_tensor(sp_, zb.ap[:, cs], 0.0, ee, ALU.max, ALU.add),
                               c, sf["sp"], t_hgdone)
                    sf["ee"][w] = d
                    dg = SPb[:, OFF[kb]:OFF[kb] + 128]
                    t_spk[kb] = [d, dve.do(lambda e: e.tensor_tensor(dg, dg, STR, ALU.mult), d)]

                def second(kb):
                    c0 = kb * 128
                    cs = slice(c0, S)
                    zb = zbs[kb]
                    pe.wait(t_spk[kb])
                    sp_, aa = kc(SPb, kb, c0), kc(AA, kb, c0)
                    t_c = pe.do(lambda e: e.matmul(zb.ap[:, cs], C[:, C_NTRI:C_NTRI + 128], sp_,
                                                   start=False, stop=(kb == 3), skip_group_check=True))
                    for k2 in range(kb + 1, 4):
                        c2 = slice(k2 * 128, S)
                        t_c = pe.do(lambda e, k2=k2, c2=c2: e.matmul(zb.ap[:, c2], C[:, C_ONE:C_ONE + 128],
                                                                     kc(SPb, k2, k2 * 128), start=False, stop=(k2 == 3),
                                                                     skip_group_check=True))
                    t_cs.append(t_c)
                    a = act.do(lambda e: e.activation(aa, zb.ap[:, cs], ACT.Exp), t_c, sf["aa"])
                    banks.give(zb, [a])
                    dg = AA[:, OFF[kb]:OFF[kb] + 128]
                    t_a[kb] = [a, dve.do(lambda e: e.tensor_tensor(dg, dg, STR, ALU.mult), a)]

                for kb in (3, 2, 1, 0):
                    yield from first(kb)
                    if kb < 3:
                        yield t_spk[kb + 1]
                        second(kb + 1)
                yield t_spk[0]
                second(0)
                sf["sp"] = t_cs
                yield t_a
                if u == 0:
                    sf["o"] = yield from take(banks)
                    pe.wait(sf["o"].free)
                ob = sf["o"]
                pe.wait(t_av)
                for qb in range(4):
                    for kb in range(qb + 1):
                        pe.wait(t_a[kb])
                        at = OFF[kb] + 128 * (qb - kb)
                        tk = pe.do(lambda e, qb=qb, kb=kb, at=at: e.matmul(
                            ob.ap[:, (qb * 2 + u) * 64:(qb * 2 + u) * 64 + 64], AA[:, at:at + 128],
                            AV[:, kb, 256 + h * 64:320 + h * 64], start=(kb == 0), stop=(kb == qb)))
                sf["aa"] = tk
                if u == 1:
                    c = 384 + 64 * (h - 1)
                    t_osb.append(act.do(lambda e: e.copy(O[:, :, c:c + 128], ob.ap[:, :].rearrange("p (t c) -> p t c", t=4)),
                                        tk, t_x2, t_turned, t_hgdone))
                    banks.give(ob, [t_osb[-1]])
                yield

            t_cmp, t_mc = [], []

            def compress():
                w1t = t_w1
                t_hc, done, t_blk = [], None, None
                for s in range(2):
                    yield from until(lambda: s in t_src)
                    pool.dma(SRX[0:64, :], SRC[64:128, s, :], s_misc[5], 32 * s + 16, t_src[s], t_xs, t_blk)
                    t_x = pool.dma(SRX[64:128, :], SRC[0:64, s, :], s_misc[5], 32 * s + 32)
                    t_blk = []
                    for j in range(2):
                        rr = slice(64 * j, 64 * j + 64)
                        for g in range(2):
                            src = SRC[rr, s, :] if g == j else SRX[rr, :]
                            for a in range(2):
                                sv = src.rearrange("p (m b k) -> p b k m", b=8, k=2)[:, :, j, a:a + 31]
                                pv_ = PO[rr, 8 * a:8 * a + 8].rearrange("p (b o) -> p b o", o=1).to_broadcast([64, 8, 31])
                                t_blk.append(dve.do(lambda e, rr=rr, g=g, a=a, sv=sv, pv_=pv_: e.tensor_tensor(
                                    BLK[rr, 8 * a:8 * a + 8, g, :], sv, pv_, ALU.add), t_src[s], t_x, t_po, done, us=0.35))
                    yield [t_blk, w1t]
                    bk = yield from take(banks)
                    pe.wait(bk.free, t_blk, w1t)
                    for l in range(16):
                        tk = pe.do(lambda e, l=l, bk=bk: e.matmul(
                            bk.ap[:, 0:62], W1[:, l * 128:l * 128 + 128], BLK[:, l, :, :].rearrange("p g n -> p (g n)"),
                            start=(l == 0), stop=(l == 15)), us=0.22)
                        if l % 4 == 3:
                            yield
                    if s == 0:
                        w1t = pool.dma(W1, w1c[1, :, :], s_misc[4], 32, tk, us=6.0)
                    t_hc.append(act.do(lambda e, s=s, bk=bk: e.activation(
                        HC[:, s, :], bk.ap[:, 0:62], ACT.Gelu_apprx_tanh), tk))
                    banks.give(bk, [t_hc[-1]])
                    act.quiet(lambda e: e.preload_act_table_set(LNEXP), us=1.3)
                    done = tk
                yield t_hc
                bk = yield from take(banks)
                pe.wait(bk.free, t_hc)
                for g in range(2):
                    tk = pe.do(lambda e, g=g: e.matmul(bk.ap[64 * g:64 * g + 64, 0:31], W2[:, 0:64], HC[:, 0, 31 * g:31 * g + 31],
                                                       start=True, stop=True))
                a = act.do(lambda e: e.copy(KCT, bk.ap[:, 0:31]), tk)
                banks.give(bk, [a])
                b2 = yield from take(banks)
                pe.wait(b2.free)
                for g in range(2):
                    tk = pe.do(lambda e, g=g: e.matmul(b2.ap[0:31, 64 * g:64 * g + 64], HC[:, 1, 31 * g:31 * g + 31], W2[:, 64:128],
                                                       start=True, stop=True))
                b = act.do(lambda e: e.copy(VC, b2.ap[0:31, 0:128].rearrange("p (g d) -> p g d", g=2)), tk)
                banks.give(b2, [b])
                for qb in range(4):
                    u0 = 415 - 128 * qb
                    n0 = min(31, (512 - u0 + 15) // 16)
                    if n0:
                        mc, ms_ = MC[:, :, qb, 0:n0], M[:, :, u0:u0 + 16 * n0 - 15:16]
                        t_mc.append(dve.do(lambda e, mc=mc, ms_=ms_: e.tensor_copy(mc, ms_), t_M))
                    if n0 < 31:
                        u1 = u0 + 16 * n0 - 512
                        mc, ms_ = MC[:, :, qb, n0:31], ME[:, :, u1:u1 + 16 * (31 - n0) - 15:16]
                        t_mc.append(dve.do(lambda e, mc=mc, ms_=ms_: e.tensor_copy(mc, ms_), t_M))
                t_cmp.extend([a, b])
                yield

            idx = lambda br, qb, h: (br * 4 + qb) * 6 + h
            fr = {"pt": [None] * DEP, "n": 0, "ot": [None, None], "o": None, "seq": []}
            t_ex, t_onsa, nsa_done = {}, {}, []

            def inst(qb, br, h):
                u = fr["n"] % DEP
                fr["n"] += 1
                g, i = h // 3, h % 3
                r = slice(64 * g, 64 * g + 64)
                if br == 0:
                    w, kT, tks = 31, KCT[r, :], t_cmp
                    bias = MC[:, h, qb, :]
                else:
                    w, kT, tks = 128 * qb + 128, NK[r, br - 1, 0:128 * qb + 128], t_nk[br - 1]
                    bias = M[:, h, 384 - 128 * qb:512]
                n = idx(br, qb, h)
                sbk = yield from take(banks)
                ts = pe.do(lambda e: e.matmul(sbk.ap[:, 0:w], NQ[r, i, qb * 128:qb * 128 + 128], kT, start=True, stop=True),
                           sbk.free, t_nq[i], tks)
                sc = SC2[:, u, 0:w]
                tt = dve.do(lambda e: e.tensor_tensor_reduce(sc, sbk.ap[:, 0:w], bias, -0.125, BIG,
                                                             ALU.add, ALU.min, NMn[:, n:n + 1]),
                            ts, t_M, t_mc, fr["pt"][u], t_cmp)
                banks.give(sbk, [tt])
                ex = act.do(lambda e: e.activation(sc, sc, ACT.Exp, bias=NMn[:, n:n + 1], scale=-1.0,
                                                   accum_out=Ln_[:, n:n + 1]), tt)
                t_ex[br, qb, h] = ex
                yield ex
                nb = max(w // 128, 1)
                tbk = yield from take(banks)
                pe.wait(tbk.free, ex)
                if br == 0:
                    tp = pe.do(lambda e: e.transpose(tbk.ap[0:31, 0:128], SC2[:, u, 0:31], ID))
                    cp = dve.do(lambda e: e.tensor_copy(PT2[0:31, u, 0:128], tbk.ap[0:31, 0:128]), tp)
                else:
                    for c in range(nb):
                        tp = pe.do(lambda e, c=c: e.transpose(tbk.ap[:, c * 128:c * 128 + 128], SC2[:, u, c * 128:c * 128 + 128], ID))
                    if h % 2:
                        cp = dve.do(lambda e: e.tensor_copy(PT2[:, u, 0:w], tbk.ap[:, 0:w]), tp)
                    else:
                        cp = act.do(lambda e: e.copy(PT2[:, u, 0:w], tbk.ap[:, 0:w]), tp)
                banks.give(tbk, [cp])
                yield cp
                yield from until(lambda: len(fr["seq"]) == (qb * 3 + br) * 6 + h)
                if h == 0:
                    fr["o"] = yield from take(banks)
                    pe.wait(fr["o"].free)
                ob = fr["o"]
                pe.wait(cp, t_av)
                for c in range(nb):
                    if br == 0:
                        f = lambda e: e.matmul(ob.ap[:, h * 64:h * 64 + 64], PT2[0:31, u, 0:128], VC[:, g, :], start=True, stop=True)
                    else:
                        vs = AV[:, c, 128 * (br - 1) + 64 * g:128 * (br - 1) + 64 * g + 64]
                        f = lambda e, c=c, vs=vs: e.matmul(ob.ap[:, h * 64:h * 64 + 64], PT2[:, u, c * 128:c * 128 + 128], vs,
                                                           start=(c == 0), stop=(c == nb - 1))
                    tk = pe.do(f)
                fr["pt"][u] = tk
                fr["seq"].append((qb, br, h))
                assert fr["seq"] == sorted(fr["seq"])
                if h < 5:
                    return
                m = idx(br, qb, 0)
                cf = CF[:, m:m + 6]
                a = dve.do(lambda e: e.reciprocal(cf, Ln_[:, m:m + 6]), [t_ex[br, qb, k] for k in range(6)])
                gt = HI[:, qb, 384 + br:402:3]
                a = dve.do(lambda e: e.tensor_tensor(cf, cf, gt, ALU.mult), a, t_g)
                if br == 0 and qb == 0:
                    a = dve.do(lambda e: e.tensor_scalar(cf, cf, C[:, C_ROW:C_ROW + 1], None, ALU.mult), a)
                o3 = ob.ap[:, 0:384].rearrange("p (h d) -> p h d", d=64)
                cb = cf.rearrange("p (h o) -> p h o", o=1).to_broadcast([P, 6, 64])
                ov = O[:, qb, 0:384]
                if br == 0:
                    t_onsa[qb] = dve.do(lambda e: e.tensor_tensor(ov.rearrange("p (h d) -> p h d", d=64), o3, cb, ALU.mult),
                                        a, tk, t_x2, t_turned)
                    banks.give(ob, [t_onsa[qb]])
                else:
                    w_ = br % 2
                    b = dve.do(lambda e: e.tensor_tensor(OT[:, w_, :].rearrange("p (h d) -> p h d", d=64), o3, cb, ALU.mult),
                               a, tk, fr["ot"][w_], t_mc)
                    banks.give(ob, [b])
                    t_onsa[qb] = fr["ot"][w_] = dve.do(lambda e: e.tensor_tensor(ov, ov, OT[:, w_, :], ALU.add), b, t_onsa[qb])
                if br == 2:
                    nsa_done.append(tk)

            t_zc = []

            def ev_z(n):
                def f(ps, tok):
                    z = SZT[:, n, :]
                    a = act.do(lambda e: e.copy(z, ps[:, :]), tok, t_ohg[n // 3])
                    t_zc.append(a)
                    if n % 4 == 3:
                        z4 = SZT[:, n - 3:n + 1, :]
                        b = act.do(lambda e: e.activation(z4, z4, ACT.Silu), t_zc, us=3.4)
                        act.quiet(lambda e: e.preload_act_table_set(LNEXP), us=1.3)
                        for m in range(n - 3, n + 1):
                            t_sz[m] = b
                            if m >= 5:
                                t_sz[m] = dve.do(lambda e, m=m: e.tensor_scalar(
                                    SZT[:, m, :], SZT[:, m, :], par(PP_HG + m - 5), None, ALU.mult), b)
                    return [a]
                return f

            t_mt = [[] for _ in range(4)]
            mxf = [None, None]

            def turn(qb, half):
                yield from until(lambda: len(nsa_done) > qb and len(t_osb) == 2 and t_hgo and main_done)
                bk = yield from take(banks)
                pe.wait(bk.free, t_onsa[qb], t_osb, t_hgo)
                for k in range(4):
                    kt = 4 * half + k
                    tk = pe.do(lambda e, k=k, kt=kt: e.transpose(bk.ap[:, k * 128:k * 128 + 128], O[:, qb, kt * 128:kt * 128 + 128], ID))
                cs = slice(qb * 128, qb * 128 + 128)
                mx = MX[:, half, :].rearrange("p (k t) -> p k t", k=4)
                m = dve.do(lambda e: e.tensor_tensor(mx, bk.ap[:, :].rearrange("p (k t) -> p k t", k=4),
                                                     SZT[:, 4 * half:4 * half + 4, cs], ALU.mult),
                           tk, list(t_sz.values()), mxf[half], t_hgdone)
                banks.give(bk, [m])
                yield
                r = split_out(mx, XH[:, 4 * half:4 * half + 4, cs], XL[:, 4 * half:4 * half + 4, cs], m, t_zmain)
                mxf[half] = r
                t_mt[qb] += r
                yield

            pool.dma(W2, w2c, s_misc[3], 16, t_old, t_xs)
            t_po = pool.dma(PO, posT, s_misc[3], 32)
            t_w1 = pool.dma(W1, w1c[0, :, :], s_misc[4], 16)
            row = lambda off_: vec_dram.offset + off_
            pool.dma(M, bass.AP(tensor=vec_dram.tensor, offset=row(127), ap=[[6 * 1024 - 1, P], [1024, 6], [1, 512]]),
                     s_misc[7], 16, t_v)
            t_M = pool.dma(ME, bass.AP(tensor=vec_dram.tensor, offset=row(127 + 512), ap=[[6 * 1024 - 1, P], [1024, 6], [1, 384]]),
                           s_misc[7], 32)
            t_hgdone, main_done, t_zmain = [], [], []

            first_two(base + B2_HGF, (ev_f(0), ev_f(1)), turn_x, xt)
            t_turned = [xt[k] for k in range(8)]
            t_kl0.append(dve.do(lambda e: e.memset(H[:, :, 384:640], 0.0), t_x2, t_turned))
            drain(chain(fm(base + B2_HGF + 2, ev_f(2)),
                        *[fm(base + B2_HGQ + i, ev_copy(HG[:, i, 0, :], t_hq, i)) for i in range(3)],
                        tm(base + B2_HGI, 402, 8, ev_b)))
            hg["t"] = [t1f[0], t1f[1]]
            act.quiet(lambda e: e.preload_act_table_set(LNEXP), us=1.3)

            def hg_end():
                yield from hgrn_norm()
                t_hgdone.extend([hg["ta"], hg["t"], hg["qu"], hg["dex"], hg["q1"]])

            sides.add([lambda p=p: hgrn(p) for p in range(3)] + [hg_end] + [lambda h=h: stick(h) for h in range(4)], 1)
            sides.add([compress], 1)
            sides.run(chain(*[fm(base + B2_C + i, ev_copy(SRC[:, i, :], t_src, i)) for i in range(2)],
                            *[fm(base + B2_K + i, ev_copy(NK[:, i, :], t_nk, i)) for i in range(2)],
                            *[fm(base + B2_Q + i, ev_copy(NQ[:, i, :], t_nq, i)) for i in range(3)],
                            tm(base + B2_V, 512, 8, ev_a),
                            until(lambda: len(t_cmp) > 0)), SLACK[3])
            sides.add([lambda a=(qb, br, h): inst(*a) for qb in range(4) for br in range(3) for h in range(6)], DEP)
            sides.add([lambda a=(qb, h): turn(*a) for qb in range(4) for h in range(2)], 2)

            def z_tile(n):
                yield from until(lambda: n // 3 in t_ohg)
                yield from fm(base + B2_Z + n, ev_z(n))

            sides.run(chain(*[fm(base + B2_SQ + i, ev_copy(SQ[:, i, :], t_sq, i, 0.125, [t_mc])) for i in range(2)],
                            *[fm(base + B2_SK + i, ev_copy(SK[:, i, :], t_sk, i, None, [t_mc])) for i in range(2)],
                            *[z_tile(n) for n in range(8)]), SLACK[4])
            main_done.append(True)
            t_zmain.append(t_used[base + B2_Z + 7])
            t_Y, t_ln, t_eps = [], [], []

            def mixed(t):
                if len(t_mt[t]) < 4:
                    return None
                if t == 3 and not t_Y:
                    t_end = [nsa_done, t_onsa[3], t_mt, fr["ot"], fr["pt"]]
                    t_Y.append(pool.dma(Y, x2_dram.rearrange("(t p) d -> p t d", p=P), s_misc[9], 16, t_end))
                    t_ln.append(pool.dma(LN, brow[1:3, :].partition_broadcast(P), s_misc[1], 16))
                    t_eps.append(dve.do(lambda e: e.memset(eps, 1e-5), t_end))
                    act.quiet(lambda e: e.preload_act_table_set("sqrt_and_others"))
                return t_mt[t]

            t_y = {}
            bst = sm2[:, 64:112]
            mv = sm2[:, 112:124]
            eps = sm2[:, 124:125]

            def ev_out(c):
                def f(t, ps, tok):
                    hs = Y[:, t, c * 512:c * 512 + 512]
                    y = dve.do(lambda e: e.scalar_tensor_tensor(hs, hs, 2.0 ** 0.25, ps[:, :], ALU.mult, ALU.add), tok, t_Y)
                    s = dve.do(lambda e: e.bn_stats(bst[:, 12 * t + 6 * c:12 * t + 6 * c + 6], hs), y)
                    t_y[t] = [*t_y.get(t, []), y, s]
                    if c == 1:
                        mu, va, nb = (mv[:, 3 * t + i:3 * t + i + 1] for i in range(3))
                        a = dve.do(lambda e: e.bn_aggr(mv[:, 3 * t:3 * t + 2], bst[:, 12 * t:12 * t + 12]), t_y[t])
                        a = act.do(lambda e: e.activation(va, va, ACT.Sqrt, bias=eps), a, t_eps)
                        a = dve.do(lambda e: e.reciprocal(va, va), a)
                        b = dve.do(lambda e: e.tensor_scalar(nb, mu, va, -1.0, ALU.mult, ALU.mult), a)
                        for half, q in enumerate((dve, pool)):
                            hc = slice(half * 512, half * 512 + 512)
                            yt = Y[:, t, hc]
                            n = act.do(lambda e, yt=yt: e.activation(yt, yt, ACT.Identity, bias=nb, scale=va), a, b, t_y[t])
                            n = q.do(lambda e, yt=yt, hc=hc: e.tensor_tensor(yt, yt, LN[:, 0, hc], ALU.mult), n, t_ln)
                            n = q.do(lambda e, yt=yt, hc=hc: e.tensor_tensor(yt, yt, LN[:, 1, hc], ALU.add), n, t_ln)
                            sp.dma(out[t * P:(t + 1) * P, hc], yt, s_out, 16 * (2 * t + half + 1), n)
                    return [y]
                return f

            sides.run(chain(until(lambda: len(nsa_done) == 4), *[tm(SLOT_WOUT2 + 4 * c, 512, 8, ev_out(c), x_tok=mixed, tail=c == 1) for c in range(2)]), SLACK[4])
            sp.wait((s_out, 128))
            p3.close()

        block = ctx.enter_context(nc.Block())

        @block.sync
        def _(e):
            sp.play(e)

        @block.tensor
        def _(e):
            pe.play(e)

        @block.scalar
        def _(e):
            act.play(e)

        @block.vector
        def _(e):
            dve.play(e)

        @block.gpsimd
        def _(e):
            pool.play(e)


def constants():
    c = np.zeros((P, C_N), np.float32)
    p = np.arange(P)
    c[:, C_ID:C_ID + 128] = np.eye(P)
    dist = p[:, None] + 128 - np.arange(256)[None]
    c[:, C_BAND:C_BAND + 256] = np.where((dist >= 0) & (dist < 128), 0.0, NEG)
    c[:, C_STRICT:C_STRICT + 128] = p[:, None] < p[None]
    c[:, C_NTRI:C_NTRI + 128] = -(p[:, None] >= p[None]).astype(np.float32)
    for n, L in enumerate(LEVELS):
        t = np.arange(P).reshape(-1, 2, L)[:, 1].reshape(-1)
        same = p[:, None] // (2 * L) == t[None] // (2 * L)
        c[:, C_LEV + 256 * n:C_LEV + 256 * n + 256] = np.tile(same & ((p[:, None] // L) % 2 == 0), (1, 4))
    c[:, C_ROW] = p >= 31
    c[:, C_ONE:C_ONE + 128] = -1.0
    r = np.arange(S)
    big = np.maximum(r, 1).astype(np.float32) / np.float32(16)
    large = 16 + (np.log(big) / np.float32(np.log(128 / 16)) * np.float32(16)).astype(np.int32)
    bucket = np.where(r < 16, r, np.clip(large, 0, 31))
    oneh = np.zeros((32, S), np.float32)
    oneh[bucket, 511 - r] = 8.0
    return c, oneh


def fm_slot(w, cols):
    return w[:, cols].reshape(-1, P, len(cols)).transpose(1, 0, 2).reshape(P, -1)


def kernel(**inputs):
    import concourse.bacc as bacc
    from concourse.bass_utils import run_bass_kernel_spmd

    a = {k: np.asarray(v) for k, v in inputs.items()}
    cst, oneh = constants()
    w_in, w_up, w_dn, w_out = a["w_in"][0], a["w_up"][0], a["w_down"][0], a["w_out"][0]
    wa, wc = a["w_attn_branch"][0], a["w_conv_branch"][0]
    w2, wo2 = a["w_in_2"][0], a["w_out_2"][0]
    ar = np.arange
    qcols = np.concatenate([np.concatenate([ar(i * 64, i * 64 + 64), ar((i + 4) * 64, (i + 4) * 64 + 64)])
                            for i in range(4)])
    cols1 = np.concatenate([qcols, ar(512, 4352)])
    tiles1 = cols1.reshape(34, P)
    slots = []

    def fms(w, t):
        slots.append(fm_slot(w, t))

    def tms(w, cols, per=2):
        b = w[:, cols].reshape(-1, P, len(cols))
        for s0 in range(0, b.shape[0], per):
            slots.append(b[s0:s0 + per].transpose(1, 0, 2).reshape(P, -1))

    for i in range(6):
        fms(w_in, tiles1[i])
    for c in range(4):
        for j in (10, 14, 6):
            fms(w_in, tiles1[j + c])
    for n in range(8):
        fms(w_in, tiles1[18 + n])
        fms(w_in, tiles1[26 + n])
        cs = ar(n * P, n * P + P)
        slots.append(np.concatenate([fm_slot(wa, cs), fm_slot(wc, cs)], axis=1))
    for c in range(2):
        tms(w_out, ar(c * 512, c * 512 + 512))
    for hf in range(2):
        for j in range(11):
            f = hf * 11 + j
            fms(w_up, ar(f * P, f * P + P))
            fms(w_up, ar((NF + f) * P, (NF + f) * P + P))
        for c in range(2):
            tms(w_dn[hf * 1408:hf * 1408 + 1408], ar(c * 512, c * 512 + 512))
    o = np.cumsum([0, 384, 128, 128, 128, 128, 128, 128, 18, 384, 256, 256, 256, 256, 384, 384, 384, 384])
    (nq, nkc, nvc, nks, nvs, nkw, nvw, ng, nz, sq, sk, sv, sz, hq, hf_, hi_, hz, _) = o
    for i in range(3):
        fms(w2, ar(hf_ + i * P, hf_ + i * P + P))
    for i in range(3):
        fms(w2, ar(hq + i * P, hq + i * P + P))
    tms(w2, np.concatenate([ar(hi_, hi_ + 384), ar(ng, ng + 18)]))
    for b in (nkc, nvc, nks, nkw):
        fms(w2, ar(b, b + P))
    for i in range(3):
        fms(w2, np.concatenate([ar(nq + i * 64, nq + i * 64 + 64), ar(nq + (i + 3) * 64, nq + (i + 3) * 64 + 64)]))
    tms(w2, np.concatenate([ar(nvs, nvs + 128), ar(nvw, nvw + 128), ar(sv, sv + 256)]))
    for b in (sq, sk):
        for i in range(2):
            fms(w2, ar(b + i * P, b + i * P + P))
    zc = np.concatenate([ar(nz, nz + 384), ar(sz, sz + 256), ar(hz, hz + 384)])
    for i in range(8):
        fms(w2, zc[i * P:i * P + P])
    for c in range(2):
        tms(wo2, ar(c * 512, c * 512 + 512))
    assert len(slots) == N_SLOTS, (len(slots), N_SLOTS)
    wp = np.zeros((N_SLOTS, P, 1024), np.float32)
    for i, s in enumerate(slots):
        wp[i, :, :s.shape[1]] = s

    pp = np.zeros((P, PP_N), np.float32)
    pp[:, PP_B:PP_B + 34] = a["b_in"][0][tiles1].T
    pp[:, PP_CW:PP_CW + 12] = a["conv_w"][0].reshape(3, 4, P).transpose(2, 1, 0).reshape(P, 12)
    pp[:, PP_FW:PP_FW + 132] = a["ffn_conv_w"][0].reshape(3, 44, P).transpose(2, 1, 0).reshape(P, 132)
    pp[:, PP_LB:PP_LB + 3] = a["hg_lb_2"][0].reshape(3, P).T
    pp[:, PP_HG:PP_HG + 3] = a["hg_norm_w_2"][0].reshape(3, P).T
    rows = np.concatenate([a["b_in"][0][640:768], a["sinks"][0]])
    brow = np.stack([a["final_norm"], a["ln_g_2"][0], a["ln_b_2"][0], a["mix_norm"][0], a["ffn_norm"][0]])
    w1c = np.stack([a[n][0].reshape(16, P, P).transpose(1, 0, 2).reshape(P, 2048) for n in ("w_ck1_2", "w_cv1_2")])
    w2c = np.concatenate([a["w_ck2_2"][0], a["w_cv2_2"][0]], axis=1)
    posT = a["cmp_pos_2"][0].reshape(16, P).T
    arrays = dict(wp=wp, x=a["x"][0], pp=pp, cst=cst, rows=rows, brow=brow, relb=a["rel_bias_2"], oneh=oneh,
                  w1c=w1c, w2c=w2c, posT=posT)
    arrays = {k: np.ascontiguousarray(v) for k, v in arrays.items()}
    nc = bacc.Bacc("TRN2", target_bir_lowering=False, num_devices=1)
    args = [nc.dram_tensor(k, v.shape, mybir.dt.from_np(v.dtype), kind="ExternalInput").ap() for k, v in arrays.items()]
    out = nc.dram_tensor("y", (S, D), F, kind="ExternalOutput").ap()
    program(nc, *args, out)
    r = run_bass_kernel_spmd(nc, [arrays], core_ids=[0])
    return r.results[0]["y"].reshape(1, S, D)
```
